# Optimizing a Trainium2 kernel written in Bass

```python
import math
import jax, jax.numpy as jnp
from jax import lax
import numpy as np
import jax
import jax.numpy as jnp

D_MODEL = 1024
BATCH = 1
SEQ = 512
DEPTH = 1

GRID_W = 64
CTX_LEN = 256
EPS = 1e-6

MLA_HEADS = 4
MLA_Q_LORA = 256
MLA_KV_LORA = 128
MLA_NOPE = 128
MLA_ROPE = 64
MLA_V = 128
MLA_WIDTH = MLA_HEADS * MLA_V
ROPE_BASE = 10000.0
ATTN_BLOCK = 128

HG_HEADS = 4
HG_K = 128
HG_V = 64
HG_WIDTH = HG_HEADS * HG_V
HG_CHUNK = 64

FN_GROUPS = 4
FN_GROUP_DIM = 64
FN_WIDTH = FN_GROUPS * FN_GROUP_DIM

MIX_WIDTH = MLA_WIDTH + HG_WIDTH + FN_WIDTH
FFN_HIDDEN = -(-8 * D_MODEL // (3 * 256)) * 256

O_CQ = 0
O_CKV = O_CQ + MLA_Q_LORA
O_KR = O_CKV + MLA_KV_LORA
O_HQ = O_KR + MLA_ROPE
O_HFF = O_HQ + HG_HEADS * HG_K
O_HFB = O_HFF + HG_HEADS * HG_K
O_HI = O_HFB + HG_HEADS * HG_K
O_HG = O_HI + HG_WIDTH
O_FN = O_HG + HG_WIDTH
IN_WIDTH = O_FN + FN_WIDTH


def rms_norm(x, g):
    xf = x.astype(jnp.float32)
    y = xf * lax.rsqrt(jnp.mean(xf * xf, axis=-1, keepdims=True) + EPS)
    return (y * g.astype(jnp.float32)).astype(x.dtype)

def modulate(x, g, shift, scale):
    return rms_norm(x, g) * (1 + scale) + shift

def axial_rope(n_tokens, dtype):
    rows = n_tokens // GRID_W
    row_pos = jnp.repeat(jnp.arange(rows, dtype=jnp.float32), GRID_W)
    col_pos = jnp.tile(jnp.arange(GRID_W, dtype=jnp.float32), rows)
    axis_dim = MLA_ROPE // 2
    inv_freq = ROPE_BASE ** (-jnp.arange(0, axis_dim, 2, dtype=jnp.float32) / axis_dim)
    ang_r = row_pos[:, None] * inv_freq
    ang_c = col_pos[:, None] * inv_freq
    ang = jnp.concatenate([ang_r, ang_r, ang_c, ang_c], axis=-1)
    return (jnp.cos(ang).astype(dtype)[None, :, None, :], jnp.sin(ang).astype(dtype)[None, :, None, :])

def apply_rope(x, cos, sin):
    r1, r2, c1, c2 = jnp.split(x, 4, axis=-1)
    rot = jnp.concatenate([-r2, r1, -c2, c1], axis=-1)
    return x * cos + rot * sin

def mla_queries(p, q_norm_g, w_uq, rope):
    b, t, _ = p.shape
    cq = rms_norm(p[..., O_CQ:O_CKV], q_norm_g)
    q = (cq @ w_uq).reshape(b, t, MLA_HEADS, MLA_NOPE + MLA_ROPE)
    q_nope, q_pe = q[..., :MLA_NOPE], q[..., MLA_NOPE:]
    if rope is not None:
        q_pe = apply_rope(q_pe, rope[0], rope[1])
    return jnp.concatenate([q_nope, q_pe], axis=-1)

def mla_keys_values(p, kv_norm_g, w_ukv, rope):
    b, t, _ = p.shape
    ckv = rms_norm(p[..., O_CKV:O_KR], kv_norm_g)
    kv = (ckv @ w_ukv).reshape(b, t, MLA_HEADS, MLA_NOPE + MLA_V)
    k_nope, v = kv[..., :MLA_NOPE], kv[..., MLA_NOPE:]
    k_pe = p[..., O_KR:O_HQ][:, :, None, :]
    if rope is not None:
        k_pe = apply_rope(k_pe, rope[0], rope[1])
    k = jnp.concatenate([k_nope, jnp.broadcast_to(k_pe, (b, t, MLA_HEADS, MLA_ROPE))], axis=-1)
    return k, v

def block_attention(q, k, v):
    b, t, h, dk = q.shape
    nb = t // ATTN_BLOCK
    qb = q.reshape(b, nb, ATTN_BLOCK, h, dk).swapaxes(0, 1)
    scale = 1.0 / math.sqrt(dk)

    def one_block(qi):
        s = jnp.einsum('bqhd,bkhd->bhqk', qi, k).astype(jnp.float32) * scale
        pr = jax.nn.softmax(s, axis=-1).astype(v.dtype)
        return jnp.einsum('bhqk,bkhd->bqhd', pr, v)

    o = lax.map(one_block, qb)
    return o.swapaxes(0, 1).reshape(b, t, h * v.shape[-1])

def chunk_gated_scan(q, k, v, log_f, s0, with_output):
    b, t, h, kd = q.shape
    n = t // HG_CHUNK

    def to_chunks(a):
        return a.reshape(b, n, HG_CHUNK, h, a.shape[-1]).swapaxes(0, 1)

    causal = jnp.tril(jnp.ones((HG_CHUNK, HG_CHUNK), dtype=bool))[None, :, :, None, None]

    def step(state, inp):
        qc, kc, vc, gc = inp
        bcum = jnp.cumsum(gc, axis=1)
        total = bcum[:, -1]
        new_state = jnp.exp(total)[..., None] * state + jnp.einsum(
            'bshk,bshv->bhkv', kc * jnp.exp(total[:, None] - bcum), vc)
        if not with_output:
            return new_state, None
        decay = jnp.exp(jnp.where(causal, bcum[:, :, None] - bcum[:, None], -jnp.inf))
        scores = jnp.einsum('bthk,btshk,bshk->bhts', qc, decay, kc)
        o = jnp.einsum('bhts,bshv->bthv', scores, vc) + jnp.einsum(
            'bthk,bhkv->bthv', qc * jnp.exp(bcum), state)
        return new_state, o

    s_fin, o = lax.scan(step, s0, (to_chunks(q), to_chunks(k), to_chunks(v), to_chunks(log_f)))
    if with_output:
        o = o.swapaxes(0, 1).reshape(b, t, h, v.shape[-1])
    return o, s_fin

def hgrn2_inputs(p, lb_fb):
    b, t, _ = p.shape
    q = jax.nn.silu(p[..., O_HQ:O_HFF].astype(jnp.float32)).reshape(b, t, HG_HEADS, HG_K)
    i = p[..., O_HI:O_HG].astype(jnp.float32).reshape(b, t, HG_HEADS, HG_V)

    def gate(z, lb):
        f = lb + (1.0 - lb) * jax.nn.sigmoid(z.astype(jnp.float32))
        return (1.0 - f).reshape(b, t, HG_HEADS, HG_K), jnp.log(f).reshape(b, t, HG_HEADS, HG_K)

    fwd = gate(p[..., O_HFF:O_HFB], lb_fb[0])
    bwd = gate(p[..., O_HFB:O_HI], lb_fb[1])
    return q, i, fwd, bwd

def hgrn2_readout(o, z_gate, gain):
    b, t = o.shape[0], o.shape[1]
    on = o * lax.rsqrt(jnp.mean(o * o, axis=-1, keepdims=True) + EPS)
    on = on * gain.astype(jnp.float32).reshape(HG_HEADS, HG_V)
    return (on.reshape(b, t, HG_WIDTH) * jax.nn.silu(z_gate.astype(jnp.float32))).astype(z_gate.dtype)

def fourier_mix(z, w):
    b, t, _ = z.shape
    zg = z.astype(jnp.float32).reshape(b, t, FN_GROUPS, FN_GROUP_DIM)
    mixed = jnp.fft.fft2(zg, axes=(1, 3), norm='ortho').real
    return mixed.reshape(b, t, FN_WIDTH).astype(z.dtype) @ w

def swiglu_ffn(h, w_gu, w_dn):
    gate, up = jnp.split(h @ w_gu, 2, axis=-1)
    return (jax.nn.silu(gate) * up) @ w_dn

def first_inputs(seed: int = 0) -> dict:
    key = jax.random.key(seed)
    ks = jax.random.split(key, 20)
    f32 = jnp.float32

    def nrm(k, shape, scale):
        return jax.random.normal(k, shape, f32) * scale

    def gain(k, shape):
        return 1.0 + 0.02 * jax.random.normal(k, shape, f32)

    return {
        'x': nrm(ks[0], (BATCH, SEQ, D_MODEL), 1.0),
        'c': nrm(ks[1], (BATCH, D_MODEL), 1.0),
        'ctx': nrm(ks[2], (BATCH, CTX_LEN, D_MODEL), 1.0),
        'c_ctx': nrm(ks[3], (D_MODEL,), 1.0),
        'w_mod': nrm(ks[4], (DEPTH, D_MODEL, 6 * D_MODEL), D_MODEL ** -0.5),
        'b_mod': nrm(ks[5], (DEPTH, 6 * D_MODEL), 0.02),
        'norm1_g': gain(ks[6], (DEPTH, D_MODEL)),
        'norm2_g': gain(ks[7], (DEPTH, D_MODEL)),
        'w_in': nrm(ks[8], (DEPTH, D_MODEL, IN_WIDTH), D_MODEL ** -0.5),
        'q_norm_g': gain(ks[9], (DEPTH, MLA_Q_LORA)),
        'w_uq': nrm(ks[10], (DEPTH, MLA_Q_LORA, MLA_HEADS * (MLA_NOPE + MLA_ROPE)), MLA_Q_LORA ** -0.5),
        'kv_norm_g': gain(ks[11], (DEPTH, MLA_KV_LORA)),
        'w_ukv': nrm(ks[12], (DEPTH, MLA_KV_LORA, MLA_HEADS * (MLA_NOPE + MLA_V)), MLA_KV_LORA ** -0.5),
        'lb_param': nrm(ks[13], (DEPTH, 2, HG_HEADS * HG_K), 1.0),
        'hg_norm_g': gain(ks[14], (DEPTH, HG_WIDTH)),
        'w_fourier': nrm(ks[15], (DEPTH, FN_WIDTH, FN_WIDTH), FN_WIDTH ** -0.5),
        'w_out': nrm(ks[16], (DEPTH, MIX_WIDTH, D_MODEL), MIX_WIDTH ** -0.5),
        'w_gate_up': nrm(ks[17], (DEPTH, D_MODEL, 2 * FFN_HIDDEN), D_MODEL ** -0.5),
        'w_down': nrm(ks[18], (DEPTH, FFN_HIDDEN, D_MODEL), FFN_HIDDEN ** -0.5),
        'final_norm_g': gain(ks[19], (D_MODEL,)),
    }

def first_block(x, c, ctx, c_ctx, w_mod, b_mod, norm1_g, norm2_g, w_in, q_norm_g, w_uq, kv_norm_g, w_ukv,
              lb_param, hg_norm_g, w_fourier, w_out, w_gate_up, w_down, final_norm_g):
    b, t, _ = x.shape
    rope = axial_rope(t, x.dtype)
    probs = jax.nn.softmax(lb_param.astype(jnp.float32), axis=0)
    lower_bounds = jnp.cumsum(probs, axis=0) - probs[0]
    s_zero = jnp.zeros((b, HG_HEADS, HG_K, HG_V), jnp.float32)
    c_act = jax.nn.silu(c)
    cc_act = jax.nn.silu(c_ctx)

    def flip(a):
        return jnp.flip(a, axis=1)

    for l in range(DEPTH):
        last = l == DEPTH - 1
        sh1, sc1, g1, sh2, sc2, g2 = jnp.split((c_act @ w_mod[l] + b_mod[l])[:, None, :], 6, axis=-1)
        csh1, csc1, cg1, csh2, csc2, cg2 = jnp.split((cc_act @ w_mod[l] + b_mod[l])[None, None, :], 6, axis=-1)

        p = modulate(x, norm1_g[l], sh1, sc1) @ w_in[l]
        pc = modulate(ctx, norm1_g[l], csh1, csc1) @ w_in[l]

        k_lat, v_lat = mla_keys_values(p, kv_norm_g[l], w_ukv[l], rope)
        k_ctx, v_ctx = mla_keys_values(pc, kv_norm_g[l], w_ukv[l], None)
        q_lat = mla_queries(p, q_norm_g[l], w_uq[l], rope)
        attn = block_attention(q_lat, jnp.concatenate([k_lat, k_ctx], axis=1),
                               jnp.concatenate([v_lat, v_ctx], axis=1))

        lb_fb = lower_bounds[l]
        qc, ic, (kcf, lcf), (kcb, lcb) = hgrn2_inputs(pc, lb_fb)
        o_cf, s_cf = chunk_gated_scan(qc, kcf, ic, lcf, s_zero, not last)
        o_cb, s_cb = chunk_gated_scan(flip(qc), flip(kcb), flip(ic), flip(lcb), s_zero, not last)
        ql, il, (klf, llf), (klb, llb) = hgrn2_inputs(p, lb_fb)
        o_lf, _ = chunk_gated_scan(ql, klf, il, llf, s_cf, True)
        o_lb, _ = chunk_gated_scan(flip(ql), flip(klb), flip(il), flip(llb), s_cb, True)
        hg = hgrn2_readout(o_lf + flip(o_lb), p[..., O_HG:O_FN], hg_norm_g[l])

        fn = fourier_mix(p[..., O_FN:IN_WIDTH], w_fourier[l])

        y = jnp.concatenate([attn, hg, fn], axis=-1) @ w_out[l]
        x_new = x + g1 * y
        x_new = x_new + g2 * swiglu_ffn(modulate(x_new, norm2_g[l], sh2, sc2), w_gate_up[l], w_down[l])

        if not last:
            attn_c = block_attention(mla_queries(pc, q_norm_g[l], w_uq[l], None), k_ctx, v_ctx)
            hg_c = hgrn2_readout(o_cf + flip(o_cb), pc[..., O_HG:O_FN], hg_norm_g[l])
            fn_c = fourier_mix(pc[..., O_FN:IN_WIDTH], w_fourier[l])
            yc = jnp.concatenate([attn_c, hg_c, fn_c], axis=-1) @ w_out[l]
            ctx = ctx + cg1 * yc
            ctx = ctx + cg2 * swiglu_ffn(modulate(ctx, norm2_g[l], csh2, csc2), w_gate_up[l], w_down[l])
        x = x_new

    return rms_norm(x, final_norm_g)


DEPTH_2 = 2

D_FF = 4 * D_MODEL
NORM_EPS = 1e-6
N_EVEN = (DEPTH_2 + 1) // 2
N_ODD = DEPTH_2 // 2

GDN_HEADS = 8
GDN_HEAD_DIM = 64
GDN_WIDTH = GDN_HEADS * GDN_HEAD_DIM
GDN_CONV = 4
GDN_CHUNK = 64

SC_WIDTH = D_MODEL - GDN_WIDTH
SC_CONV = 3

EVEN_IN = 4 * GDN_WIDTH + 2 * GDN_HEADS + 3 * SC_WIDTH

NSA_HEADS = 16
NSA_HEAD_DIM = D_MODEL // NSA_HEADS
NSA_KV_GROUPS = 4
NSA_HPG = NSA_HEADS // NSA_KV_GROUPS
NSA_KV_WIDTH = NSA_KV_GROUPS * NSA_HEAD_DIM
CMP_BLOCK = 32
CMP_STRIDE = 16
CMP_HIDDEN = 256
SEL_BLOCK = 64
N_SELECT = 16
WINDOW = 512
Q_BLOCK = 128
ODD_IN = NSA_HEADS * NSA_HEAD_DIM + 6 * NSA_KV_WIDTH + 3 * NSA_HEADS

ROPE_THETA = 500000.0
ROPE_DIM = NSA_HEAD_DIM // 4


def _split_points(sizes):
    return [int(v) for v in np.cumsum(sizes)[:-1]]

def rms_norm_2(x, w):
    xf = x.astype(jnp.float32)
    y = xf * lax.rsqrt(jnp.mean(xf * xf, axis=-1, keepdims=True) + NORM_EPS)
    return (y * w.astype(jnp.float32)).astype(x.dtype)

def l2_normalize(x):
    xf = x.astype(jnp.float32)
    return xf * lax.rsqrt(jnp.sum(xf * xf, axis=-1, keepdims=True) + NORM_EPS)

def causal_dwconv(x, w):
    k_width = w.shape[0]
    t_len = x.shape[1]
    xp = jnp.pad(x, ((0, 0), (k_width - 1, 0), (0, 0)))
    return sum(xp[:, j:j + t_len] * w[j] for j in range(k_width))

def masked_softmax(s, mask):
    s = jnp.where(mask, s, -jnp.inf)
    m = jnp.max(s, axis=-1, keepdims=True)
    m = jnp.where(jnp.isfinite(m), m, 0.0)
    e = jnp.exp(s - m)
    den = jnp.sum(e, axis=-1, keepdims=True)
    return e / jnp.where(den > 0.0, den, 1.0)

def rope_tables(t_len):
    inv_freq = ROPE_THETA ** (-jnp.arange(0, ROPE_DIM, 2, dtype=jnp.float32) / ROPE_DIM)
    ang = jnp.arange(t_len, dtype=jnp.float32)[:, None] * inv_freq[None, :]
    return jnp.cos(ang), jnp.sin(ang)

def apply_partial_rope(x, cos, sin):
    half = ROPE_DIM // 2
    xf = x.astype(jnp.float32)
    x1, x2, rest = xf[..., :half], xf[..., half:ROPE_DIM], xf[..., ROPE_DIM:]
    c = cos[None, :, None, :]
    s = sin[None, :, None, :]
    return jnp.concatenate([x1 * c - x2 * s, x2 * c + x1 * s, rest], axis=-1).astype(x.dtype)

def squared_relu_mlp(h, w_up, w_down):
    return jnp.square(jax.nn.relu(h @ w_up)) @ w_down

def gated_delta_rule_chunked(q, k, v, g, beta):
    f32 = jnp.float32
    b_sz, t_len, n_h, dk = q.shape
    dv = v.shape[-1]
    c = GDN_CHUNK
    n_chunks = t_len // c

    def chunks(a):
        a = a.astype(f32).reshape((b_sz, n_chunks, c, n_h) + a.shape[3:])
        return jnp.moveaxis(a, (1, 3), (0, 2))

    qc = chunks(q) * (dk ** -0.5)
    kc = chunks(k)
    vc = chunks(v)
    bc = chunks(beta)
    gc = jnp.cumsum(chunks(g), axis=-1)
    incl = jnp.tril(jnp.ones((c, c), bool))
    strict = jnp.tril(jnp.ones((c, c), bool), -1)
    decay = jnp.exp(jnp.where(incl, gc[..., :, None] - gc[..., None, :], -jnp.inf))
    kb = kc * bc[..., None]
    m_low = jnp.where(strict, jnp.einsum('nbhik,nbhjk->nbhij', kb, kc) * decay, 0.0)
    a_mat = m_low + jnp.eye(c, dtype=f32)
    u = lax.linalg.triangular_solve(a_mat, vc * bc[..., None], left_side=True, lower=True, unit_diagonal=True)
    w = lax.linalg.triangular_solve(a_mat, kb * jnp.exp(gc)[..., None], left_side=True, lower=True, unit_diagonal=True)
    attn = jnp.einsum('nbhik,nbhjk->nbhij', qc, kc) * decay

    def step(state, inp):
        q_c, k_c, u_c, w_c, attn_c, g_c = inp
        v_new = u_c - jnp.einsum('bhck,bhkv->bhcv', w_c, state)
        o_c = (jnp.einsum('bhck,bhkv->bhcv', q_c * jnp.exp(g_c)[..., None], state)
               + jnp.einsum('bhij,bhjv->bhiv', attn_c, v_new))
        g_last = g_c[..., -1:]
        state = (state * jnp.exp(g_last)[..., None]
                 + jnp.einsum('bhck,bhcv->bhkv', k_c * jnp.exp(g_last - g_c)[..., None], v_new))
        return state, o_c

    s0 = jnp.zeros((b_sz, n_h, dk, dv), f32)
    _, o = lax.scan(step, s0, (qc, kc, u, w, attn, gc))
    return jnp.moveaxis(o, (0, 2), (1, 3)).reshape(b_sz, t_len, n_h, dv)

def gdn_shortconv_mixer(h, w_in, qkv_conv, a_log, dt_bias, o_norm, sc_conv, w_out):
    f32 = jnp.float32
    b_sz, t_len, _ = h.shape
    sizes = (3 * GDN_WIDTH, GDN_WIDTH, GDN_HEADS, GDN_HEADS, SC_WIDTH, SC_WIDTH, SC_WIDTH)
    qkv, z, a, b, b_gate, c_gate, hs = jnp.split(h @ w_in, _split_points(sizes), axis=-1)
    qkv = jax.nn.silu(causal_dwconv(qkv, qkv_conv))
    q, k, v = [t.reshape(b_sz, t_len, GDN_HEADS, GDN_HEAD_DIM) for t in jnp.split(qkv, 3, axis=-1)]
    g = -jnp.exp(a_log.astype(f32)) * jax.nn.softplus(a.astype(f32) + dt_bias.astype(f32))
    beta = jax.nn.sigmoid(b.astype(f32))
    o = gated_delta_rule_chunked(l2_normalize(q), l2_normalize(k), v, g, beta)
    o = rms_norm_2(o, o_norm) * jax.nn.silu(z.reshape(b_sz, t_len, GDN_HEADS, GDN_HEAD_DIM).astype(f32))
    y_a = o.reshape(b_sz, t_len, GDN_WIDTH).astype(h.dtype)
    y_b = b_gate * causal_dwconv(c_gate * hs, sc_conv)
    return jnp.concatenate([y_a, y_b], axis=-1) @ w_out

def compress_blocks(x, pos, w1, w2):
    b_sz, t_len, g_sz, d = x.shape
    r = CMP_BLOCK // CMP_STRIDE
    n_cmp = t_len // CMP_STRIDE - r + 1
    ch = x.reshape(b_sz, t_len // CMP_STRIDE, CMP_STRIDE, g_sz, d)
    blk = jnp.concatenate([ch[:, i:i + n_cmp] for i in range(r)], axis=2)
    blk = blk + pos[None, None, :, None, :].astype(x.dtype)
    blk = jnp.moveaxis(blk, 3, 2).reshape(b_sz, n_cmp, g_sz, CMP_BLOCK * d)
    return jax.nn.silu(blk @ w1) @ w2

def gather_blocks(blocks, idx):
    return jax.vmap(jax.vmap(lambda bl, ix: bl[ix]))(blocks, idx)

def nsa_mixer(h, w_in, cmp_pos, cmp_k_w1, cmp_k_w2, cmp_v_w1, cmp_v_w2, w_out):
    f32 = jnp.float32
    b_sz, t_len, _ = h.shape
    n_g, hpg, dh = NSA_KV_GROUPS, NSA_HPG, NSA_HEAD_DIM
    sizes = (NSA_HEADS * dh,) + (NSA_KV_WIDTH,) * 6 + (3 * NSA_HEADS,)
    q, k_c, v_c, k_s, v_s, k_w, v_w, gl = jnp.split(h @ w_in, _split_points(sizes), axis=-1)
    q = q.reshape(b_sz, t_len, NSA_HEADS, dh)
    k_c, v_c, k_s, v_s, k_w, v_w = [a.reshape(b_sz, t_len, n_g, dh) for a in (k_c, v_c, k_s, v_s, k_w, v_w)]
    gates = jax.nn.sigmoid(gl.astype(f32)).reshape(b_sz, t_len, n_g, hpg, 3)
    cos, sin = rope_tables(t_len)
    q_r = apply_partial_rope(q, cos, sin)
    k_s = apply_partial_rope(k_s, cos, sin)
    k_w = apply_partial_rope(k_w, cos, sin)
    kc_blk = compress_blocks(k_c, cmp_pos, cmp_k_w1, cmp_k_w2).astype(f32)
    vc_blk = compress_blocks(v_c, cmp_pos, cmp_v_w1, cmp_v_w2).astype(f32)
    n_cmp = kc_blk.shape[1]
    cmp_end = jnp.arange(n_cmp) * CMP_STRIDE + CMP_BLOCK - 1
    n_sel_blocks = t_len // SEL_BLOCK
    n_sel = min(N_SELECT, n_sel_blocks)
    c_start = jnp.arange(n_cmp)[:, None] * CMP_STRIDE
    s_start = jnp.arange(n_sel_blocks)[None, :] * SEL_BLOCK
    overlap = ((c_start < s_start + SEL_BLOCK) & (c_start + CMP_BLOCK > s_start)).astype(f32)
    ks_blk = jnp.moveaxis(k_s.reshape(b_sz, n_sel_blocks, SEL_BLOCK, n_g, dh), 3, 1)
    vs_blk = jnp.moveaxis(v_s.reshape(b_sz, n_sel_blocks, SEL_BLOCK, n_g, dh), 3, 1)
    pad = ((0, 0), (WINDOW, 0), (0, 0), (0, 0))
    kw_pad = jnp.pad(k_w, pad)
    vw_pad = jnp.pad(v_w, pad)
    scale = dh ** -0.5
    blk_ids = jnp.arange(n_sel_blocks)
    in_blk = jnp.arange(SEL_BLOCK)
    win_off = jnp.arange(Q_BLOCK + WINDOW)

    def query_block(qb):
        q0 = qb * Q_BLOCK
        t = q0 + jnp.arange(Q_BLOCK)
        take = lambda a: lax.dynamic_slice_in_dim(a, q0, Q_BLOCK, axis=1)
        qn = take(q).astype(f32).reshape(b_sz, Q_BLOCK, n_g, hpg, dh) * scale
        qr = take(q_r).astype(f32).reshape(b_sz, Q_BLOCK, n_g, hpg, dh) * scale
        p_c = masked_softmax(jnp.einsum('bqghd,bcgd->bghqc', qn, kc_blk), cmp_end[None, :] <= t[:, None])
        o_c = jnp.einsum('bghqc,bcgd->bqghd', p_c, vc_blk)
        imp = jnp.einsum('bghqc,cs->bgqs', p_c, overlap)
        cur = (t // SEL_BLOCK)[:, None]
        js = blk_ids[None, :]
        forced = (js == 0) | (js == cur) | (js == cur - 1)
        imp = jnp.where(js > cur, -jnp.inf, jnp.where(forced, jnp.inf, imp))
        _, idx = lax.top_k(imp, n_sel)
        k_sel = gather_blocks(ks_blk, idx).astype(f32).reshape(b_sz, n_g, Q_BLOCK, n_sel * SEL_BLOCK, dh)
        v_sel = gather_blocks(vs_blk, idx).astype(f32).reshape(b_sz, n_g, Q_BLOCK, n_sel * SEL_BLOCK, dh)
        kpos = (idx[..., None] * SEL_BLOCK + in_blk).reshape(b_sz, n_g, Q_BLOCK, n_sel * SEL_BLOCK)
        p_s = masked_softmax(jnp.einsum('bqghd,bgqkd->bghqk', qr, k_sel), (kpos <= t[:, None])[:, :, None])
        o_s = jnp.einsum('bghqk,bgqkd->bqghd', p_s, v_sel)
        spos = q0 - WINDOW + win_off
        dist = t[:, None] - spos[None, :]
        m_w = (dist >= 0) & (dist < WINDOW) & (spos[None, :] >= 0)
        kwin = lax.dynamic_slice_in_dim(kw_pad, q0, Q_BLOCK + WINDOW, axis=1).astype(f32)
        vwin = lax.dynamic_slice_in_dim(vw_pad, q0, Q_BLOCK + WINDOW, axis=1).astype(f32)
        p_w = masked_softmax(jnp.einsum('bqghd,bkgd->bghqk', qr, kwin), m_w)
        o_w = jnp.einsum('bghqk,bkgd->bqghd', p_w, vwin)
        g = take(gates)
        o = g[..., 0:1] * o_c + g[..., 1:2] * o_s + g[..., 2:3] * o_w
        return o.reshape(b_sz, Q_BLOCK, NSA_HEADS * dh).astype(h.dtype)

    out = lax.map(query_block, jnp.arange(t_len // Q_BLOCK))
    out = jnp.moveaxis(out, 0, 1).reshape(b_sz, t_len, NSA_HEADS * dh)
    return out @ w_out

def second_inputs(seed: int = 0) -> dict:
    key = jax.random.key(seed)
    ks = jax.random.split(key, 24)
    f32 = jnp.float32

    def nrm(k, shape, scale):
        return jax.random.normal(k, shape, f32) * scale

    def gain(k, shape):
        return 1.0 + 0.01 * jax.random.normal(k, shape, f32)

    dt = jnp.exp(jax.random.uniform(ks[9], (N_EVEN, GDN_HEADS), f32, math.log(1e-3), math.log(0.1)))
    return {
        'x': nrm(ks[0], (BATCH, SEQ, D_MODEL), 1.0),
        'mix_norm': gain(ks[1], (DEPTH_2, D_MODEL)),
        'mlp_norm': gain(ks[2], (DEPTH_2, D_MODEL)),
        'w_up': nrm(ks[3], (DEPTH_2, D_MODEL, D_FF), D_MODEL ** -0.5),
        'w_down': nrm(ks[4], (DEPTH_2, D_FF, D_MODEL), D_FF ** -0.5),
        'final_norm': gain(ks[5], (D_MODEL,)),
        'ev_w_in': nrm(ks[6], (N_EVEN, D_MODEL, EVEN_IN), D_MODEL ** -0.5),
        'ev_qkv_conv': nrm(ks[7], (N_EVEN, GDN_CONV, 3 * GDN_WIDTH), GDN_CONV ** -0.5),
        'ev_a_log': jnp.log(jax.random.uniform(ks[8], (N_EVEN, GDN_HEADS), f32, 1.0, 16.0)),
        'ev_dt_bias': dt + jnp.log(-jnp.expm1(-dt)),
        'ev_o_norm': gain(ks[10], (N_EVEN, GDN_HEAD_DIM)),
        'ev_sc_conv': nrm(ks[11], (N_EVEN, SC_CONV, SC_WIDTH), SC_CONV ** -0.5),
        'ev_w_out': nrm(ks[12], (N_EVEN, GDN_WIDTH + SC_WIDTH, D_MODEL), D_MODEL ** -0.5),
        'od_w_in': nrm(ks[13], (N_ODD, D_MODEL, ODD_IN), D_MODEL ** -0.5),
        'od_cmp_pos': nrm(ks[14], (N_ODD, CMP_BLOCK, NSA_HEAD_DIM), 0.1),
        'od_cmp_k_w1': nrm(ks[15], (N_ODD, CMP_BLOCK * NSA_HEAD_DIM, CMP_HIDDEN), (CMP_BLOCK * NSA_HEAD_DIM) ** -0.5),
        'od_cmp_k_w2': nrm(ks[16], (N_ODD, CMP_HIDDEN, NSA_HEAD_DIM), CMP_HIDDEN ** -0.5),
        'od_cmp_v_w1': nrm(ks[17], (N_ODD, CMP_BLOCK * NSA_HEAD_DIM, CMP_HIDDEN), (CMP_BLOCK * NSA_HEAD_DIM) ** -0.5),
        'od_cmp_v_w2': nrm(ks[18], (N_ODD, CMP_HIDDEN, NSA_HEAD_DIM), CMP_HIDDEN ** -0.5),
        'od_w_out': nrm(ks[19], (N_ODD, NSA_HEADS * NSA_HEAD_DIM, D_MODEL), D_MODEL ** -0.5),
    }

def second_block(x, mix_norm, mlp_norm, w_up, w_down, final_norm,
              ev_w_in, ev_qkv_conv, ev_a_log, ev_dt_bias, ev_o_norm, ev_sc_conv, ev_w_out,
              od_w_in, od_cmp_pos, od_cmp_k_w1, od_cmp_k_w2, od_cmp_v_w1, od_cmp_v_w2, od_w_out):
    for layer in range(DEPTH_2):
        h = rms_norm_2(x, mix_norm[layer])
        i = layer // 2
        if layer % 2 == 0:
            x = x + gdn_shortconv_mixer(h, ev_w_in[i], ev_qkv_conv[i], ev_a_log[i], ev_dt_bias[i],
                                        ev_o_norm[i], ev_sc_conv[i], ev_w_out[i])
        else:
            x = x + nsa_mixer(h, od_w_in[i], od_cmp_pos[i], od_cmp_k_w1[i], od_cmp_k_w2[i],
                              od_cmp_v_w1[i], od_cmp_v_w2[i], od_w_out[i])
        x = x + squared_relu_mlp(rms_norm_2(x, mlp_norm[layer]), w_up[layer], w_down[layer])
    return rms_norm_2(x, final_norm)


def setup_inputs(seed=0):
    out = dict(first_inputs(seed))
    for name, value in second_inputs(seed + 1).items():
        if name != "x":
            out[name + "_2"] = value
    return out


def reference(
    x, c, ctx, c_ctx, w_mod, b_mod, norm1_g, norm2_g, w_in, q_norm_g, w_uq, kv_norm_g, w_ukv,
    lb_param, hg_norm_g, w_fourier, w_out, w_gate_up, w_down, final_norm_g, mix_norm_2,
    mlp_norm_2, w_up_2, w_down_2, final_norm_2, ev_w_in_2, ev_qkv_conv_2, ev_a_log_2,
    ev_dt_bias_2, ev_o_norm_2, ev_sc_conv_2, ev_w_out_2, od_w_in_2, od_cmp_pos_2, od_cmp_k_w1_2,
    od_cmp_k_w2_2, od_cmp_v_w1_2, od_cmp_v_w2_2, od_w_out_2,
):
    x = first_block(
        x, c, ctx, c_ctx, w_mod, b_mod, norm1_g, norm2_g, w_in, q_norm_g, w_uq, kv_norm_g,
        w_ukv, lb_param, hg_norm_g, w_fourier, w_out, w_gate_up, w_down, final_norm_g,
    )
    return second_block(
        x, mix_norm_2, mlp_norm_2, w_up_2, w_down_2, final_norm_2, ev_w_in_2, ev_qkv_conv_2,
        ev_a_log_2, ev_dt_bias_2, ev_o_norm_2, ev_sc_conv_2, ev_w_out_2, od_w_in_2,
        od_cmp_pos_2, od_cmp_k_w1_2, od_cmp_k_w2_2, od_cmp_v_w1_2, od_cmp_v_w2_2, od_w_out_2,
    )


_drawn_inputs = setup_inputs


def setup_inputs(seed=0):
    import zlib

    import numpy as np

    out = dict(_drawn_inputs(seed))
    spreads = {}
    factors = {'norm1_g': 4.46,
     'q_norm_g': 8.0,
     'kv_norm_g': 8.0,
     'hg_norm_g': 7.572,
     'mix_norm_2': 38.477,
     'mlp_norm_2': 200.0,
     'final_norm_2': 190.141,
     'ev_o_norm_2': 200.0,
     'od_cmp_pos_2': 200.0,
     'norm2_g': 8.0,
     'od_cmp_k_w1_2': 23.272,
     'od_cmp_k_w2_2': 23.176,
     'od_w_in_2': 8.0,
     'od_cmp_v_w1_2': 8.0,
     'od_cmp_v_w2_2': 8.0,
     'od_w_out_2': 8.0}
    for name, (base, spread) in spreads.items():
        noise = np.random.default_rng([zlib.crc32(name.encode()), seed]).standard_normal(out[name].shape)
        drawn = base * np.exp(spread * noise) if base else spread * noise
        out[name] = jnp.asarray(drawn.astype(out[name].dtype))
    for name, factor in factors.items():
        out[name] = (out[name] * factor).astype(out[name].dtype)
    return out
```

```python
import math
from contextlib import ExitStack

import numpy as np

import concourse.bass as bass
from concourse import mybir

F32 = mybir.dt.float32
U32 = mybir.dt.uint32
ALU = mybir.AluOpType
ACT = mybir.ActivationFunctionType
AX = mybir.AxisListType

P = 128
D = 1024
KD = D // P
T = 512
TT = T // P
TC = 256
TCT = TC // P
TA = T + TC
TAT = TT + TCT
EPS = 1e-6
GRID_W = 64
QL, KVL, NOPE, ROPE, VH, MH = 256, 128, 128, 64, 128, 4
HH, HK, HV = 4, 128, 64
FFN = 2816
FT = FFN // P
MLA_SCALE = 1.0 / math.sqrt(NOPE + ROPE)
GH, GD = 8, 64
DFF = 4096
NH, ND, NG = 16, 64, 4
NB_CMP = 31
CMP_STRIDE, CMP_BLOCK, CMP_HID = 16, 32, 256
NSA_ROPE = 16
LEVELS = 7
SLOT = 4096
RING = 3
NEG = -1.0e30


def level_mask(lev, later_free):
    half = 1 << lev
    a = np.arange(P)
    blk, sec = a // (2 * half), (a // half) % 2
    m = (blk[:, None] == blk[None, :]) & (sec[:, None] == 0) & (sec[None, :] == 1)
    return (m if later_free else m.T).astype(np.float32)


def rotation(dim, total):
    r = np.zeros((total, total), np.float32)
    for lo in dim:
        n = dim[lo]
        for i in range(n // 2):
            r[lo + n // 2 + i, lo + i] = -1.0
            r[lo + i, lo + n // 2 + i] = 1.0
    return r


def twice(a):
    z = np.zeros_like(a)
    return np.block([[a, z], [z, a]])


def constants():
    out = {}
    a = np.arange(P)
    out["ident"] = np.eye(P, dtype=np.float32)
    out["ones"] = np.ones((P, P), np.float32)
    out["blk64"] = twice(np.ones((64, 64), np.float32))
    out["rot_mla"] = twice(rotation({0: 32, 32: 32}, 64))
    out["rot_nsa"] = twice(rotation({0: NSA_ROPE}, 64))
    ang = 2 * np.pi * np.outer(np.arange(64), np.arange(64)) / 64
    out["dft_cos64"] = twice((np.cos(ang) / 8).astype(np.float32))
    out["dft_nsin64"] = twice((-np.sin(ang) / 8).astype(np.float32))
    out["upto"] = (a[:, None] <= a[None, :]).astype(np.float32)
    out["causal_neg"] = np.where(a[None, :] <= a[:, None], 0.0, NEG).astype(np.float32)
    for lev in range(LEVELS):
        out[f"first_second{lev}"] = level_mask(lev, True)
    for lev in range(LEVELS):
        out[f"second_first{lev}"] = level_mask(lev, False)
    f32 = np.float32
    rows = np.repeat(np.arange(T // GRID_W, dtype=f32), GRID_W)
    cols = np.tile(np.arange(GRID_W, dtype=f32), T // GRID_W)
    inv = (f32(10000.0) ** (-np.arange(0, 32, 2, dtype=f32) / f32(32))).astype(f32)
    ar, ac = rows[:, None] * inv, cols[:, None] * inv
    ang = np.concatenate([ar, ar, ac, ac], axis=-1).T
    out["cos_mla"] = np.tile(np.cos(ang), (2, 1)).astype(f32)
    out["sin_mla"] = np.tile(np.sin(ang), (2, 1)).astype(f32)
    inv = (f32(500000.0) ** (-np.arange(0, NSA_ROPE, 2, dtype=f32) / f32(NSA_ROPE))).astype(f32)
    ang = (np.arange(T, dtype=f32)[:, None] * inv[None, :]).T
    c = np.ones((64, T), f32)
    s = np.zeros((64, T), f32)
    c[0:8], c[8:16], s[0:8], s[8:16] = np.cos(ang), np.cos(ang), np.sin(ang), np.sin(ang)
    out["cos_nsa"] = np.tile(c, (2, 1))
    out["sin_nsa"] = np.tile(s, (2, 1))
    t = (np.arange(TT)[None, :, None] * P + a[:, None, None])
    end = np.arange(32)[None, None, :] * CMP_STRIDE + CMP_BLOCK - 1
    ok = (end <= t) & (np.arange(32)[None, None, :] < NB_CMP)
    out["cmp_neg"] = np.where(ok, 0.0, NEG).astype(f32).reshape(P, TT * 32)
    out["cmp_ok"] = ok.astype(f32).reshape(P, TT * 32)
    out["eighth"] = np.full((P, 1), 0.125, f32)
    out["one"] = np.ones((P, 1), f32)
    return out


CONSTS = constants()
CONST_AT = {}
_n = 0
for _name, _a in CONSTS.items():
    CONST_AT[_name] = (_n, _a.shape[1])
    _n += _a.shape[1]
NCONST = _n

VECS = [("c2", 2 * KD), ("b_mod", 48), ("norm1_g", KD), ("norm2_g", KD), ("q_norm_g", 2), ("kv_norm_g", 1),
        ("lb_param", 2 * HH), ("hg_norm_g", 2), ("final_norm_g", KD), ("mix0", KD), ("mix1", KD), ("mlp0", KD),
        ("mlp1", KD), ("final_norm", KD), ("conv", 12 * 4), ("o_norm", 1), ("sc_conv", 4 * 3), ("pos", 16),
        ("a_log", GH), ("dt_bias", GH)]
VEC_AT = {}
_n = 0
for _name, _w in VECS:
    VEC_AT[_name] = (_n, _w)
    _n += _w
NVEC = _n


def plan():
    out = [(f"mod{i}", SLOT) for i in range(4)]
    out += [("hi_fn", SLOT), ("mla_in", SLOT), ("hg_gate", 8 * 256), ("dft", SLOT), ("fourier", 2 * 256),
            ("mla_up", 2 * 768 + 1024), ("hff", SLOT), ("hfb", SLOT), ("hq", SLOT)]
    out += [(f"mod{i}", SLOT) for i in range(4, 12)]
    out += [(f"out{i}", SLOT) for i in range(2)]
    out += [(f"gu{i}", SLOT) for i in range(11)]
    out += [(f"dn{h}_{k}", (8, 8, 6)[k] * 512) for h in range(2) for k in range(3)]
    out += [("ev_ab", 8 * 16)] + [(f"ev{i}", SLOT) for i in range(7)]
    out += [(f"evo{i}", SLOT) for i in range(2)]
    out += [(f"up0_{i}", SLOT) for i in range(8)] + [(f"down0_{h}_{k}", SLOT) for h in range(2) for k in range(4)]
    out += [("gl", 8 * 48)] + [(f"od{i}", SLOT) for i in range(5)]
    out += [("kw1", SLOT), ("vw1", SLOT), ("cw2", 256)]
    out += [(f"odo{i}", SLOT) for i in range(2)]
    out += [(f"up1_{i}", SLOT) for i in range(8)] + [(f"down1_{h}_{k}", SLOT) for h in range(2) for k in range(4)]
    return out


PLAN = plan()
PLAN_AT = []
_n = 0
for _name, _w in PLAN:
    PLAN_AT.append(_n)
    _n += _w * P
NWEIGHT = _n


def program(nc, weights, consts_d, vecs_d, x_d, ctx_d, out_d):
    ctx = ExitStack()
    with ctx:
        nsem = [0]

        def sem(name):
            nsem[0] += 1
            return ctx.enter_context(nc.semaphore(f"{name}_{nsem[0]}"))

        def sb(name, shape, stack=None):
            if stack is None:
                return ctx.enter_context(nc.sbuf_tensor(name, shape, F32))
            n = int(np.prod(shape[1:]))
            n += n % 2
            at = next(a for a in sorted([0] + [b for _, b in held])
                      if all(b <= a or a + n <= a0 for a0, b in held))
            assert at + n <= ARENA, (name, at + n, ARENA)
            held.append((at, at + n))
            stack.callback(held.remove, (at, at + n))
            axes = "abcd"[:len(shape) - 1]
            flat = arena[:, at:at + int(np.prod(shape[1:]))]
            if len(axes) == 1:
                return flat
            return flat.rearrange(f"p ({' '.join(axes)}) -> p {' '.join(axes)}", **dict(zip(axes, shape[1:])))

        psum = ctx.enter_context(nc.psum_tensor("psum", [P, 4096], F32))

        def bank(b, n=512):
            return psum[:, b * 512:b * 512 + n]

        xT = sb("xT", [P, KD, T])
        hT = sb("hT", [P, KD, T])
        mixT = sb("mixT", [P, KD, T])
        cst = sb("cst", [P, NCONST])
        vec = sb("vec", [P, NVEC])
        ring = sb("ring", [P, RING, SLOT])
        sums = sb("sums", [P, 64])
        rstd = sb("rstd", [P, 64])
        mod = sb("mod", [P, 48, 2])
        gmod = sb("gmod", [P, 3 * KD])
        epsc = sb("epsc", [P, 1])
        ARENA = 22760
        arena = sb("arena", [P, ARENA])
        held = []

        def C(name, lo=0, n=None):
            at, w = CONST_AT[name]
            return cst[:, at + lo:at + (w if n is None else lo + n)]

        def V(name, lo=0, n=None):
            at, w = VEC_AT[name]
            return vec[:, at + lo:at + (w if n is None else lo + n)]

        ident = C("ident")

        weight_landed = [sem(f"weight_landed{i}") for i in range(RING)]
        weight_used = sem("weight_used")
        cursor = [0]
        issued = [0]
        read_at = []
        plain = [0]

        def feed(sync):
            while issued[0] < min(len(PLAN), cursor[0] + RING):
                i = issued[0]
                w = PLAN[i][1]
                if i >= RING:
                    sync.wait_ge(*read_at[i - RING])
                src = weights[PLAN_AT[i]:PLAN_AT[i] + P * w].rearrange("(p n) -> p n", p=P)
                sync.dma_start(ring[:, i % RING, 0:w], src).then_inc(weight_landed[i % RING], 16)
                issued[0] += 1

        def take(pe, name):
            i = cursor[0]
            assert PLAN[i][0] == name, (PLAN[i], name)
            cursor[0] += 1
            pe.wait_ge(weight_landed[i % RING], 16 * (i // RING + 1))
            return ring[:, i % RING, :]

        def used(signal, value):
            read_at.append((signal, value))

        def used_after(last):
            plain[0] += 1
            last.then_inc(weight_used, 1)
            read_at.append((weight_used, plain[0]))

        def chain(eng, name, make=None):
            s, n = (make or sem)(name), [0]

            def link(ins):
                n[0] += 1
                ins.then_inc(s, 1)
                eng.wait_ge(s, n[0])
            return link

        def product(pe, out, lhs, rhs, n):
            for k in range(n):
                last = pe.matmul(out, lhs(k), rhs(k), start=(k == 0), stop=(k == n - 1))
            return last

        vec_loaded, loaded = sem("vec_loaded"), sem("loaded")
        early = ExitStack()
        ctxT = mixT[:, 0:4, :].rearrange("p a (b n) -> p (a b) n", b=2)
        hcT = sb("hcT", [P, KD, TC], early)
        csil = sb("csil", [P, KD, 2], early)
        bm = V("b_mod")
        eps_set = sem("eps_set")
        with nc.Block() as block:
            @block.sync
            def _(sync):
                feed(sync)

            @block.vector
            def _(dve):
                dve.memset(epsc[:, :], EPS).then_inc(eps_set, 1)
                dve.wait_ge(eps_set, 1)

            @block.scalar
            def _(act):
                act.dma_start(vec[:, :], vecs_d).then_inc(vec_loaded, 16)
                act.dma_start(xT[:, :, :], x_d).then_inc(loaded, 16)
                act.dma_start(mixT[:, 0:4, :], ctx_d.rearrange("p (a b) n -> p a (b n)", b=2)).then_inc(loaded, 16)
                act.dma_start(cst[:, :], consts_d).then_inc(loaded, 16)
                act.wait_ge(vec_loaded, 16)

        silu_done, mod_done, biased = sem("silu_done"), sem("mod_done"), sem("biased")
        MODB = 6 * 512

        def mod_tile(pe, view, t):
            last = product(pe, psum[:, MODB + 2 * t:MODB + 2 * t + 2],
                           lambda k: view[:, k, (t % 4) * P:(t % 4 + 1) * P], lambda k: csil[:, k, :], KD)
            last.then_inc(mod_done, 1)
            if t % 4 == 3:
                used(mod_done, t + 1)

        def mod_finish(dve, a, b):
            dve.wait_ge(mod_done, b)
            bias = bm[:, a:b].rearrange("p (n o) -> p n o", o=1).to_broadcast([P, b - a, 2])
            dve.tensor_tensor(mod[:, a:b, :], psum[:, MODB + 2 * a:MODB + 2 * b].rearrange("p (n o) -> p n o", o=2),
                              bias, ALU.add).then_inc(biased, 1)
            dve.wait_ge(biased, 1 if a == 0 else 2)
            for at, norm_g, j, who in ((0, "norm1_g", 1, 0), (1, "norm1_g", 1, 1)) if a == 0 else ((2, "norm2_g", 4, 0),):
                dve.scalar_tensor_tensor(out=gmod[:, at * KD:(at + 1) * KD], in0=mod[:, j * KD:(j + 1) * KD, who],
                                         scalar=1.0, in1=V(norm_g), op0=ALU.add, op1=ALU.mult)

        with nc.Block() as block:
            @block.scalar
            def _(act):
                act.activation(csil[:, :, :].rearrange("p k n -> p (k n)"), V("c2"), ACT.Silu).then_inc(silu_done, 1)
                act.wait_ge(loaded, 48)

            @block.tensor
            def _(pe):
                pe.wait_ge(silu_done, 1)
                for t in range(16):
                    if t % 4 == 0:
                        view = take(pe, f"mod{t // 4}").rearrange("p (k n) -> p k n", k=KD)
                    mod_tile(pe, view, t)

            @block.vector
            def _(dve):
                mod_finish(dve, 0, 16)

            @block.sync
            def _(sync):
                feed(sync)

        norm_names = ("squares", "summed", "rooted", "inverted", "spread", "scaled", "row_free")
        norm_sems = [sem(n) for n in norm_names]
        norm_at = dict.fromkeys(norm_names, 0)

        def norm(src, sq, dst, kt, tiles, scale, gain, shift=None, heads=False, times=None,
                 presummed=False):
            base = dict(norm_at)
            first = 0 if presummed else 1
            for name, n in (("squares", first * kt), ("summed", first), ("rooted", 1), ("inverted", 1),
                            ("spread", kt if heads else 0), ("scaled", kt), ("row_free", max(0, kt - 6) if heads else 0)):
                norm_at[name] += n
            squares, summed, rooted, inverted, spread, scaled, row_free = norm_sems
            if not heads:
                norm_all(src, sq, dst, kt, tiles, scale, gain, shift, base, presummed)
                return
            ncol = 2 * kt * tiles

            def row_bank(r):
                return 1 + r % 6

            with nc.Block() as block:
                @block.scalar
                def _(act):
                    for k in range(kt):
                        act.activation(sq[:, k, :], src[:, k, :], ACT.Square).then_inc(squares, 1)
                    act.wait_ge(summed, base["summed"] + 1)
                    act.activation(sums[:, 0:ncol], psum[:, 0:ncol], ACT.Sqrt, bias=epsc[:, 0:1], scale=scale)\
                       .then_inc(rooted, 1)

                @block.tensor
                def _(pe):
                    for k in range(kt):
                        pe.wait_ge(squares, base["squares"] + k + 1)
                        for i in range(TT):
                            at = 2 * (k * TT + i)
                            last = pe.matmul(psum[:, at:at + 2], sq[:, k, i * P:(i + 1) * P],
                                             C("blk64")[:, 0:P:64], start=True, stop=True)
                    last.then_inc(summed, 1)
                    pe.wait_ge(inverted, base["inverted"] + 1)
                    for r in range(kt):
                        if r >= 6:
                            pe.wait_ge(row_free, base["row_free"] + r - 5)
                        for i in range(TT):
                            b = row_bank(r) * 512 + i * P
                            at = 2 * (r * TT + i)
                            for o in range(2):
                                last = pe.matmul(psum[64 * o:64 * o + 64, b:b + P],
                                                 rstd[:, at + o:at + o + 1].to_broadcast([P, 64]), ident,
                                                 start=True, stop=True)
                        last.then_inc(spread, 1)

                @block.vector
                def _(dve):
                    dve.wait_ge(rooted, base["rooted"] + 1)
                    dve.reciprocal(rstd[:, 0:ncol], sums[:, 0:ncol]).then_inc(inverted, 1)
                    for k in range(kt):
                        dve.wait_ge(spread, base["spread"] + k + 1)
                        dve.scalar_tensor_tensor(out=dst[:, k, :], in0=src[:, k, :], scalar=gain(k),
                                                 in1=bank(row_bank(k)), op0=ALU.mult, op1=ALU.mult).then_inc(scaled, 1)
                        if k < kt - 6:
                            dve.wait_ge(scaled, base["scaled"] + k + 1)
                            dve.sem_inc(row_free, 1)
                        if times is not None:
                            dve.wait_ge(scaled, base["scaled"] + k + 1)
                            dve.tensor_tensor(times(k), dst[:, k, :], times(k), ALU.mult)

                @block.sync
                def _(sync):
                    feed(sync)

        def norm_all(src, sq, dst, kt, tiles, scale, gain, shift, base, presummed):
            squares, summed, rooted, inverted, spread, scaled, row_free = norm_sems
            parts = [(a, min(4, tiles - a) * P) for a in range(0, tiles, 4)]
            width = tiles * P
            with nc.Block() as block:
                @block.scalar
                def _(act):
                    if not presummed:
                        for k in range(kt):
                            act.activation(sq[:, k, 0:width], src[:, k, 0:width], ACT.Square).then_inc(squares, 1)
                        act.wait_ge(summed, base["summed"] + 1)
                    act.activation(psum[:, 0:width], psum[:, 0:width], ACT.Sqrt, bias=epsc[:, 0:1], scale=scale)\
                       .then_inc(rooted, 1)
                    if shift is not None:
                        for k in range(kt):
                            act.wait_ge(scaled, base["scaled"] + k + 1)
                            act.activation(dst[:, k, 0:width], dst[:, k, 0:width], ACT.Identity, bias=shift(k),
                                           scale=1.0)

                @block.tensor
                def _(pe):
                    if presummed:
                        return
                    for k in range(kt):
                        pe.wait_ge(squares, base["squares"] + k + 1)
                        for a, n in parts:
                            last = pe.matmul(bank(a // 4, n), C("ones"), sq[:, k, a * P:a * P + n], start=(k == 0),
                                             stop=(k == kt - 1))
                    last.then_inc(summed, 1)

                @block.vector
                def _(dve):
                    dve.wait_ge(rooted, base["rooted"] + 1)
                    dve.reciprocal(psum[:, 1024:1024 + width], psum[:, 0:width]).then_inc(inverted, 1)
                    dve.wait_ge(inverted, base["inverted"] + 1)
                    for k in range(kt):
                        dve.scalar_tensor_tensor(out=dst[:, k, 0:width], in0=src[:, k, 0:width], scalar=gain(k),
                                                 in1=psum[:, 1024:1024 + width], op0=ALU.mult, op1=ALU.mult)\
                           .then_inc(scaled, 1)

                @block.sync
                def _(sync):
                    feed(sync)

        norm(xT, hT, hT, KD, TT, 1.0 / D, lambda k: gmod[:, k:k + 1], shift=lambda k: mod[:, k, 0:1])
        norm(ctxT, hcT, hcT, KD, TCT, 1.0 / D, lambda k: gmod[:, KD + k:KD + k + 1], shift=lambda k: mod[:, k, 1:2])

        s1 = ExitStack()
        v_hg = sb("v_hg", [P, TAT, HH * HV], early)
        s2 = ExitStack()
        fn_tok = sb("fn_tok", [P, TT, 256], s2)
        cqT = sb("cqT", [P, 2, T], s1)
        ckvT = sb("ckvT", [P, 1, TA], s1)
        kpe_raw = sb("kpe_raw", [P, TA], s1)
        tile_done, tile_out = sem("tile_done"), sem("tile_out")
        with nc.Block() as block:
            @block.tensor
            def _(pe):
                w = take(pe, "hi_fn").rearrange("p (k n) -> p k n", k=KD)
                for i in range(TT):
                    last = product(pe, bank(i), lambda k: hT[:, k, i * P:(i + 1) * P], lambda k: w[:, k, :], KD)
                    last.then_inc(tile_done, 1)
                for i in range(TCT):
                    last = product(pe, bank(4 + i, 256), lambda k: hcT[:, k, i * P:(i + 1) * P],
                                   lambda k: w[:, k, 0:256], KD)
                    last.then_inc(tile_done, 1)
                used(tile_done, 6)
                w = take(pe, "mla_in").rearrange("p (k n) -> p k n", k=KD)
                for j in range(4):
                    if j >= 2:
                        pe.wait_ge(tile_out, j - 1)
                    last = product(pe, bank((6 + j) % 8), lambda k: w[:, k, j * P:(j + 1) * P],
                                   lambda k: hT[:, k, :], KD)
                    last.then_inc(tile_done, 1)
                for j in (2, 3):
                    pe.wait_ge(tile_out, j + 1)
                    last = product(pe, bank(j, TC), lambda k: w[:, k, j * P:(j + 1) * P],
                                   lambda k: hcT[:, k, :], KD)
                    last.then_inc(tile_done, 1)
                used(tile_done, 12)
                w = take(pe, "hg_gate")[:, 0:8 * 256].rearrange("p (k n) -> p k n", k=KD)
                for j in range(2):
                    pe.wait_ge(tile_out, 5 + j)
                    last = product(pe, bank(4 + j), lambda k: w[:, k, j * P:(j + 1) * P], lambda k: hT[:, k, :], KD)
                    last.then_inc(tile_done, 1)
                used(tile_done, 14)

            @block.scalar
            def _(act):
                n = 0
                for i in range(TAT):
                    n += 1
                    act.wait_ge(tile_done, n)
                    if i < TT:
                        act.copy(fn_tok[:, i, :], bank(i)[:, 256:512])
                    act.copy(v_hg[:, i, :], bank(i, 256)).then_inc(tile_out, 1)
                for b, dst in ((6, cqT[:, 0, :]), (7, cqT[:, 1, :]), (0, ckvT[:, 0, 0:T]), (1, kpe_raw[:, 0:T])):
                    n += 1
                    act.wait_ge(tile_done, n)
                    act.copy(dst, bank(b)).then_inc(tile_out, 1)
                for b, dst in ((2, ckvT[:, 0, T:TA]), (3, kpe_raw[:, T:TA])):
                    n += 1
                    act.wait_ge(tile_done, n)
                    act.copy(dst, bank(b, TC)).then_inc(tile_out, 1)
                for j in range(2):
                    n += 1
                    act.wait_ge(tile_done, n)
                    act.activation(mixT[:, 4 + j, :], bank(4 + j), ACT.Silu)

            @block.sync
            def _(sync):
                feed(sync)

        s3 = ExitStack()
        fa = sb("fa", [P, 2, 2, T], s3)
        fm = sb("fm", [P, 2, T], s3)
        f_done, f_out = sem("f_done"), sem("f_out")
        with nc.Block() as block:
            @block.tensor
            def _(pe):
                w = take(pe, "dft").rearrange("p (f k n) -> p f k n", f=2, k=TT)
                for f in range(2):
                    for j in range(2):
                        last = product(pe, bank(2 * f + j), lambda k: fn_tok[:, k, j * P:(j + 1) * P],
                                       lambda k: w[:, f, k, :], TT)
                        last.then_inc(f_done, 1)
                used(f_done, 4)
                pe.wait_ge(f_out, 4)
                for j in range(2):
                    pe.matmul(bank(4 + j), C("dft_cos64"), fa[:, 0, j, :], start=True, stop=False)
                    pe.matmul(bank(4 + j), C("dft_nsin64"), fa[:, 1, j, :], start=False, stop=True).then_inc(f_done, 1)
                pe.wait_ge(f_out, 6)
                w = take(pe, "fourier")[:, 0:512].rearrange("p (k n) -> p k n", k=2)
                for j in range(2):
                    last = product(pe, bank(6 + j), lambda k: w[:, k, j * P:(j + 1) * P], lambda k: fm[:, k, :], 2)
                    last.then_inc(f_done, 1)
                used(f_done, 8)

            @block.scalar
            def _(act):
                for n in range(8):
                    act.wait_ge(f_done, n + 1)
                    dst = fa[:, n // 2, n % 2, :] if n < 4 else fm[:, n - 4, :] if n < 6 else mixT[:, n, :]
                    act.copy(dst, bank(n)).then_inc(f_out, 1)

            @block.sync
            def _(sync):
                feed(sync)
        s3.close()
        s2.close()

        norm(cqT, mixT, cqT, 2, TT, 1.0 / QL, lambda k: V("q_norm_g", k, 1))
        sqk = mixT[:, 0:2, :].rearrange("p (o a) n -> p o (a n)", o=1)
        norm(ckvT, sqk, ckvT, 1, TAT, 1.0 / KVL, lambda k: V("kv_norm_g", k, 1))
        s4 = ExitStack()
        qn = mixT[:, 0:4, :]
        qp = sb("qp", [P, 2, T], s4)
        kn = sb("kn", [P, MH, TA], s4)
        v_mla = sb("v_mla", [P, TAT, MH * VH], s4)
        t_done, t_out, rot_done, roped = sem("t_done"), sem("t_out"), sem("rot_done"), sem("roped")
        with nc.Block() as block:
            outs = [(T, qp[:, j, :]) for j in range(2)] + [(T, qn[:, h, :]) for h in range(MH)]
            outs += [(n, kn[:, h, a:a + n]) for h in range(MH) for a, n in ((0, T), (T, TC))]
            outs += [(512, v_mla[:, i, :]) for i in range(TAT)]

            @block.tensor
            def _(pe):
                ch = take(pe, "mla_up")
                wq = ch[:, 0:2 * 768].rearrange("p (k n) -> p k n", k=2)
                wkv = ch[:, 2 * 768:2 * 768 + 1024]
                for n, (width, _) in enumerate(outs):
                    if n >= 6:
                        pe.wait_ge(t_out, n - 5)
                    out = bank(n % 6, width)
                    if n < 6:
                        c0 = (512 + n * P) if n < 2 else (n - 2) * P
                        last = product(pe, out, lambda k: wq[:, k, c0:c0 + P], lambda k: cqT[:, k, :], 2)
                    elif n < 6 + 2 * MH:
                        h, a = (n - 6) // 2, (n - 6) % 2
                        last = pe.matmul(out, wkv[:, h * P:(h + 1) * P], ckvT[:, 0, a * T:a * T + width],
                                         start=True, stop=True)
                    else:
                        i = n - 6 - 2 * MH
                        last = pe.matmul(out, ckvT[:, 0, i * P:(i + 1) * P], wkv[:, 512:1024], start=True, stop=True)
                    last.then_inc(t_done, 1)
                used(t_done, len(outs))
                for r in range(3):
                    if r == 2:
                        pe.wait_ge(roped, 1)
                    src = qp[:, r, :] if r < 2 else kpe_raw[:, 0:T]
                    pe.wait_ge(t_out, 2)
                    pe.matmul(bank(6 + r % 2), C("rot_mla"), src, start=True, stop=True).then_inc(rot_done, 1)

            @block.scalar
            def _(act):
                for n, (width, dst) in enumerate(outs):
                    act.wait_ge(t_done, n + 1)
                    act.copy(dst, bank(n % 6, width)).then_inc(t_out, 1)

            @block.vector
            def _(dve):
                link = chain(dve, "rope_chain")
                for r in range(3):
                    x = qp[:, r, :] if r < 2 else kpe_raw[:, 0:T]
                    dve.wait_ge(rot_done, r + 1)
                    link(dve.tensor_tensor(bank(6 + r % 2), bank(6 + r % 2), C("sin_mla"), ALU.mult))
                    link(dve.tensor_tensor(x, x, C("cos_mla"), ALU.mult))
                    dve.tensor_tensor(x, x, bank(6 + r % 2), ALU.add).then_inc(roped, 1)

            @block.sync
            def _(sync):
                feed(sync)

        s5 = ExitStack()
        prob = sb("prob", [P, 2, TA], s5)
        probT = sb("probT", [P, 2, TAT, T], s5)
        stat = sb("stat", [P, 16, 4], s5)
        score_done, max_done, exp_done, prob_done = (sem(n) for n in ("score_done", "max_done", "exp_done", "prob_done"))
        turn_done, turn_a, turn_v, pv_done, pv_out = (sem(n) for n in ("turn_done", "turn_a", "turn_v", "pv_done", "pv_out"))
        units = [(h, i) for h in range(MH) for i in range(TT)]
        with nc.Block() as block:
            @block.tensor
            def _(pe):
                def scores(u):
                    h, i = units[u]
                    par = 64 * (h % 2)
                    if u >= 2:
                        pe.wait_ge(exp_done, u - 1)
                    for a, n in ((0, T), (T, TC)):
                        out = bank(2 * (u % 2) + a // T, n)
                        pe.matmul(out, qn[:, h, i * P:(i + 1) * P], kn[:, h, a:a + n], start=True, stop=False)
                        last = pe.matmul(out, qp[par:par + 64, h // 2, i * P:(i + 1) * P],
                                         kpe_raw[par:par + 64, a:a + n], start=False, stop=True)
                    last.then_inc(score_done, 1)

                def turn(u):
                    pe.wait_ge(prob_done, u + 1)
                    if u >= 1:
                        pe.wait_ge(turn_a, u)
                        pe.wait_ge(turn_v, u)
                    for k in range(TAT):
                        last = pe.transpose(psum[:, 4 * 512 + k * P:4 * 512 + (k + 1) * P],
                                            prob[:, u % 2, k * P:(k + 1) * P], ident)
                    last.then_inc(turn_done, 1)

                def values(h):
                    pe.wait_ge(turn_a, 4 * h + 4)
                    pe.wait_ge(turn_v, 4 * h + 4)
                    if h >= 2:
                        pe.wait_ge(pv_out, h - 1)
                    product(pe, bank(6 + h % 2), lambda k: v_mla[:, k, h * VH:(h + 1) * VH],
                            lambda k: probT[:, h % 2, k, :], TAT).then_inc(pv_done, 1)

                scores(0)
                scores(1)
                for u in range(16):
                    if u + 2 < 16:
                        scores(u + 2)
                    if u % 4 == 1 and u > 1:
                        values(u // 4 - 1)
                    turn(u)
                values(MH - 1)

            @block.vector
            def _(dve):
                link = chain(dve, "softmax_chain")

                def peak(u):
                    dve.wait_ge(score_done, u + 1)
                    s = psum[:, 2 * (u % 2) * 512:2 * (u % 2) * 512 + TA]
                    link(dve.tensor_reduce(stat[:, u, 0:1], s, AX.X, ALU.max, negate=True))
                    dve.tensor_scalar(stat[:, u, 1:2], stat[:, u, 0:1], MLA_SCALE, None, ALU.mult).then_inc(max_done, 1)

                def out(u):
                    h, i = units[u]
                    dve.wait_ge(turn_done, u + 1)
                    dve.tensor_copy(probT[:, h % 2, 4:6, i * P:(i + 1) * P],
                                    bank(5, 256).rearrange("p (k n) -> p k n", k=2)).then_inc(turn_v, 1)

                peak(0)
                peak(1)
                for u in range(16):
                    dve.wait_ge(exp_done, u + 1)
                    link(dve.reciprocal(stat[:, u, 3:4], stat[:, u, 2:3]))
                    dve.tensor_scalar(prob[:, u % 2, :], prob[:, u % 2, :], stat[:, u, 3:4], None, ALU.mult)\
                       .then_inc(prob_done, 1)
                    if u + 2 < 16:
                        peak(u + 2)
                    out(u)

            @block.scalar
            def _(act):
                def exps(u):
                    act.wait_ge(max_done, u + 1)
                    if u >= 2:
                        act.wait_ge(turn_done, u - 1)
                    s = psum[:, 2 * (u % 2) * 512:2 * (u % 2) * 512 + TA]
                    act.activation(prob[:, u % 2, :], s, ACT.Exp, bias=stat[:, u, 1:2], scale=MLA_SCALE,
                                   accum_out=stat[:, u, 2:3]).then_inc(exp_done, 1)

                exps(0)
                for u in range(16):
                    h, i = units[u]
                    if u + 1 < 16:
                        exps(u + 1)
                    act.wait_ge(turn_done, u + 1)
                    act.copy(probT[:, h % 2, 0:4, i * P:(i + 1) * P],
                             bank(4).rearrange("p (k n) -> p k n", k=4)).then_inc(turn_a, 1)
                    if i == 1 and h >= 1:
                        act.wait_ge(pv_done, h)
                        act.copy(mixT[:, h - 1, :], bank(6 + (h - 1) % 2)).then_inc(pv_out, 1)
                act.wait_ge(pv_done, MH)
                act.copy(mixT[:, MH - 1, :], bank(6 + (MH - 1) % 2)).then_inc(pv_out, 1)
        s5.close()
        s4.close()
        s1.close()

        s6 = ExitStack()
        WB = P + 1
        hq = sb("hq", [P, HH, T], s6)
        kk = sb("kk", [P, 2, HH, TA], s6)
        cum = sb("cum", [P, 2 * HH, TAT, WB], s6)
        lb = sb("lb", [P, 4, 8], s6)
        logf = sb("logf", [P, 2, TA], s6)
        z_done, z_out, sig_done, f_done, ln_done, scan_done = (
            sem(n) for n in ("z_done", "z_out", "sig_done", "f_done", "ln_done", "scan_done"))
        with nc.Block() as block:
            @block.tensor
            def _(pe):
                n = 0
                for d, name in enumerate(("hff", "hfb")):
                    w = take(pe, name).rearrange("p (k n) -> p k n", k=KD)
                    for h in range(HH):
                        for part, src in ((0, hT), (1, hcT)):
                            if n >= 8:
                                pe.wait_ge(sig_done, n - 7)
                            last = product(pe, bank(n % 8, T if part == 0 else TC),
                                           lambda k: w[:, k, h * P:(h + 1) * P], lambda k: src[:, k, :], KD)
                            last.then_inc(z_done, 1)
                            n += 1
                    used(z_done, n)
                w = take(pe, "hq").rearrange("p (k n) -> p k n", k=KD)
                for h in range(HH):
                    pe.wait_ge(sig_done, n - 7)
                    last = product(pe, bank(n % 8), lambda k: w[:, k, h * P:(h + 1) * P], lambda k: hT[:, k, :], KD)
                    last.then_inc(z_done, 1)
                    n += 1
                used(z_done, n)

            @block.scalar
            def _(act):
                for n in range(16):
                    act.wait_ge(z_done, n + 1)
                    j, part = n // 2, n % 2
                    width = T if part == 0 else TC
                    act.activation(kk[:, j // 4, j % 4, part * T:part * T + width], bank(n % 8, width), ACT.Sigmoid)\
                       .then_inc(sig_done, 1)
                for h in range(HH):
                    act.wait_ge(z_done, 17 + h)
                    act.activation(hq[:, h, :], bank((16 + h) % 8), ACT.Silu).then_inc(sig_done, 1)
                for j in range(2 * HH):
                    act.wait_ge(f_done, j + 1)
                    if j >= 2:
                        act.wait_ge(scan_done, j - 1)
                    act.activation(logf[:, j % 2, :], kk[:, j // 4, j % 4, :], ACT.Ln).then_inc(ln_done, 1)

            @block.vector
            def _(dve):
                link = chain(dve, "gate_chain")
                p = V("lb_param")
                link(dve.tensor_tensor(lb[:, 0, :], p, p, ALU.subtract))
                link(dve.tensor_scalar(lb[:, 1, :], lb[:, 0, :], 1.0, None, ALU.add))
                link(dve.tensor_tensor(lb[:, 2, :], lb[:, 1, :], lb[:, 1, :], ALU.subtract))
                link(dve.tensor_scalar(lb[:, 3, :], lb[:, 2, :], -1.0, 1.0, ALU.mult, ALU.add))
                link(dve.memset(cum[:, :, :, 0:1], 0.0))
                for j in range(2 * HH):
                    k = kk[:, j // 4, j % 4, :]
                    dve.wait_ge(sig_done, 2 * j + 2)
                    link(dve.tensor_scalar(k, k, lb[:, 3, j:j + 1], lb[:, 2, j:j + 1], ALU.mult, ALU.add))
                    dve.tensor_scalar(k, k, 2.0 ** -63, None, ALU.max).then_inc(f_done, 1)
                for j in range(2 * HH):
                    dve.wait_ge(ln_done, j + 1)
                    k = kk[:, j // 4, j % 4, :]
                    dve.tensor_scalar(k, k, -1.0, 1.0, ALU.mult, ALU.add)
                    for i in range(TAT):
                        x = logf[:, j % 2, i * P:(i + 1) * P]
                        last = dve.tensor_tensor_scan(cum[:, j, i, 1:WB], C("ones"), x, 0.0, ALU.mult, ALU.add)
                    last.then_inc(scan_done, 1)

            @block.sync
            def _(sync):
                feed(sync)

        wsc = hT[:, 0:4, :]
        e_buf = [hT[:, 4, :], hT[:, 5, :]]
        q_buf = [hT[:, 6, :], hT[:, 7, :]]
        k_buf = [hcT[:, 0:2, :].rearrange("p a b -> p (a b)"), hcT[:, 2:4, :].rearrange("p a b -> p (a b)")]
        k_sum = hcT[:, 4:6, :].rearrange("p a b -> p (a b)")
        d_buf = [logf[:, 0, 0:T], logf[:, 1, 0:T]]
        s7 = ExitStack()
        state = sb("state", [P, 2 * HH, 6, HV], s7)
        dec = sb("dec", [P, 2 * HH, TAT], s7)
        lev_units = [(h, d, lev) for h in range(HH) for d in range(2) for lev in range(LEVELS)]
        NU = len(lev_units)

        def halves(ap, lev):
            v = ap.rearrange("p i (b s n) -> p i b s n", s=2, n=1 << lev)
            return v[:, :, :, 0, :], v[:, :, :, 1, :]

        diff_done, e_done, pair_done, lev_done, sel_done, ksum_done = (
            sem(n) for n in ("diff_done", "e_done", "pair_done", "lev_done", "sel_done", "ksum_done"))
        diag_done = sem("diag_done")
        with nc.Block() as block:
            @block.vector
            def _(dve):
                link = chain(dve, "pair_chain")

                def differ(u):
                    h, d, lev = lev_units[u]
                    j = d * HH + h
                    if u >= 2:
                        dve.wait_ge(e_done, u - 1)
                    view = cum[:, j, 0:TT, 1 - d:WB - d]
                    first, second = halves(view, lev)
                    df, ds = halves(d_buf[u % 2].rearrange("p (i n) -> p i n", i=TT), lev)
                    half = 1 << lev
                    nb = 64 // half
                    mid = cum[:, j, 0:TT, half:P:2 * half].rearrange("p i (b o) -> p i b o", o=1)\
                        .to_broadcast([P, TT, nb, half])
                    dve.tensor_tensor(df, mid, first, ALU.subtract)
                    dve.tensor_tensor(ds, second, mid, ALU.subtract).then_inc(diff_done, 1)

                def pairs(u):
                    h, d, lev = lev_units[u]
                    if u % (2 * LEVELS) == 0:
                        if h >= 1:
                            dve.wait_ge(diag_done, h)
                        dve.tensor_tensor(k_sum, kk[:, 0, h, 0:T], kk[:, 1, h, 0:T], ALU.add).then_inc(ksum_done, 1)
                    dve.wait_ge(e_done, u + 1)
                    if u >= 2:
                        dve.wait_ge(lev_done, u - 1)
                    ef, es = halves(e_buf[u % 2].rearrange("p (i n) -> p i n", i=TT), lev)
                    qf, qs = halves(q_buf[u % 2].rearrange("p (i n) -> p i n", i=TT), lev)
                    kf, ks = halves(k_buf[u % 2].rearrange("p (i n) -> p i n", i=TT), lev)
                    q1, q2 = halves(hq[:, h, :].rearrange("p (i n) -> p i n", i=TT), lev)
                    k1, k2 = halves(kk[:, d, h, 0:T].rearrange("p (i n) -> p i n", i=TT), lev)
                    if d == 0:
                        dve.tensor_tensor(qs, q2, es, ALU.mult)
                        dve.tensor_tensor(kf, k1, ef, ALU.mult).then_inc(pair_done, 1)
                    else:
                        dve.tensor_tensor(qf, q1, ef, ALU.mult)
                        dve.tensor_tensor(ks, k2, es, ALU.mult).then_inc(pair_done, 1)

                def choose(u):
                    h, d, lev = lev_units[u]
                    w = wsc[:, h, :].rearrange("p (i n) -> p i n", i=TT)
                    if u % (2 * LEVELS) == 0:
                        dve.wait_ge(diag_done, h + 1)
                        link(dve.tensor_copy(w, bank(4 + h % 2).rearrange("p (i n) -> p i n", i=TT)))
                    dve.wait_ge(lev_done, u + 1)
                    mask = C(("first_second" if d == 0 else "second_first") + str(lev)).bitcast(U32)
                    mask = mask.rearrange("p (o n) -> p o n", o=1).to_broadcast([P, TT, P])
                    link(dve.copy_predicated(w, mask, bank(u % 4).rearrange("p (i n) -> p i n", i=TT)))
                    dve.sem_inc(sel_done, 1)

                for b in (q_buf[0], q_buf[1], k_buf[0], k_buf[1]):
                    link(dve.memset(b, 0.0))
                differ(0)
                for u in range(NU):
                    if u + 1 < NU:
                        differ(u + 1)
                    pairs(u)
                    if u >= 1:
                        choose(u - 1)
                choose(NU - 1)
                mod_finish(dve, 16, 48)

            @block.scalar
            def _(act):
                for j in range(2 * HH):
                    act.activation(dec[:, j, :], cum[:, j, :, P], ACT.Exp)
                for u in range(NU):
                    act.wait_ge(diff_done, u + 1)
                    if u >= 2:
                        act.wait_ge(pair_done, u - 1)
                    act.activation(e_buf[u % 2], d_buf[u % 2], ACT.Exp).then_inc(e_done, 1)

            @block.tensor
            def _(pe):
                for u in range(NU):
                    h, d, lev = lev_units[u]
                    if u % (2 * LEVELS) == 0:
                        pe.wait_ge(ksum_done, h + 1)
                        if h >= 2:
                            pe.wait_ge(sel_done, (h - 1) * 2 * LEVELS)
                        for i in range(TT):
                            last = pe.matmul(bank(4 + h % 2)[:, i * P:(i + 1) * P], k_sum[:, i * P:(i + 1) * P],
                                             hq[:, h, i * P:(i + 1) * P], start=True, stop=True)
                        last.then_inc(diag_done, 1)
                    pe.wait_ge(pair_done, u + 1)
                    if u >= 4:
                        pe.wait_ge(sel_done, u - 3)
                    for i in range(TT):
                        sl = slice(i * P, (i + 1) * P)
                        last = pe.matmul(bank(u % 4)[:, sl], k_buf[u % 2][:, sl], q_buf[u % 2][:, sl],
                                         start=True, stop=True)
                    last.then_inc(lev_done, 1)
                    t = 16 + u - 4
                    if 16 <= t < 48:
                        if t % 4 == 0:
                            view = take(pe, f"mod{t // 4}").rearrange("p (k n) -> p k n", k=KD)
                        mod_tile(pe, view, t)

            @block.sync
            def _(sync):
                feed(sync)

        kd_all = hT[:, 4:6, :].rearrange("p a b -> p (a b)")
        kt_all = hT[:, 6:8, :].rearrange("p a b -> p (a b)")
        order = ((4, 5, 0, 1, 2), (5, 4, 3, 2, 1))
        kd_ready, kd_e, kd_turn, kd_tok, kd_upd, kd_state = (
            sem(n) for n in ("kd_ready", "kd_e", "kd_turn", "kd_tok", "kd_upd", "kd_state"))
        with nc.Block() as block:
            @block.vector
            def _(dve):
                link = chain(dve, "state_chain")
                for j in range(2 * HH):
                    d, h = j // HH, j % HH
                    kd = kd_all[:, 0:TA].rearrange("p (i n) -> p i n", i=TAT)
                    if d == 0:
                        end = cum[:, j, :, P:WB].to_broadcast([P, TAT, P])
                        if j >= 1:
                            dve.wait_ge(kd_turn, j)
                        dve.tensor_tensor(kd, end, cum[:, j, :, 1:WB], ALU.subtract).then_inc(kd_ready, 1)
                    dve.wait_ge(kd_e, j + 1)
                    dve.tensor_tensor(kd, kd, kk[:, d, h, :].rearrange("p (i n) -> p i n", i=TAT), ALU.mult)\
                       .then_inc(kd_ready, 1)
                    dve.wait_ge(kd_turn, j + 1)
                    dve.tensor_copy(kt_all[:, 0:5 * P], psum[:, 0:5 * P]).then_inc(kd_tok, 1)
                    dve.wait_ge(kd_upd, j + 1)
                    for n in range(5):
                        u_n = bank(2)[:, n * HV:(n + 1) * HV]
                        if n == 0:
                            link(dve.tensor_copy(state[:, j, 1, :], u_n))
                        else:
                            i = order[d][n]
                            link(dve.scalar_tensor_tensor(out=state[:, j, n + 1, :], in0=state[:, j, n, :],
                                                          scalar=dec[:, j, i:i + 1], in1=u_n, op0=ALU.mult,
                                                          op1=ALU.add))
                    dve.sem_inc(kd_state, 1)

            @block.scalar
            def _(act):
                for j in range(2 * HH):
                    d = j // HH
                    kd = kd_all[:, 0:TA].rearrange("p (i n) -> p i n", i=TAT)
                    if d == 0:
                        act.wait_ge(kd_ready, 2 * j + 1)
                        act.activation(kd, kd, ACT.Exp).then_inc(kd_e, 1)
                    else:
                        act.wait_ge(kd_turn, j)
                        act.activation(kd, cum[:, j, :, 0:P], ACT.Exp).then_inc(kd_e, 1)

            @block.tensor
            def _(pe):
                for j in range(2 * HH):
                    d, h = j // HH, j % HH
                    pe.wait_ge(kd_ready, 2 * j + 2 if d == 0 else HH + j + 1)
                    if j >= 1:
                        pe.wait_ge(kd_tok, j)
                    for n in range(5):
                        i = order[d][n]
                        last = pe.transpose(psum[:, n * P:(n + 1) * P], kd_all[:, i * P:(i + 1) * P], ident)
                    last.then_inc(kd_turn, 1)
                    pe.wait_ge(kd_tok, j + 1)
                    if j >= 1:
                        pe.wait_ge(kd_state, j)
                    for n in range(5):
                        i = order[d][n]
                        last = pe.matmul(bank(2)[:, n * HV:(n + 1) * HV], kt_all[:, n * P:(n + 1) * P],
                                         v_hg[:, i, h * HV:(h + 1) * HV], start=True, stop=True)
                    last.then_inc(kd_upd, 1)

        o_hg = logf.rearrange("p a n -> p (a n)")[:, 0:2 * T].rearrange("p (a n) -> p a n", a=2)
        qd = [hT[:, 4, :], hT[:, 5, :]]
        qd2 = [hT[:, 6, :], hT[:, 7, :]]
        qe_diff, qe_exp, qe_done, oh_done = (sem(n) for n in ("qe_diff", "qe_exp", "qe_done", "oh_done"))
        with nc.Block() as block:
            @block.vector
            def _(dve):
                for h in range(HH):
                    b = h % 2
                    if h >= 2:
                        dve.wait_ge(oh_done, h - 1)
                    j = HH + h
                    end = cum[:, j, 0:TT, P:WB].to_broadcast([P, TT, P])
                    dve.tensor_tensor(qd2[b].rearrange("p (i n) -> p i n", i=TT), end, cum[:, j, 0:TT, 0:P],
                                      ALU.subtract).then_inc(qe_diff, 1)
                    dve.wait_ge(qe_exp, h + 1)
                    dve.tensor_tensor(qd[b], qd[b], hq[:, h, :], ALU.mult)
                    dve.tensor_tensor(qd2[b], qd2[b], hq[:, h, :], ALU.mult).then_inc(qe_done, 1)

            @block.scalar
            def _(act):
                for h in range(HH):
                    b = h % 2
                    if h >= 2:
                        act.wait_ge(oh_done, h - 1)
                    act.activation(qd[b].rearrange("p (i n) -> p i n", i=TT), cum[:, h, 0:TT, 1:WB], ACT.Exp)
                    act.wait_ge(qe_diff, h + 1)
                    act.activation(qd2[b], qd2[b], ACT.Exp).then_inc(qe_exp, 1)
                for h in range(HH):
                    act.wait_ge(oh_done, h + 1)
                    par = 64 * (h % 2)
                    act.copy(o_hg[par:par + 64, h // 2, :], psum[par:par + 64, h * 512:(h + 1) * 512])

            @block.tensor
            def _(pe):
                for h in range(HH):
                    b, par = h % 2, 64 * (h % 2)
                    pe.wait_ge(qe_done, h + 1)
                    for i in range(TT):
                        out = psum[par:par + 64, h * 512 + i * P:h * 512 + (i + 1) * P]
                        sl = slice(i * P, (i + 1) * P)
                        pe.matmul(out, v_hg[:, i, h * HV:(h + 1) * HV], wsc[:, h, sl], start=True, stop=False)
                        pe.matmul(out, state[:, h, 2 + i, :], qd[b][:, sl], start=False, stop=False)
                        last = pe.matmul(out, state[:, HH + h, 5 - i, :], qd2[b][:, sl], start=False, stop=True)
                    last.then_inc(oh_done, 1)
        norm(o_hg, hT, o_hg, 2, TT, 1.0 / HV, lambda k: V("hg_norm_g", k, 1), heads=True,
             times=lambda k: mixT[:, 4 + k, :])
        s7.close()
        s6.close()

        early.close()

        acc_done, projected = sem("acc_done"), [0]

        x_set, sq_set = sem("x_set"), sem("sq_set")

        def project(names, src, kts, gate):
            base = projected[0]
            projected[0] += 8
            with nc.Block() as block:
                @block.tensor
                def _(pe):
                    for half in range(2):
                        k0 = 0
                        for c, name in enumerate(names[half]):
                            kt = kts[c]
                            w = take(pe, name)[:, 0:kt * 512].rearrange("p (k n) -> p k n", k=kt)
                            for j in range(4):
                                for k in range(kt):
                                    last = pe.matmul(bank(4 * half + j), w[:, k, j * P:(j + 1) * P],
                                                     src[:, k0 + k, :], start=(k0 + k == 0),
                                                     stop=(k0 + k == sum(kts) - 1))
                                if c == len(kts) - 1:
                                    last.then_inc(acc_done, 1)
                            if c == len(kts) - 1:
                                used(acc_done, base + 4 * half + 4)
                            else:
                                used_after(last)
                            k0 += kt
                    pe.wait_ge(x_set, base + 1)
                    for n in range(8):
                        pe.wait_ge(sq_set, base + n + 1)
                        pe.matmul(bank(0), C("ones"), hT[:, n, :], start=(n == 0), stop=(n == 7))

                @block.scalar
                def _(act):
                    for n in range(8):
                        act.wait_ge(x_set, base + n + 1)
                        act.activation(hT[:, n, :], xT[:, n, :], ACT.Square).then_inc(sq_set, 1)

                @block.vector
                def _(dve):
                    for n in range(8):
                        dve.wait_ge(acc_done, base + n + 1)
                        if gate is None:
                            ins = dve.tensor_tensor(xT[:, n, :], bank(n), xT[:, n, :], ALU.add)
                        else:
                            ins = dve.scalar_tensor_tensor(out=xT[:, n, :], in0=bank(n), scalar=gate(n),
                                                           in1=xT[:, n, :], op0=ALU.mult, op1=ALU.add)
                        ins.then_inc(x_set, 1)

                @block.sync
                def _(sync):
                    feed(sync)

        project([["out0"], ["out1"]], mixT, [8], lambda n: mod[:, 2 * KD + n, 0:1])
        norm(xT, hT, hT, KD, TT, 1.0 / D, lambda k: gmod[:, 2 * KD + k:2 * KD + k + 1],
             shift=lambda k: mod[:, 3 * KD + k, 0:1], presummed=True)
        s8 = ExitStack()
        hid = sb("hid", [P, 32, T], s8)
        gu_done, gate_out, up_out = sem("gu_done"), sem("gate_out"), sem("up_out")
        with nc.Block() as block:
            @block.tensor
            def _(pe):
                for c in range(11):
                    w = take(pe, f"gu{c}").rearrange("p (k n) -> p k n", k=KD)
                    if c >= 2:
                        pe.wait_ge(gate_out, 2 * (c - 1))
                        pe.wait_ge(up_out, 2 * (c - 1))
                    for j in range(4):
                        last = product(pe, bank(4 * (c % 2) + j), lambda k: w[:, k, j * P:(j + 1) * P],
                                       lambda k: hT[:, k, :], KD)
                        last.then_inc(gu_done, 1)
                    used(gu_done, 4 * c + 4)

            @block.scalar
            def _(act):
                for c in range(11):
                    for j in range(2):
                        act.wait_ge(gu_done, 4 * c + j + 1)
                        act.activation(hid[:, 2 * c + j, :], bank(4 * (c % 2) + j), ACT.Silu).then_inc(gate_out, 1)

            @block.vector
            def _(dve):
                for c in range(11):
                    for j in range(2):
                        dve.wait_ge(gu_done, 4 * c + j + 3)
                        dve.wait_ge(gate_out, 2 * c + j + 1)
                        dve.tensor_tensor(hid[:, 2 * c + j, :], hid[:, 2 * c + j, :], bank(4 * (c % 2) + 2 + j),
                                          ALU.mult).then_inc(up_out, 1)

            @block.sync
            def _(sync):
                feed(sync)
        project([[f"dn{h}_{k}" for k in range(3)] for h in range(2)], hid, [8, 8, 6],
                lambda n: mod[:, 5 * KD + n, 0:1])
        s8.close()
        norm(xT, hT, xT, KD, TT, 1.0 / D, lambda k: V("final_norm_g", k, 1), presummed=True)

        norm(xT, hT, hT, KD, TT, 1.0 / D, lambda k: V("mix0", k, 1))
        e1 = ExitStack()
        cv = sb("cv", [P, 12, T], e1)
        tok = sb("tok", [P, 12, TT * GH], e1)
        e2 = ExitStack()
        ch = sb("ch", [P, 4, T], e2)
        cs = sb("cs", [P, 4, T], e2)
        p_done, conv_out, act_out = sem("p_done"), sem("conv_out"), sem("act_out")
        z_out, cg_out, hs_out = sem("z_out"), sem("cg_out"), sem("hs_out")
        with nc.Block() as block:
            @block.tensor
            def _(pe):
                w = take(pe, "ev_ab")[:, 0:128].rearrange("p (k n) -> p k n", k=KD)
                for i in range(TT):
                    last = product(pe, psum[:, i * 16:(i + 1) * 16], lambda k: hT[:, k, i * P:(i + 1) * P],
                                   lambda k: w[:, k, :], KD)
                used_after(last)
                for n in range(28):
                    if n % 4 == 0:
                        w = take(pe, f"ev{n // 4}").rearrange("p (k n) -> p k n", k=KD)
                    m = n - 7
                    if 0 <= m < 12:
                        pe.wait_ge(conv_out, m + 1)
                    elif 12 <= m < 20:
                        pe.wait_ge(z_out, m - 12 + 1)
                    elif m >= 20:
                        pe.wait_ge(hs_out, m - 20 + 1)
                    last = product(pe, bank(1 + n % 7), lambda k: w[:, k, (n % 4) * P:(n % 4 + 1) * P],
                                   lambda k: hT[:, k, :], KD)
                    last.then_inc(p_done, 1)
                    if n % 4 == 3:
                        used(p_done, n + 1)

            @block.vector
            def _(dve):
                link = chain(dve, "conv_chain")

                def conv(dst, src, taps, width, last_sem):
                    link(dve.tensor_scalar(dst, src, taps(width - 1), None, ALU.mult))
                    for j in range(1, width):
                        ins = dve.scalar_tensor_tensor(out=dst[:, j:T], in0=src[:, 0:T - j], scalar=taps(width - 1 - j),
                                                       in1=dst[:, j:T], op0=ALU.mult, op1=ALU.add)
                        if j < width - 1:
                            link(ins)
                    ins.then_inc(last_sem, 1)

                for n in range(12):
                    dve.wait_ge(p_done, n + 1)
                    conv(cv[:, n, :], bank(1 + n % 7), lambda j: V("conv", 4 * n + j, 1), 4, conv_out)
                for n in range(20, 24):
                    i = n - 20
                    dve.wait_ge(p_done, n + 1)
                    dve.wait_ge(z_out, 4 + i + 1)
                    dve.tensor_tensor(ch[:, i, :], bank(1 + n % 7), ch[:, i, :], ALU.mult).then_inc(hs_out, 1)
                    dve.wait_ge(hs_out, i + 1)
                    conv(cs[:, i, :], ch[:, i, :], lambda j: V("sc_conv", 3 * i + j, 1), 3, cg_out)
                for n in range(24, 28):
                    i = n - 24
                    dve.wait_ge(p_done, n + 1)
                    dve.wait_ge(cg_out, i + 1)
                    dve.tensor_tensor(mixT[:, 4 + i, :], bank(1 + n % 7), cs[:, i, :], ALU.mult)

            @block.scalar
            def _(act):
                for n in range(12):
                    act.wait_ge(conv_out, n + 1)
                    act.activation(cv[:, n, :], cv[:, n, :], ACT.Silu)
                for n in range(12, 16):
                    act.wait_ge(p_done, n + 1)
                    act.activation(mixT[:, n - 12, :], bank(1 + n % 7), ACT.Silu).then_inc(z_out, 1)
                for n in range(16, 20):
                    act.wait_ge(p_done, n + 1)
                    act.copy(ch[:, n - 16, :], bank(1 + n % 7)).then_inc(z_out, 1)

            @block.sync
            def _(sync):
                feed(sync)
        e2.close()

        G, BETA, GC, GTOT, EGC, KDE, BEG, T0, T1, T2 = range(10)

        def tk(i):
            return tok[:, i, :].rearrange("p (c h) -> p c h", h=GH)

        lin, lin2, abs_done, exp1, sp_done, g_done, gc_done, gd2 = (
            sem(n) for n in ("lin", "lin2", "abs_done", "exp1", "sp_done", "g_done", "gc_done", "gd2"))
        alog = sb("alog", [P, GH], e1)
        with nc.Block() as block:
            ab = psum[:, 0:64].rearrange("p (c n) -> p c n", n=16)

            @block.vector
            def _(dve):
                link = chain(dve, "tok_chain")
                dtb = V("dt_bias").rearrange("p (o h) -> p o h", o=1).to_broadcast([P, TT, GH])
                dve.tensor_tensor(tk(T0), ab[:, :, 0:GH], dtb, ALU.add).then_inc(lin, 1)
                dve.wait_ge(sp_done, 1)
                link(dve.tensor_scalar(tk(T2), tk(T0), 0.0, None, ALU.max))
                link(dve.tensor_tensor(tk(T2), tk(T2), tk(T1), ALU.add))
                link(dve.tensor_scalar(tk(T2), tk(T2), -1.0, None, ALU.mult))
                ea = alog[:, :].rearrange("p (o h) -> p o h", o=1).to_broadcast([P, TT, GH])
                dve.tensor_tensor(tk(G), tk(T2), ea, ALU.mult).then_inc(g_done, 1)
                dve.wait_ge(gc_done, 1)
                link(dve.tensor_copy(tk(GC), psum[:, 512:544].rearrange("p (c h) -> p c h", h=GH)))
                dve.tensor_tensor(tk(T1), psum[:, 1024:1056].rearrange("p (c h) -> p c h", h=GH), tk(GC),
                                  ALU.subtract).then_inc(lin2, 1)
                dve.wait_ge(gd2, 1)
                dve.tensor_tensor(tk(BEG), tk(EGC), tk(BETA), ALU.mult)

            @block.scalar
            def _(act):
                act.activation(alog[:, :], V("a_log"), ACT.Exp)
                act.wait_ge(lin, 1)
                act.activation(tk(BETA), ab[:, :, GH:2 * GH], ACT.Sigmoid)
                act.activation(tk(T1), tk(T0), ACT.Abs).then_inc(abs_done, 1)
                act.wait_ge(abs_done, 1)
                act.activation(tk(T1), tk(T1), ACT.Exp, scale=-1.0).then_inc(exp1, 1)
                act.wait_ge(exp1, 1)
                act.activation(tk(T1), tk(T1), ACT.Ln, bias=1.0, scale=1.0).then_inc(sp_done, 1)
                act.wait_ge(lin2, 1)
                act.activation(tk(KDE), tk(T1), ACT.Exp)
                act.activation(tk(EGC), tk(GC), ACT.Exp).then_inc(gd2, 1)

            @block.tensor
            def _(pe):
                pe.wait_ge(g_done, 1)
                for c in range(TT):
                    pe.matmul(psum[:, 512 + c * GH:512 + (c + 1) * GH], C("upto"), tk(G)[:, c, :],
                              start=True, stop=True)
                for c in range(TT):
                    last = pe.matmul(psum[:, 1024 + c * GH:1024 + (c + 1) * GH], C("ones"), tk(G)[:, c, :],
                                     start=True, stop=True)
                last.then_inc(gc_done, 1)

        norm(cv, hT, cv, 8, TT, 1.0, lambda k: C("eighth") if k < 4 else C("one"), heads=True)

        mt = hT[:, 0:4, :]
        attn = hT[:, 4:8, :]
        e3 = ExitStack()
        X = sb("X", [P, 4, T], e3)
        XT = sb("XT", [P, 4, T], e3)
        Y = sb("Y", [P, 4, T], e3)
        ml = sb("ml", [P, 4, T], e3)
        kbg = sb("kbg", [P, TT, 4 * GD], e3)
        kde = sb("kde", [P, TT, 4 * GD], e3)
        bv = sb("bv", [P, TT, 4 * GD], e3)
        qg = sb("qg", [P, 2, T], e3)
        edge = sb("edge", [P, 4, TT], e3)
        st = sb("st", [P, 2, GD], e3)
        vn = sb("vn", [P, 4, GD], e3)

        def c4(ap):
            return ap.rearrange("p (c n) -> p c n", c=TT)

        half_sems = {}
        sem_of_program = sem

        def half_sem(name):
            if name not in half_sems:
                half_sems[name] = sem_of_program(name)
            return half_sems[name]

        for half in range(2):
            h0 = 4 * half
            if half:
                with nc.Block() as block:
                    @block.gpsimd
                    def _(pool):
                        for s in half_sems.values():
                            pool.sem_clear(s)
            kv_turn, kv_out = half_sem("kv_turn"), half_sem("kv_out")
            with nc.Block() as block:
                @block.tensor
                def _(pe):
                    for c in range(TT):
                        for s, base in enumerate((4, 8)):
                            for j in range(2):
                                at = c * 1024 + s * 512
                                last = pe.transpose(psum[:, at + j * P:at + (j + 1) * P],
                                                    cv[:, base + 2 * half + j, c * P:(c + 1) * P], ident)
                        last.then_inc(kv_turn, 1)

                @block.vector
                def _(dve):
                    for c in range(TT):
                        dve.wait_ge(kv_turn, c + 1)

                        def per_head(i):
                            return tk(i)[:, c, h0:h0 + 4].rearrange("p (h o) -> p h o", o=1).to_broadcast([P, 4, GD])

                        def heads(ap):
                            return ap.rearrange("p (h n) -> p h n", h=4)
                        k_t, v_t = heads(psum[:, c * 1024:c * 1024 + 256]), heads(psum[:, c * 1024 + 512:c * 1024 + 768])
                        dve.tensor_tensor(heads(kbg[:, c, :]), k_t, per_head(BEG), ALU.mult)
                        dve.tensor_tensor(heads(kde[:, c, :]), k_t, per_head(KDE), ALU.mult)
                        dve.tensor_tensor(heads(bv[:, c, :]), v_t, per_head(BETA), ALU.mult)

            raw_done, dt_done, dec_done, raw_free, edge_done = (
                half_sem(n) for n in ("raw_done", "dt_done", "dec_done", "raw_free", "edge_done"))
            with nc.Block() as block:
                @block.tensor
                def _(pe):
                    for n in range(4):
                        h = h0 + n
                        par, tile = 64 * (h % 2), h // 2
                        b = 4 * (n % 2)
                        if n >= 2:
                            pe.wait_ge(raw_free, n - 1)
                            pe.wait_ge(edge_done, n - 1)
                        for c in range(TT):
                            sl = slice(c * P, (c + 1) * P)
                            kT = cv[par:par + 64, 4 + tile, sl]
                            qT = cv[par:par + 64, tile, sl]
                            pe.matmul(bank(b)[:, sl], tk(G)[:, c, h:h + 1].to_broadcast([P, P]), C("upto"),
                                      start=True, stop=True)
                            pe.matmul(bank(b + 1)[:, sl], tk(BETA)[:, c, h:h + 1].to_broadcast([P, P]), ident,
                                      start=True, stop=True)
                            pe.matmul(bank(b + 2)[:, sl], kT, kT, start=True, stop=True)
                            last = pe.matmul(bank(b + 3)[:, sl], kT, qT, start=True, stop=True)
                        last.then_inc(raw_done, 1)

                @block.vector
                def _(dve):
                    link = chain(dve, "m_chain", half_sem)
                    for n in range(4):
                        h = h0 + n
                        b = 4 * (n % 2)
                        par, tile = 64 * (h % 2), h // 2
                        dve.wait_ge(raw_done, n + 1)
                        gc = tk(GC)[:, :, h:h + 1].to_broadcast([P, TT, P])
                        d = Y[:, n, :]
                        link(dve.tensor_tensor(c4(d), c4(bank(b)), gc, ALU.subtract))
                        dve.tensor_scalar(d, d, 0.0, None, ALU.min).then_inc(dt_done, 1)
                        dve.wait_ge(dec_done, n + 1)
                        upto = C("upto").rearrange("p (o n) -> p o n", o=1).to_broadcast([P, TT, P])
                        link(dve.tensor_tensor(c4(d), c4(d), upto, ALU.mult))
                        dve.tensor_tensor(attn[:, n, :], bank(b + 3), d, ALU.mult)
                        link(dve.tensor_tensor(mt[:, n, :], bank(b + 2), d, ALU.mult))
                        dve.tensor_tensor(mt[:, n, :], mt[:, n, :], bank(b + 1), ALU.mult).then_inc(raw_free, 1)
                        dve.wait_ge(edge_done, n + 1)
                        rows = slice(par, par + 64)
                        dve.tensor_tensor(qg[rows, n // 2, :], cv[rows, tile, :], X[rows, n, :], ALU.mult)

                @block.scalar
                def _(act):
                    for n in range(4):
                        b = 4 * (n % 2)
                        act.wait_ge(dt_done, n + 1)
                        act.activation(X[:, n, :], bank(b), ACT.Exp)
                        act.activation(edge[:, n, :], c4(bank(b))[:, :, P - 1], ACT.Exp).then_inc(edge_done, 1)
                        act.activation(Y[:, n, :], Y[:, n, :], ACT.Exp).then_inc(dec_done, 1)

            init_done, x_turn, xi_set = half_sem("init_done"), half_sem("x_turn"), half_sem("xi_set")
            ml_done, y_done, y_out, zz_done, xx_done = (half_sem(n) for n in ("ml_done", "y_done", "y_out", "zz_done", "xx_done"))
            NS = 4 * (LEVELS - 1)
            with nc.Block() as block:
                @block.vector
                def _(dve):
                    link = chain(dve, "init_chain", half_sem)
                    idb = ident.rearrange("p (o n) -> p o n", o=1).to_broadcast([P, TT, P])

                    def mask(lev):
                        return C(f"first_second{lev}").rearrange("p (o n) -> p o n", o=1).to_broadcast([P, TT, P])
                    for n in range(4):
                        link(dve.tensor_tensor(c4(XT[:, n, :]), c4(mt[:, n, :]), mask(0), ALU.mult))
                        dve.tensor_tensor(c4(XT[:, n, :]), idb, c4(XT[:, n, :]), ALU.subtract).then_inc(init_done, 1)

                    def masked(s):
                        lev, n = 1 + s // 4, s % 4
                        if s >= 4:
                            dve.wait_ge(y_done, s - 3)
                        dve.tensor_tensor(c4(ml[:, s % 4, :]), c4(mt[:, n, :]), mask(lev), ALU.mult).then_inc(ml_done, 1)
                    for s in range(4):
                        masked(s)
                    for s in range(NS):
                        n = s % 4
                        dve.wait_ge(zz_done, s + 1)
                        if s < NS - 4:
                            dve.tensor_tensor(X[:, n, :], X[:, n, :], bank(4 + 2 * (s % 2)), ALU.subtract)
                        dve.tensor_tensor(XT[:, n, :], XT[:, n, :], bank(5 + 2 * (s % 2)), ALU.subtract)\
                           .then_inc(xx_done, 1)
                        if s + 4 < NS:
                            masked(s + 4)

                @block.tensor
                def _(pe):
                    for n in range(4):
                        pe.wait_ge(init_done, n + 1)
                        for c in range(TT):
                            sl = slice(c * P, (c + 1) * P)
                            last = pe.transpose(bank(n)[:, sl], XT[:, n, sl], ident)
                        last.then_inc(x_turn, 1)

                    def first(s):
                        n = s % 4
                        pe.wait_ge(ml_done, s + 1)
                        if s >= 4:
                            pe.wait_ge(xx_done, s - 3)
                            pe.wait_ge(y_out, s - 3)
                        else:
                            pe.wait_ge(xi_set, n + 1)
                        for c in range(TT):
                            sl = slice(c * P, (c + 1) * P)
                            last = pe.matmul(bank(s % 4)[:, sl], ml[:, s % 4, sl], X[:, n, sl], start=True, stop=True)
                        last.then_inc(y_done, 1)

                    def second(s):
                        n = s % 4
                        pe.wait_ge(y_out, s + 1)
                        if s >= 2:
                            pe.wait_ge(xx_done, s - 1)
                        for c in range(TT):
                            sl = slice(c * P, (c + 1) * P)
                            if s < NS - 4:
                                pe.matmul(bank(4 + 2 * (s % 2))[:, sl], XT[:, n, sl], Y[:, n, sl], start=True, stop=True)
                            last = pe.matmul(bank(5 + 2 * (s % 2))[:, sl], Y[:, n, sl], XT[:, n, sl], start=True,
                                             stop=True)
                        last.then_inc(zz_done, 1)
                    first(0)
                    for s in range(NS):
                        if s + 1 < NS:
                            first(s + 1)
                        second(s)

                @block.scalar
                def _(act):
                    for n in range(4):
                        act.wait_ge(x_turn, n + 1)
                        act.copy(X[:, n, :], bank(n)).then_inc(xi_set, 1)
                    for s in range(NS):
                        act.wait_ge(y_done, s + 1)
                        if s >= 4:
                            act.wait_ge(zz_done, s - 3)
                        act.copy(Y[:, s % 4, :], bank(s % 4)).then_inc(y_out, 1)

            uw_done, uw_out = half_sem("uw_done"), half_sem("uw_out")
            u_v = X[:, 0:2, :].rearrange("p a (c n) -> p (a c) n", c=2)
            w_t = Y[:, 0:2, :]
            with nc.Block() as block:
                @block.tensor
                def _(pe):
                    for n in range(4):
                        par = 64 * (n % 2)
                        for c in range(TT):
                            sl = slice(c * P, (c + 1) * P)
                            pe.matmul(bank(n)[:, c * GD:(c + 1) * GD], XT[:, n, sl], bv[:, c, n * GD:(n + 1) * GD],
                                      start=True, stop=True)
                        for c in range(TT):
                            sl = slice(c * P, (c + 1) * P)
                            last = pe.matmul(psum[par:par + 64, (4 + n) * 512 + c * P:(4 + n) * 512 + (c + 1) * P],
                                             kbg[:, c, n * GD:(n + 1) * GD], XT[:, n, sl], start=True, stop=True)
                        last.then_inc(uw_done, 1)

                @block.scalar
                def _(act):
                    for n in range(4):
                        par = 64 * (n % 2)
                        act.wait_ge(uw_done, n + 1)
                        act.copy(u_v[:, n, :], bank(n, 256))
                        act.copy(w_t[par:par + 64, n // 2, :], psum[par:par + 64, (4 + n) * 512:(5 + n) * 512])

            pred_done, vn_done, o_done, up_done, st_done = (
                half_sem(n) for n in ("pred_done", "vn_done", "o_done", "up_done", "st_done"))
            with nc.Block() as block:
                @block.tensor
                def _(pe):
                    for c in range(TT):
                        sl = slice(c * P, (c + 1) * P)
                        for n in range(4):
                            par = 64 * (n % 2)
                            rows = slice(par, par + 64)
                            if c >= 1:
                                pe.wait_ge(st_done, 4 * (c - 1) + n + 1)
                                pe.matmul(bank(n)[:, 0:GD], w_t[rows, n // 2, sl], st[rows, n // 2, :],
                                          start=True, stop=True).then_inc(pred_done, 1)
                        for n in range(4):
                            par = 64 * (n % 2)
                            rows = slice(par, par + 64)
                            pe.wait_ge(vn_done, 4 * c + n + 1)
                            out = psum[par:par + 64, (4 + n) * 512 + c * P:(4 + n) * 512 + (c + 1) * P]
                            pe.matmul(out, vn[:, n, :], attn[:, n, sl], start=True, stop=(c == 0))
                            if c >= 1:
                                pe.matmul(out, st[rows, n // 2, :], qg[rows, n // 2, sl], start=False, stop=True)
                            pe.matmul(psum[par:par + 64, n * 512 + 256:n * 512 + 256 + GD],
                                      kde[:, c, n * GD:(n + 1) * GD], vn[:, n, :], start=True, stop=True)\
                              .then_inc(up_done, 1)

                @block.vector
                def _(dve):
                    for c in range(TT):
                        for n in range(4):
                            u_c = u_v[:, n, c * GD:(c + 1) * GD]
                            if c == 0:
                                dve.tensor_copy(vn[:, n, :], u_c).then_inc(vn_done, 1)
                            else:
                                dve.wait_ge(pred_done, 4 * (c - 1) + n + 1)
                                dve.wait_ge(up_done, 4 * (c - 1) + n + 1)
                                dve.tensor_tensor(vn[:, n, :], u_c, bank(n)[:, 0:GD], ALU.subtract).then_inc(vn_done, 1)
                        for n in range(4):
                            par = 64 * (n % 2)
                            rows = slice(par, par + 64)
                            dve.wait_ge(up_done, 4 * c + n + 1)
                            up = psum[rows, n * 512 + 256:n * 512 + 256 + GD]
                            if c == 0:
                                dve.tensor_copy(st[rows, n // 2, :], up).then_inc(st_done, 1)
                            else:
                                dve.wait_ge(st_done, 4 * (c - 1) + n + 1)
                                dve.scalar_tensor_tensor(out=st[rows, n // 2, :], in0=st[rows, n // 2, :],
                                                         scalar=edge[rows, n, c:c + 1], in1=up, op0=ALU.mult,
                                                         op1=ALU.add).then_inc(st_done, 1)

                @block.scalar
                def _(act):
                    act.wait_ge(up_done, 16)
                    for n in range(4):
                        par = 64 * (n % 2)
                        act.copy(cv[par:par + 64, 8 + 2 * half + n // 2, :],
                                 psum[par:par + 64, (4 + n) * 512:(5 + n) * 512])
        e3.close()
        norm(cv[:, 8:12, :], hT, cv[:, 8:12, :], 4, TT, 1.0 / GD, lambda k: V("o_norm"), heads=True,
             times=lambda k: mixT[:, k, :])
        e1.close()
        project([["evo0"], ["evo1"]], mixT, [8], None)

        def mlp(layer):
            norm(xT, hT, hT, KD, TT, 1.0 / D, lambda k: V(f"mlp{layer}", k, 1), presummed=True)
            with ExitStack() as m:
                hid = sb("hid2", [P, 32, T], m)
                up_done, relu_out = sem("up_done"), sem("relu_out")
                with nc.Block() as block:
                    @block.tensor
                    def _(pe):
                        for n in range(32):
                            if n % 4 == 0:
                                w = take(pe, f"up{layer}_{n // 4}").rearrange("p (k n) -> p k n", k=KD)
                            if n >= 8:
                                pe.wait_ge(relu_out, n - 7)
                            last = product(pe, bank(n % 8), lambda k: w[:, k, (n % 4) * P:(n % 4 + 1) * P],
                                           lambda k: hT[:, k, :], KD)
                            last.then_inc(up_done, 1)
                            if n % 4 == 3:
                                used(up_done, n + 1)

                    @block.scalar
                    def _(act):
                        for n in range(32):
                            act.wait_ge(up_done, n + 1)
                            act.activation(hid[:, n, :], bank(n % 8), ACT.Relu).then_inc(relu_out, 1)

                    @block.vector
                    def _(dve):
                        for n in range(32):
                            dve.wait_ge(relu_out, n + 1)
                            dve.tensor_tensor(hid[:, n, :], hid[:, n, :], hid[:, n, :], ALU.mult)

                    @block.sync
                    def _(sync):
                        feed(sync)
                project([[f"down{layer}_{h}_{k}" for k in range(4)] for h in range(2)], hid, [8] * 4, None)

        mlp(0)

        norm(xT, hT, hT, KD, TT, 1.0 / D, lambda k: V("mix1", k, 1), presummed=True)
        n1 = ExitStack()
        qr = sb("qr", [P, 8, T], n1)
        kr = sb("kr", [P, 4, T], n1)
        vtok = sb("vtok", [P, TT, 512], n1)
        gates = sb("gates", [P, TT, 48], n1)
        n2 = ExitStack()
        qT = sb("qTn", [P, 8, T], n2)
        kvc = sb("kvc", [P, 4, T], n2)
        t_done, t_out = sem("t_done"), sem("t_out")
        with nc.Block() as block:
            dests = [(qT[:, n, :], 0.125) for n in range(8)] + [(kvc[:, n, :], 1.0) for n in range(4)]
            dests += [(kr[:, n, :], 1.0) for n in range(4)] + [(vtok[:, n, :], 1.0) for n in range(4)]

            @block.tensor
            def _(pe):
                w = take(pe, "gl")[:, 0:8 * 48].rearrange("p (k n) -> p k n", k=KD)
                for i in range(TT):
                    last = product(pe, psum[:, i * 48:(i + 1) * 48], lambda k: hT[:, k, i * P:(i + 1) * P],
                                   lambda k: w[:, k, :], KD)
                last.then_inc(t_done, 1)
                used(t_done, 1)
                for n in range(20):
                    if n % 4 == 0:
                        w = take(pe, f"od{n // 4}").rearrange("p (k n) -> p k n", k=KD)
                    if n >= 7:
                        pe.wait_ge(t_out, n - 6)
                    if n < 16:
                        last = product(pe, bank(1 + n % 7), lambda k: w[:, k, (n % 4) * P:(n % 4 + 1) * P],
                                       lambda k: hT[:, k, :], KD)
                    else:
                        i = n - 16
                        last = product(pe, bank(1 + n % 7), lambda k: hT[:, k, i * P:(i + 1) * P],
                                       lambda k: w[:, k, :], KD)
                    last.then_inc(t_done, 1)
                    if n % 4 == 3:
                        used(t_done, n + 2)

            @block.scalar
            def _(act):
                act.wait_ge(t_done, 1)
                act.activation(gates[:, :, :].rearrange("p c n -> p (c n)"), psum[:, 0:192], ACT.Sigmoid)
                for n, (dst, scale) in enumerate(dests):
                    act.wait_ge(t_done, n + 2)
                    act.mul(dst, bank(1 + n % 7), scale).then_inc(t_out, 1)

            @block.sync
            def _(sync):
                feed(sync)

        r_done, r_out, stacked = sem("r_done"), sem("r_out"), sem("stacked")
        pairs_ = hT[:, :, :].rearrange("p (v g) n -> p v g n", v=2)
        with nc.Block() as block:
            @block.sync
            def _(sync):
                for kv in range(2):
                    for g in range(NG):
                        src = kvc[64 * (g % 2):64 * (g % 2) + 64, 2 * kv + g // 2, :]
                        sync.dma_start(pairs_[0:64, kv, g, :], src).then_inc(stacked, 16)
                        sync.dma_start(pairs_[64:P, kv, g, 0:T - 1], src[:, 1:T]).then_inc(stacked, 16)
                sync.wait_ge(stacked, 16 * 16)
                feed(sync)

            @block.tensor
            def _(pe):
                for n in range(12):
                    if n >= 8:
                        pe.wait_ge(r_out, n - 7)
                    pe.matmul(bank(n % 8), C("rot_nsa"), qT[:, n, :] if n < 8 else kr[:, n - 8, :],
                              start=True, stop=True).then_inc(r_done, 1)

            @block.vector
            def _(dve):
                link = chain(dve, "rope2_chain")
                for n in range(12):
                    src = qT[:, n, :] if n < 8 else kr[:, n - 8, :]
                    dst = qr[:, n, :] if n < 8 else kr[:, n - 8, :]
                    dve.wait_ge(r_done, n + 1)
                    link(dve.tensor_tensor(bank(n % 8), bank(n % 8), C("sin_nsa"), ALU.mult))
                    link(dve.tensor_tensor(dst, src, C("cos_nsa"), ALU.mult))
                    dve.tensor_tensor(dst, dst, bank(n % 8), ALU.add).then_inc(r_out, 1)

        n3 = ExitStack()
        hidc = sb("hidc", [P, 2, 2, NG * 31], n3).rearrange("p v m (g n) -> p v m g n", g=NG)
        posb = sb("posb", [P, 2, 2], n3)
        kcb = sb("kcb", [P, 62], n3)
        vcb = sb("vcb", [P, NG * ND], n3)
        h_done, b_out, hid_out, w2_done = sem("h_done"), sem("b_out"), sem("hid_out"), sem("w2_done")
        with nc.Block() as block:
            @block.tensor
            def _(pe):
                for kv in range(2):
                    w = take(pe, f"{'kv'[kv]}w1").rearrange("p (l n) -> p l n", l=16)
                    pe.wait_ge(stacked, 16 * 16)
                    for m in range(2):
                        b = 2 * (2 * kv + m)
                        if b >= 6:
                            pe.wait_ge(hid_out, 1)
                        for l in range(16):
                            lhs = w[:, l, m * P:(m + 1) * P]
                            rhs = pairs_[:, kv, :, 2 * l:2 * l + 30 * CMP_STRIDE + 1:CMP_STRIDE]
                            pe.matmul(psum[:, (b % 6) * 512:(b % 6) * 512 + 124].rearrange("p (a b) -> p a b", a=NG),
                                      lhs, rhs, start=(l == 0), stop=(l == 15))
                            last = pe.matmul(psum[:, (b % 6 + 1) * 512:(b % 6 + 1) * 512 + 1], lhs, V("pos", l, 1),
                                             start=(l == 0), stop=(l == 15))
                        last.then_inc(h_done, 1)
                    used(h_done, 2 * kv + 2)
                pe.wait_ge(hid_out, 4)
                w2 = take(pe, "cw2")[:, 0:256].rearrange("p (v m n) -> p v m n", v=2, m=2)
                for par in range(2):
                    product(pe, psum[64 * par:64 * par + 64, 6 * 512:6 * 512 + 62]
                            .rearrange("p (a b) -> p a b", a=2), lambda m: w2[:, 0, m, :],
                            lambda m: hidc[:, 0, m, :, :].rearrange("p (t q) n -> p q t n", q=2)[:, par], 2)
                for g in range(NG):
                    tile, par = g // 2, g % 2
                    for j in range(4):
                        last = product(pe, psum[32 * j:32 * j + 31, 7 * 512 + g * ND:7 * 512 + (g + 1) * ND],
                                       lambda m: hidc[:, 1, m, g, :],
                                       lambda m: w2[:, 1, m, :], 2)
                last.then_inc(w2_done, 1)
                used(w2_done, 1)

            @block.scalar
            def _(act):
                for n in range(4):
                    kv, m = n // 2, n % 2
                    b = (2 * n % 6) * 512
                    act.wait_ge(h_done, n + 1)
                    act.copy(posb[:, kv, m:m + 1], psum[:, b + 512:b + 513]).then_inc(b_out, 1)
                    act.wait_ge(b_out, n + 1)
                    act.activation(hidc[:, kv, m, :, :].rearrange("p g n -> p (g n)"), psum[:, b:b + 124],
                                   ACT.Silu, bias=posb[:, kv, m:m + 1], scale=1.0).then_inc(hid_out, 1)
                act.wait_ge(w2_done, 1)
                act.copy(kcb[:, :], psum[:, 6 * 512:6 * 512 + 62])
                for j in range(4):
                    rows = slice(32 * j, 32 * j + 31)
                    act.copy(vcb[rows, :], psum[rows, 7 * 512:7 * 512 + 256])

            @block.sync
            def _(sync):
                feed(sync)

        pc = sb("pc", [P, 2, NH, 32], n3)
        cst8 = sb("cst8", [P, TT, 4, NH], n3)
        n4 = ExitStack()
        pcT = hT[:, 0:4, :]
        cs_done, cs_sub, cs_exp, cs_prob, cs_turn, cs_out = (
            sem(n) for n in ("cs_done", "cs_sub", "cs_exp", "cs_prob", "cs_turn", "cs_out"))
        with nc.Block() as block:
            @block.tensor
            def _(pe):
                def cmp_scores(i):
                    for h in range(NH):
                        g, j = h // 4, h % 4
                        rows = slice(64 * (g % 2), 64 * (g % 2) + 64)
                        at = 512 * (i + 4 * (g % 2)) + (4 * (g // 2) + j) * 32
                        last = pe.matmul(psum[:, at:at + 31], qT[rows, 4 * (g // 2) + j, i * P:(i + 1) * P],
                                         kcb[rows, (g // 2) * 31:(g // 2) * 31 + 31], start=True, stop=True)
                    last.then_inc(cs_done, 1)
                for i in range(TT):
                    cmp_scores(i)
                for i in range(TT):
                    pe.wait_ge(cs_prob, i + 1)
                    for g in range(NG):
                        last = pe.transpose(bank(i)[:, g * P:(g + 1) * P],
                                            pc[:, i % 2, 4 * g:4 * g + 4, :].rearrange("p a b -> p (a b)"), ident)
                    last.then_inc(cs_turn, 1)

            @block.vector
            def _(dve):
                link = chain(dve, "cmp_chain")
                link(dve.memset(pc[:, :, :, :], 0.0))
                for i in range(TT):
                    e = pc[:, i % 2, :, 0:31]

                    def row(name, n=NH):
                        return C(name, 32 * i, 31).rearrange("p (o n) -> p o n", o=1).to_broadcast([P, n, 31])

                    def col(k):
                        return cst8[:, i, k, :].rearrange("p (h o) -> p h o", o=1)
                    dve.wait_ge(cs_done, i + 1)
                    if i >= 2:
                        dve.wait_ge(cs_turn, i - 1)
                    for g in range(NG):
                        s = bank(i + 4 * (g % 2))[:, 128 * (g // 2):128 * (g // 2) + P]
                        last = dve.tensor_tensor(e[:, 4 * g:4 * g + 4, :],
                                                 s.rearrange("p (h n) -> p h n", n=32)[:, :, 0:31],
                                                 row("cmp_neg", 4), ALU.add)
                    link(last)
                    link(dve.tensor_reduce(cst8[:, i, 0, :], e, AX.X, ALU.max))
                    dve.tensor_tensor(e, e, col(0).to_broadcast([P, NH, 31]), ALU.subtract).then_inc(cs_sub, 1)
                    dve.wait_ge(cs_exp, i + 1)
                    link(dve.tensor_tensor(e, e, row("cmp_ok"), ALU.mult))
                    link(dve.tensor_reduce(cst8[:, i, 1, :], e, AX.X, ALU.add))
                    link(dve.tensor_scalar(cst8[:, i, 2, :], cst8[:, i, 1, :], 0.0, None, ALU.is_equal))
                    link(dve.tensor_tensor(cst8[:, i, 1, :], cst8[:, i, 1, :], cst8[:, i, 2, :], ALU.add))
                    link(dve.reciprocal(cst8[:, i, 2, :], cst8[:, i, 1, :]))
                    link(dve.tensor_tensor(cst8[:, i, 3, :], cst8[:, i, 2, :], gates[:, i, 0:48:3], ALU.mult))
                    dve.tensor_tensor(e, e, col(3).to_broadcast([P, NH, 31]), ALU.mult).then_inc(cs_prob, 1)

            @block.scalar
            def _(act):
                for i in range(TT):
                    act.wait_ge(cs_sub, i + 1)
                    e = pc[:, i % 2, :, 0:31]
                    act.activation(e, e, ACT.Exp).then_inc(cs_exp, 1)
                for i in range(TT):
                    act.wait_ge(cs_turn, i + 1)
                    act.copy(pcT[:, :, i * P:(i + 1) * P], bank(i).rearrange("p (g n) -> p g n", g=NG))

        n2.close()
        n5 = ExitStack()
        pp = sb("pp", [P, 2, 2, T], n5)
        pT = [sb(f"pT{b}", [P, 2, TT, T], n5) for b in range(2)]
        st2 = sb("st2", [P, 64, 8], n5)
        heads_ = [(g, j) for g in range(NG) for j in range(4)]
        units = [(hd, i) for hd in range(NH) for i in range(TT)]
        NU2 = len(units)
        score_done, max_done, exp_done, prob_done = (sem(n) for n in ("score2", "max2", "exp2", "prob2"))
        turn_done, turn_a, turn_v, pv_done, pv_out = (sem(n) for n in ("turn2", "turn_a2", "turn_v2", "pv2", "pv_out2"))
        with nc.Block() as block:
            @block.tensor
            def _(pe):
                def scores(u):
                    hd, i = units[u]
                    g, j = heads_[hd]
                    rows = slice(64 * (g % 2), 64 * (g % 2) + 64)
                    if u >= 2:
                        pe.wait_ge(exp_done, u - 1)
                    for br in range(2):
                        last = pe.matmul(bank(2 * (u % 2) + br, (i + 1) * P), qr[rows, 4 * (g // 2) + j, i * P:(i + 1) * P],
                                         kr[rows, 2 * br + g // 2, 0:(i + 1) * P], start=True, stop=True)
                    last.then_inc(score_done, 1)

                def turn(u):
                    hd, i = units[u]
                    pe.wait_ge(prob_done, u + 1)
                    if u >= 1:
                        pe.wait_ge(turn_a, u)
                        pe.wait_ge(turn_v, u)
                    for br in range(2):
                        for k in range(i + 1):
                            last = pe.transpose(bank(4 + br)[:, k * P:(k + 1) * P], pp[:, u % 2, br, k * P:(k + 1) * P],
                                                ident)
                    last.then_inc(turn_done, 1)

                def values(hd):
                    g, j = heads_[hd]
                    rows = slice(64 * (g % 2), 64 * (g % 2) + 64)
                    pe.wait_ge(turn_a, 4 * hd + 4)
                    pe.wait_ge(turn_v, 4 * hd + 4)
                    if hd >= 2:
                        pe.wait_ge(pv_out, hd - 1)
                    b = (6 + hd % 2) * 512
                    for br in range(2):
                        for k in range(TT):
                            pe.matmul(psum[rows, b + k * P:b + 512], vtok[:, k, br * 256 + g * ND:br * 256 + (g + 1) * ND],
                                      pT[hd % 2][:, br, k, k * P:T], start=(br == 0 and k == 0), stop=False)
                    blk = slice(32 * j, 32 * j + 31)
                    pe.matmul(psum[rows, b:b + 512], vcb[blk, g * ND:(g + 1) * ND], pcT[blk, g, :], start=False,
                              stop=True).then_inc(pv_done, 1)

                scores(0)
                scores(1)
                for u in range(NU2):
                    if u + 2 < NU2:
                        scores(u + 2)
                    if u % 4 == 1 and u > 1:
                        values(u // 4 - 1)
                    turn(u)
                values(NH - 1)

            @block.vector
            def _(dve):
                link = chain(dve, "soft2_chain")

                def peak(u):
                    hd, i = units[u]
                    dve.wait_ge(score_done, u + 1)
                    s = psum[:, 2 * (u % 2) * 512:(2 * (u % 2) + 2) * 512].rearrange("p (b n) -> p b n", b=2)
                    diag = s[:, :, i * P:(i + 1) * P]
                    neg = C("causal_neg").rearrange("p (o n) -> p o n", o=1).to_broadcast([P, 2, P])
                    link(dve.tensor_tensor(diag, diag, neg, ALU.add))
                    dve.tensor_reduce(st2[:, u, 0:2], s[:, :, 0:(i + 1) * P], AX.X, ALU.max, negate=True)\
                       .then_inc(max_done, 1)

                peak(0)
                peak(1)
                for u in range(NU2):
                    hd, i = units[u]
                    g, j = heads_[hd]
                    h = 4 * g + j
                    dve.wait_ge(exp_done, u + 1)
                    link(dve.reciprocal(st2[:, u, 4:6], st2[:, u, 2:4]))
                    link(dve.tensor_tensor(st2[:, u, 6:8], st2[:, u, 4:6], gates[:, i, 3 * h + 1:3 * h + 3], ALU.mult))
                    w = (i + 1) * P
                    for br in range(2):
                        last = dve.tensor_scalar(pp[:, u % 2, br, 0:w], pp[:, u % 2, br, 0:w],
                                                 st2[:, u, 6 + br:7 + br], None, ALU.mult)
                    last.then_inc(prob_done, 1)
                    if u + 2 < NU2:
                        peak(u + 2)
                    dve.wait_ge(turn_done, u + 1)
                    dve.tensor_copy(pT[hd % 2][:, 1, 0:i + 1, i * P:(i + 1) * P],
                                    bank(5, w).rearrange("p (k n) -> p k n", n=P)).then_inc(turn_v, 1)

            @block.scalar
            def _(act):
                def exps(u):
                    hd, i = units[u]
                    act.wait_ge(max_done, u + 1)
                    if u >= 2:
                        act.wait_ge(turn_done, u - 1)
                    w = (i + 1) * P
                    for br in range(2):
                        last = act.activation(pp[:, u % 2, br, 0:w], bank(2 * (u % 2) + br, w), ACT.Exp,
                                              bias=st2[:, u, br:br + 1], scale=1.0, accum_out=st2[:, u, 2 + br:3 + br])
                    last.then_inc(exp_done, 1)

                def store(hd):
                    g, j = heads_[hd]
                    rows = slice(64 * (g % 2), 64 * (g % 2) + 64)
                    b = (6 + hd % 2) * 512
                    act.wait_ge(pv_done, hd + 1)
                    act.copy(mixT[rows, 4 * (g // 2) + j, :], psum[rows, b:b + 512]).then_inc(pv_out, 1)

                exps(0)
                for u in range(NU2):
                    hd, i = units[u]
                    if u + 1 < NU2:
                        exps(u + 1)
                    act.wait_ge(turn_done, u + 1)
                    act.copy(pT[hd % 2][:, 0, 0:i + 1, i * P:(i + 1) * P],
                             bank(4, (i + 1) * P).rearrange("p (k n) -> p k n", n=P)).then_inc(turn_a, 1)
                    if hd >= 1 and i == 1:
                        store(hd - 1)
                store(NH - 1)
        n5.close()
        n3.close()
        n1.close()
        project([["odo0"], ["odo1"]], mixT, [8], None)
        mlp(1)
        norm(xT, hT, xT, KD, TT, 1.0 / D, lambda k: V("final_norm", k, 1), presummed=True)
        stored = sem("stored")
        with nc.Block() as block:
            @block.sync
            def _(sync):
                sync.dma_start(out_d, xT[:, :, :]).then_inc(stored, 16)
                sync.wait_ge(stored, 16)
        assert cursor[0] == len(PLAN)


def chunk(w, cols, rows=None):
    w = w[:, cols] if rows is None else w[rows][:, cols]
    return w.reshape(-1, P, w.shape[1]).transpose(1, 0, 2).reshape(P, -1)


def span(a, n):
    return list(range(a, a + n))


def lay_out(inp):
    f = {k: np.asarray(v) for k, v in inp.items()}
    w_mod, w_in = f["w_mod"][0], f["w_in"][0]
    o_cq, o_ckv, o_kr, o_hq, o_hff, o_hfb, o_hi, o_hg, o_fn = 0, 256, 384, 448, 960, 1472, 1984, 2240, 2496
    parts = {}
    for i in range(12):
        parts[f"mod{i}"] = chunk(w_mod, slice(512 * i, 512 * i + 512))
    parts["hi_fn"] = chunk(w_in, span(o_hi, 256) + span(o_fn, 256))
    parts["mla_in"] = chunk(w_in, span(o_cq, 256) + span(o_ckv, 128) + span(o_kr, 64) * 2)
    parts["hg_gate"] = chunk(w_in, span(o_hg, 256))
    parts["hff"], parts["hfb"], parts["hq"] = (chunk(w_in, span(o, 512)) for o in (o_hff, o_hfb, o_hq))
    n = np.arange(T)
    ang = 2 * np.pi * ((np.outer(n, n)) % T) / T
    both = [(g(ang) / math.sqrt(T)).astype(np.float32).reshape(TT, P, T).transpose(1, 0, 2).reshape(P, -1)
            for g in (np.cos, np.sin)]
    parts["dft"] = np.concatenate(both, axis=1)
    parts["fourier"] = chunk(f["w_fourier"][0], slice(0, 256))
    qcols = [h * 192 + i for h in range(MH) for i in range(128)] + [h * 192 + 128 + i for h in range(MH) for i in range(64)]
    kcols = [h * 256 + i for h in range(MH) for i in range(128)] + [h * 256 + 128 + i for h in range(MH) for i in range(128)]
    parts["mla_up"] = np.concatenate([chunk(f["w_uq"][0], qcols), chunk(f["w_ukv"][0], kcols)], axis=1)
    for i in range(2):
        parts[f"out{i}"] = chunk(f["w_out"][0], slice(512 * i, 512 * i + 512))
    for i in range(11):
        parts[f"gu{i}"] = chunk(f["w_gate_up"][0], span(256 * i, 256) + span(FFN + 256 * i, 256))
    for h in range(2):
        for k in range(3):
            parts[f"dn{h}_{k}"] = chunk(f["w_down"][0], slice(512 * h, 512 * h + 512),
                                        slice(1024 * k, min(FFN, 1024 * k + 1024)))
    ev = f["ev_w_in_2"][0]
    parts["ev_ab"] = chunk(ev, span(2048, 16))
    order = span(0, 2048) + span(2064 + 512, 512) + span(2064 + 1024, 512) + span(2064, 512)
    for i in range(7):
        parts[f"ev{i}"] = chunk(ev, order[512 * i:512 * i + 512])
    for i in range(2):
        parts[f"evo{i}"] = chunk(f["ev_w_out_2"][0], slice(512 * i, 512 * i + 512))
    for l in range(2):
        for i in range(8):
            parts[f"up{l}_{i}"] = chunk(f["w_up_2"][l], slice(512 * i, 512 * i + 512))
        for h in range(2):
            for k in range(4):
                parts[f"down{l}_{h}_{k}"] = chunk(f["w_down_2"][l], slice(512 * h, 512 * h + 512),
                                                  slice(1024 * k, 1024 * k + 1024))
    od = f["od_w_in_2"][0]
    slots = [(2 * (i // 4) + p) * 4 + i % 4 for i in range(8) for p in range(2)]
    qcols = [h * 64 + i for h in slots for i in range(64)]
    kc, vc, ks, vs, kw, vw, gl = (1024 + 256 * i for i in range(7))
    cols = qcols + span(kc, 256) + span(vc, 256) + span(ks, 256) + span(kw, 256) + span(vs, 256) + span(vw, 256)
    parts["gl"] = chunk(od, span(gl, 48))
    for i in range(5):
        parts[f"od{i}"] = chunk(od, cols[512 * i:512 * i + 512])
    for n_, key in (("k", "od_cmp_k_w1_2"), ("v", "od_cmp_v_w1_2")):
        parts[f"{n_}w1"] = chunk(f[key][0], slice(0, 256))
    parts["cw2"] = np.concatenate([chunk(f[k][0], slice(0, 64)) for k in ("od_cmp_k_w2_2", "od_cmp_v_w2_2")], axis=1)
    for i in range(2):
        parts[f"odo{i}"] = chunk(f["od_w_out_2"][0][qcols], slice(512 * i, 512 * i + 512))
    for name, w in PLAN:
        assert parts[name].shape == (P, w), (name, parts[name].shape, w)
    weights = np.concatenate([parts[name].reshape(-1) for name, _ in PLAN])

    def col(v):
        return v.reshape(-1, P).T

    v = {}
    v["c2"] = np.stack([col(f["c"][0]), col(f["c_ctx"])], axis=2).reshape(P, -1)
    v["b_mod"] = col(f["b_mod"][0])
    for name in ("norm1_g", "norm2_g", "q_norm_g", "kv_norm_g", "hg_norm_g"):
        v[name] = col(f[name][0])
    v["lb_param"] = col(f["lb_param"][0].reshape(-1))
    v["final_norm_g"], v["final_norm"] = col(f["final_norm_g"]), col(f["final_norm_2"])
    for l in range(2):
        v[f"mix{l}"], v[f"mlp{l}"] = col(f["mix_norm_2"][l]), col(f["mlp_norm_2"][l])
    v["conv"] = f["ev_qkv_conv_2"][0].T.reshape(12, P, 4).transpose(1, 0, 2).reshape(P, -1)
    v["o_norm"] = np.concatenate([f["ev_o_norm_2"][0]] * 2).reshape(P, 1)
    v["sc_conv"] = f["ev_sc_conv_2"][0].T.reshape(4, P, 3).transpose(1, 0, 2).reshape(P, -1)
    v["pos"] = col(f["od_cmp_pos_2"][0].reshape(-1))
    v["a_log"] = np.broadcast_to(f["ev_a_log_2"][0][None, :], (P, GH))
    v["dt_bias"] = np.broadcast_to(f["ev_dt_bias_2"][0][None, :], (P, GH))
    vecs = np.concatenate([v[name] for name, _ in VECS], axis=1)
    assert vecs.shape == (P, NVEC)
    xt = f["x"][0].T.reshape(KD, P, T).transpose(1, 0, 2)
    ct = f["ctx"][0].T.reshape(KD, P, TC).transpose(1, 0, 2)
    consts = np.concatenate(list(CONSTS.values()), axis=1)
    return [weights, consts, vecs, xt, ct]


INPUTS = [("weights", (NWEIGHT,)), ("consts", (P, NCONST)), ("vecs", (P, NVEC)), ("xin", (P, KD, T)),
          ("ctxin", (P, KD, TC))]


def kernel(**inputs):
    import concourse.bacc as bacc
    from concourse.bass_utils import run_bass_kernel_spmd
    arrays = lay_out(inputs)
    nc = bacc.Bacc("TRN2", target_bir_lowering=False, num_devices=1)
    aps = [nc.dram_tensor(n, s, F32, kind="ExternalInput").ap() for n, s in INPUTS]
    out = nc.dram_tensor("out", (P, KD, T), F32, kind="ExternalOutput").ap()
    program(nc, *aps, out)
    r = run_bass_kernel_spmd(nc, [{n: np.ascontiguousarray(a) for (n, _), a in zip(INPUTS, arrays)}], core_ids=[0])
    return r.results[0]["out"].transpose(1, 0, 2).reshape(D, T).T.reshape(1, T, D)
```

```python
import math
from contextlib import ExitStack

import numpy as np

import concourse.bass as bass
from concourse import mybir

F32 = mybir.dt.float32
F32R = mybir.dt.float32r
U32 = mybir.dt.uint32
ALU = mybir.AluOpType
ACT = mybir.ActivationFunctionType
AX = mybir.AxisListType

P = 128
D = 1024
KD = D // P
T = 512
TT = T // P
TC = 256
TCT = TC // P
TA = T + TC
TAT = TT + TCT
EPS = 1e-6
GRID_W = 64
QL, KVL, NOPE, ROPE, VH, MH = 256, 128, 128, 64, 128, 4
HH, HK, HV = 4, 128, 64
FFN = 2816
FT = FFN // P
MLA_SCALE = 1.0 / math.sqrt(NOPE + ROPE)
GH, GD = 8, 64
DFF = 4096
NH, ND, NG = 16, 64, 4
NB_CMP = 31
CMP_STRIDE, CMP_BLOCK, CMP_HID = 16, 32, 256
NSA_ROPE = 16
LEVELS = 7
SLOT = 4096
RING = 3
NEG = -1.0e30


def level_mask(lev, later_free):
    half = 1 << lev
    a = np.arange(P)
    blk, sec = a // (2 * half), (a // half) % 2
    m = (blk[:, None] == blk[None, :]) & (sec[:, None] == 0) & (sec[None, :] == 1)
    return (m if later_free else m.T).astype(np.float32)


def rotation(dim, total):
    r = np.zeros((total, total), np.float32)
    for lo in dim:
        n = dim[lo]
        for i in range(n // 2):
            r[lo + n // 2 + i, lo + i] = -1.0
            r[lo + i, lo + n // 2 + i] = 1.0
    return r


def twice(a):
    z = np.zeros_like(a)
    return np.block([[a, z], [z, a]])


def constants():
    out = {}
    a = np.arange(P)
    out["ident"] = np.eye(P, dtype=np.float32)
    out["ones"] = np.ones((P, P), np.float32)
    out["blk64"] = twice(np.ones((64, 64), np.float32))
    out["rot_mla"] = twice(rotation({0: 32, 32: 32}, 64))
    out["rot_nsa"] = twice(rotation({0: NSA_ROPE}, 64))
    ang = 2 * np.pi * np.outer(np.arange(64), np.arange(64)) / 64
    out["dft_cos64"] = twice((np.cos(ang) / 8).astype(np.float32))
    out["dft_nsin64"] = twice((-np.sin(ang) / 8).astype(np.float32))
    out["upto"] = (a[:, None] <= a[None, :]).astype(np.float32)
    out["causal_neg"] = np.where(a[None, :] <= a[:, None], 0.0, NEG).astype(np.float32)
    for lev in range(LEVELS):
        out[f"first_second{lev}"] = level_mask(lev, True)
    for lev in range(LEVELS):
        out[f"second_first{lev}"] = level_mask(lev, False)
    f32 = np.float32
    rows = np.repeat(np.arange(T // GRID_W, dtype=f32), GRID_W)
    cols = np.tile(np.arange(GRID_W, dtype=f32), T // GRID_W)
    inv = (f32(10000.0) ** (-np.arange(0, 32, 2, dtype=f32) / f32(32))).astype(f32)
    ar, ac = rows[:, None] * inv, cols[:, None] * inv
    ang = np.concatenate([ar, ar, ac, ac], axis=-1).T
    out["cos_mla"] = np.tile(np.cos(ang), (2, 1)).astype(f32)
    out["sin_mla"] = np.tile(np.sin(ang), (2, 1)).astype(f32)
    inv = (f32(500000.0) ** (-np.arange(0, NSA_ROPE, 2, dtype=f32) / f32(NSA_ROPE))).astype(f32)
    ang = (np.arange(T, dtype=f32)[:, None] * inv[None, :]).T
    c = np.ones((64, T), f32)
    s = np.zeros((64, T), f32)
    c[0:8], c[8:16], s[0:8], s[8:16] = np.cos(ang), np.cos(ang), np.sin(ang), np.sin(ang)
    out["cos_nsa"] = np.tile(c, (2, 1))
    out["sin_nsa"] = np.tile(s, (2, 1))
    t = (np.arange(TT)[None, :, None] * P + a[:, None, None])
    end = np.arange(32)[None, None, :] * CMP_STRIDE + CMP_BLOCK - 1
    ok = (end <= t) & (np.arange(32)[None, None, :] < NB_CMP)
    out["cmp_neg"] = np.where(ok, 0.0, NEG).astype(f32).reshape(P, TT * 32)
    out["cmp_ok"] = ok.astype(f32).reshape(P, TT * 32)
    out["eighth"] = np.full((P, 1), 0.125, f32)
    out["one"] = np.ones((P, 1), f32)
    return out


CONSTS = constants()
CONST_AT = {}
_n = 0
for _name, _a in CONSTS.items():
    CONST_AT[_name] = (_n, _a.shape[1])
    _n += _a.shape[1]
NCONST = _n

VECS = [("c2", 2 * KD), ("b_mod", 48), ("norm1_g", KD), ("norm2_g", KD), ("q_norm_g", 2), ("kv_norm_g", 1),
        ("lb_param", 2 * HH), ("hg_norm_g", 2), ("final_norm_g", KD), ("mix0", KD), ("mix1", KD), ("mlp0", KD),
        ("mlp1", KD), ("final_norm", KD), ("conv", 12 * 4), ("o_norm", 1), ("sc_conv", 4 * 3), ("pos", 16),
        ("a_log", GH), ("dt_bias", GH)]
VEC_AT = {}
_n = 0
for _name, _w in VECS:
    VEC_AT[_name] = (_n, _w)
    _n += _w
NVEC = _n


FFN1_UP, FFN1_DOWN = (6, 5), ((8, 4), (8, 2))
MLP_UP, MLP_DOWN = (4, 4), ((8, 8), (8, 8))


def ffn_plan(up, ups, down, downs):
    out, c = [], 0
    for part in range(2):
        out += [(f"{up}{c + i}", SLOT) for i in range(ups[part])]
        c += ups[part]
        out += [(f"{down}{part}_{h}_{i}", kt * 512) for h in range(2) for i, kt in enumerate(downs[part])]
    return out


def plan():
    out = [(f"mod{i}", SLOT) for i in range(4)]
    out += [("hi_fn", SLOT), ("mla_in", SLOT), ("hg_gate", 8 * 256), ("dft", SLOT), ("fourier", 2 * 256),
            ("mla_up", 2 * 768 + 1024), ("hff", SLOT), ("hfb", SLOT), ("hq", SLOT)]
    out += [(f"mod{i}", SLOT) for i in range(4, 12)]
    out += [(f"out{i}", SLOT) for i in range(2)]
    out += ffn_plan("gu", FFN1_UP, "dn", FFN1_DOWN)
    out += [("ev_ab", 8 * 16)] + [(f"ev{i}", SLOT) for i in range(7)]
    out += [(f"evo{i}", SLOT) for i in range(2)]
    out += ffn_plan("up0_", MLP_UP, "down0_", MLP_DOWN)
    out += [("gl", 8 * 48)] + [(f"od{i}", SLOT) for i in range(5)]
    out += [("kw1", SLOT), ("vw1", SLOT), ("cw2", 256)]
    out += [(f"odo{i}", SLOT) for i in range(2)]
    out += ffn_plan("up1_", MLP_UP, "down1_", MLP_DOWN)
    return out


PLAN = plan()
PLAN_AT = []
_n = 0
for _name, _w in PLAN:
    PLAN_AT.append(_n)
    _n += _w * P
NWEIGHT = _n


def program(nc, weights, consts_d, vecs_d, x_d, ctx_d, out_d):
    ctx = ExitStack()
    with ctx:
        nsem = [0]

        def sem(name):
            nsem[0] += 1
            return ctx.enter_context(nc.semaphore(f"{name}_{nsem[0]}"))

        def sb(name, shape, stack=None):
            if stack is None:
                return ctx.enter_context(nc.sbuf_tensor(name, shape, F32))
            n = int(np.prod(shape[1:]))
            n += n % 2
            fits = [(part, a) for part in arena for a in sorted([part[1]] + [b for _, b in held])
                    if part[1] <= a and a + n <= part[2] and all(b <= a or a + n <= a0 for a0, b in held)]
            assert fits, (name, n, held)
            part, at = fits[0]
            held.append((at, at + n))
            stack.callback(held.remove, (at, at + n))
            axes = "abcd"[:len(shape) - 1]
            flat = part[0][:, at - part[1]:at - part[1] + int(np.prod(shape[1:]))]
            if len(axes) == 1:
                return flat
            return flat.rearrange(f"p ({' '.join(axes)}) -> p {' '.join(axes)}", **dict(zip(axes, shape[1:])))

        psum = ctx.enter_context(nc.psum_tensor("psum", [P, 4096], F32))

        def bank(b, n=512):
            return psum[:, b * 512:b * 512 + n]

        xT = sb("xT", [P, KD, T])
        cst = sb("cst", [P, NCONST])
        vec = sb("vec", [P, NVEC])
        ring = sb("ring", [P, RING, SLOT])
        sums = sb("sums", [P, 64])
        rstd = sb("rstd", [P, 64])
        mod = sb("mod", [P, 48, 2])
        gmod = sb("gmod", [P, 3 * KD])
        epsc = sb("epsc", [P, 1])
        ARENA = 22760
        held = []

        arena = []
        PARTS = 2 * KD * T + 4 * 1024
        upper = [ExitStack()]
        LOW = ARENA - PARTS

        def mixer_memory(n, low):
            phase = ExitStack()
            hT, mixT = (phase.enter_context(nc.sbuf_tensor(f"{name}{n}", [P, KD, T], F32)) for name in ("hT", "mixT"))
            if low:
                arena.append((phase.enter_context(nc.sbuf_tensor(f"arena_low{n}", [P, low], F32)), 0, low))
            phase.callback(arena.clear)
            return phase, hT, mixT

        def open_upper(n, low):
            upper[0] = ExitStack()
            arena.append((upper[0].enter_context(nc.sbuf_tensor(f"arena{n}", [P, ARENA - low], F32)), low, ARENA))

        def close_upper():
            part = arena.pop()
            assert all(b <= part[1] for _, b in held), held
            upper[0].close()

        def split_space(n):
            mem = ExitStack()
            return (mem, mem.enter_context(nc.sbuf_tensor(f"hs{n}", [P, 2, KD, T], F32R)),
                    mem.enter_context(nc.sbuf_tensor(f"wsp{n}", [P, 2, 2, 1024], F32R)))

        phase, hT, mixT = mixer_memory(0, 0)
        open_upper(0, 0)

        def C(name, lo=0, n=None):
            at, w = CONST_AT[name]
            return cst[:, at + lo:at + (w if n is None else lo + n)]

        def V(name, lo=0, n=None):
            at, w = VEC_AT[name]
            return vec[:, at + lo:at + (w if n is None else lo + n)]

        ident = C("ident")

        weight_landed = [sem(f"weight_landed{i}") for i in range(RING)]
        weight_used = sem("weight_used")
        cursor = [0]
        issued = [0]
        read_at = []
        plain = [0]

        def feed(sync):
            while issued[0] < min(len(PLAN), cursor[0] + RING):
                i = issued[0]
                w = PLAN[i][1]
                if i >= RING:
                    sync.wait_ge(*read_at[i - RING])
                src = weights[PLAN_AT[i]:PLAN_AT[i] + P * w].rearrange("(p n) -> p n", p=P)
                sync.dma_start(ring[:, i % RING, 0:w], src).then_inc(weight_landed[i % RING], 16)
                issued[0] += 1

        def take(pe, name):
            i = cursor[0]
            assert PLAN[i][0] == name, (PLAN[i], name)
            cursor[0] += 1
            pe.wait_ge(weight_landed[i % RING], 16 * (i // RING + 1))
            return ring[:, i % RING, :]

        def claim(name):
            i = cursor[0]
            assert PLAN[i][0] == name, (PLAN[i], name)
            cursor[0] += 1
            return i

        def used(signal, value):
            read_at.append((signal, value))

        def used_after(last):
            plain[0] += 1
            last.then_inc(weight_used, 1)
            read_at.append((weight_used, plain[0]))

        def chain(eng, name, make=None):
            s, n = (make or sem)(name), [0]

            def link(ins):
                n[0] += 1
                ins.then_inc(s, 1)
                eng.wait_ge(s, n[0])
            return link

        def product(pe, out, lhs, rhs, n):
            for k in range(n):
                last = pe.matmul(out, lhs(k), rhs(k), start=(k == 0), stop=(k == n - 1))
            return last

        f_names = ("w_hi", "w_lo", "unit_done", "act_a", "act_b", "act_hi", "act_lo", "res_set", "sq2_set", "sq2_read",
                   "nrm_root", "nrm_inv", "nrm_h", "nrm_s", "nrm_hi", "nrm_lo")
        f_sems = {n: sem(n) for n in f_names}
        f_at = dict.fromkeys(f_names, 0)

        def split_products(names, src, hs, wsp, tokens=()):
            s, b0 = f_sems, dict(f_at)
            NU = 4 * len(names)
            raw = []
            for g, name in enumerate(names):
                raw.append(claim(name))
                used(s["w_lo"], b0["w_lo"] + 4 * g + 4)

            def weights_of(q):
                return ring[:, raw[q // 4] % RING, (q % 4) * 1024:(q % 4 + 1) * 1024]

            def high(act, q):
                if q >= NU:
                    return
                if q < 4:
                    for k in (2 * q, 2 * q + 1):
                        act.copy(hs[:, 0, k, :], src[:, k, :]).then_inc(s["nrm_hi"], 1)
                i = raw[q // 4]
                act.wait_ge(weight_landed[i % RING], 16 * (i // RING + 1))
                if q >= 2:
                    act.wait_ge(s["unit_done"], b0["unit_done"] + q - 1)
                act.copy(wsp[:, q % 2, 0, :], weights_of(q)).then_inc(s["w_hi"], 1)

            def low(dve, q):
                if q >= NU:
                    return
                if q < 4:
                    for k in (2 * q, 2 * q + 1):
                        dve.wait_ge(s["nrm_hi"], b0["nrm_hi"] + k + 1)
                        dve.tensor_tensor(hs[:, 1, k, :], src[:, k, :], hs[:, 0, k, :].bitcast(F32), ALU.subtract)\
                           .then_inc(s["nrm_lo"], 1)
                dve.wait_ge(s["w_hi"], b0["w_hi"] + q + 1)
                dve.tensor_tensor(wsp[:, q % 2, 1, :], weights_of(q), wsp[:, q % 2, 0, :].bitcast(F32),
                                  ALU.subtract).then_inc(s["w_lo"], 1)

            def unit(pe, q):
                g, u = q // 4, q % 4
                pe.wait_ge(s["w_lo"], b0["w_lo"] + q + 1)
                if q < 4:
                    pe.wait_ge(s["nrm_lo"], b0["nrm_lo"] + 2 * q + 2)
                for j in range(4):
                    out = bank(4 * (g % 2) + j)
                    for i in range(2):
                        for a, b in ((0, 0), (0, 1), (1, 0)):
                            ends = dict(start=(u == 0 and i == 0 and a == 0 and b == 0),
                                        stop=(u == 3 and i == 1 and a == 1))
                            if g in tokens:
                                last = pe.matmul(out, hs[:, b, 2 * u + i, j * P:(j + 1) * P],
                                                 wsp[:, q % 2, a, i * 512:(i + 1) * 512], **ends)
                            else:
                                last = pe.matmul(out, wsp[:, q % 2, a, i * 512 + j * P:i * 512 + (j + 1) * P],
                                                 hs[:, b, 2 * u + i, :], **ends)
                last.then_inc(s["unit_done"], 1)

            def group_done(eng, g):
                eng.wait_ge(s["unit_done"], b0["unit_done"] + 4 * g + 4)

            for name, n in (("w_hi", NU), ("w_lo", NU), ("unit_done", NU), ("nrm_hi", KD), ("nrm_lo", KD)):
                f_at[name] += n
            return high, low, unit, group_done

        vec_loaded, loaded = sem("vec_loaded"), sem("loaded")
        early = ExitStack()
        ctxT = mixT[:, 0:4, :].rearrange("p a (b n) -> p (a b) n", b=2)
        hcT = sb("hcT", [P, KD, TC], early)
        csil = sb("csil", [P, KD, 2], early)
        bm = V("b_mod")
        eps_set = sem("eps_set")
        with nc.Block() as block:
            @block.sync
            def _(sync):
                feed(sync)

            @block.vector
            def _(dve):
                dve.memset(epsc[:, :], EPS).then_inc(eps_set, 1)
                dve.wait_ge(eps_set, 1)

            @block.scalar
            def _(act):
                act.dma_start(vec[:, :], vecs_d).then_inc(vec_loaded, 16)
                act.dma_start(xT[:, :, :], x_d).then_inc(loaded, 16)
                act.dma_start(mixT[:, 0:4, :], ctx_d.rearrange("p (a b) n -> p a (b n)", b=2)).then_inc(loaded, 16)
                act.dma_start(cst[:, :], consts_d).then_inc(loaded, 16)
                act.wait_ge(vec_loaded, 16)

        silu_done, mod_rows, mod_copied, mod_done, biased = (
            sem(n) for n in ("silu_done", "mod_rows", "mod_copied", "mod_done", "biased"))
        MODB = 7 * 512
        mod_row = hcT[0:2, 6:8, :].rearrange("p a b -> p (a b)")

        def mod_step(pe, view, ch, k):
            if k == 0 and ch >= 1:
                pe.wait_ge(mod_copied, ch)
            last = pe.matmul(psum[0:2, 6 * 512:7 * 512], csil[:, k, :], view[:, k, :], start=(k == 0),
                             stop=(k == KD - 1))
            if k == KD - 1:
                last.then_inc(mod_rows, 1)
                used(mod_rows, ch + 1)

        def mod_copy(act, ch):
            act.wait_ge(mod_rows, ch + 1)
            if ch >= 1:
                act.wait_ge(mod_done, ch)
            act.copy(mod_row, psum[0:2, 6 * 512:7 * 512]).then_inc(mod_copied, 1)

        def mod_turn(pe, ch):
            pe.wait_ge(mod_copied, ch + 1)
            for j in range(4):
                at = MODB + 2 * (4 * ch + j)
                last = pe.transpose(psum[:, at:at + 2], mod_row[:, j * P:(j + 1) * P], ident[0:2, 0:2])
            last.then_inc(mod_done, 1)

        def mod_finish(dve, a, b):
            dve.wait_ge(mod_done, b // 4)
            bias = bm[:, a:b].rearrange("p (n o) -> p n o", o=1).to_broadcast([P, b - a, 2])
            dve.tensor_tensor(mod[:, a:b, :], psum[:, MODB + 2 * a:MODB + 2 * b].rearrange("p (n o) -> p n o", o=2),
                              bias, ALU.add).then_inc(biased, 1)
            dve.wait_ge(biased, 1 if a == 0 else 2)
            for at, norm_g, j, who in ((0, "norm1_g", 1, 0), (1, "norm1_g", 1, 1)) if a == 0 else ((2, "norm2_g", 4, 0),):
                dve.scalar_tensor_tensor(out=gmod[:, at * KD:(at + 1) * KD], in0=mod[:, j * KD:(j + 1) * KD, who],
                                         scalar=1.0, in1=V(norm_g), op0=ALU.add, op1=ALU.mult)

        with nc.Block() as block:
            @block.scalar
            def _(act):
                act.activation(csil[:, :, :].rearrange("p k n -> p (k n)"), V("c2"), ACT.Silu).then_inc(silu_done, 1)
                for ch in range(4):
                    mod_copy(act, ch)
                act.wait_ge(loaded, 48)

            @block.tensor
            def _(pe):
                pe.wait_ge(silu_done, 1)
                for ch in range(4):
                    view = take(pe, f"mod{ch}").rearrange("p (k n) -> p k n", k=KD)
                    for k in range(KD):
                        mod_step(pe, view, ch, k)
                    if ch == 0:
                        pe.wait_ge(loaded, 48)
                    mod_turn(pe, ch)

            @block.vector
            def _(dve):
                mod_finish(dve, 0, 16)

            @block.sync
            def _(sync):
                feed(sync)

        norm_names = ("squares", "summed", "rooted", "inverted", "spread", "scaled", "row_free")
        norm_sems = [sem(n) for n in norm_names]
        norm_at = dict.fromkeys(norm_names, 0)

        def norm(src, sq, dst, kt, tiles, scale, gain, shift=None, heads=False, times=None,
                 presummed=False):
            base = dict(norm_at)
            first = 0 if presummed else 1
            for name, n in (("squares", first * kt), ("summed", first), ("rooted", 1), ("inverted", 1),
                            ("spread", kt if heads else 0), ("scaled", kt), ("row_free", max(0, kt - 6) if heads else 0)):
                norm_at[name] += n
            squares, summed, rooted, inverted, spread, scaled, row_free = norm_sems
            if not heads:
                norm_all(src, sq, dst, kt, tiles, scale, gain, shift, base, presummed)
                return
            ncol = 2 * kt * tiles

            def row_bank(r):
                return 1 + r % 6

            with nc.Block() as block:
                @block.scalar
                def _(act):
                    for k in range(kt):
                        act.activation(sq[:, k, :], src[:, k, :], ACT.Square).then_inc(squares, 1)
                    act.wait_ge(summed, base["summed"] + 1)
                    act.activation(sums[:, 0:ncol], psum[:, 0:ncol], ACT.Sqrt, bias=epsc[:, 0:1], scale=scale)\
                       .then_inc(rooted, 1)

                @block.tensor
                def _(pe):
                    for k in range(kt):
                        pe.wait_ge(squares, base["squares"] + k + 1)
                        for i in range(TT):
                            at = 2 * (k * TT + i)
                            last = pe.matmul(psum[:, at:at + 2], sq[:, k, i * P:(i + 1) * P],
                                             C("blk64")[:, 0:P:64], start=True, stop=True)
                    last.then_inc(summed, 1)
                    pe.wait_ge(inverted, base["inverted"] + 1)
                    for r in range(kt):
                        if r >= 6:
                            pe.wait_ge(row_free, base["row_free"] + r - 5)
                        for i in range(TT):
                            b = row_bank(r) * 512 + i * P
                            at = 2 * (r * TT + i)
                            for o in range(2):
                                last = pe.matmul(psum[64 * o:64 * o + 64, b:b + P],
                                                 rstd[:, at + o:at + o + 1].to_broadcast([P, 64]), ident,
                                                 start=True, stop=True)
                        last.then_inc(spread, 1)

                @block.vector
                def _(dve):
                    dve.wait_ge(rooted, base["rooted"] + 1)
                    dve.reciprocal(rstd[:, 0:ncol], sums[:, 0:ncol]).then_inc(inverted, 1)
                    for k in range(kt):
                        dve.wait_ge(spread, base["spread"] + k + 1)
                        dve.scalar_tensor_tensor(out=dst[:, k, :], in0=src[:, k, :], scalar=gain(k),
                                                 in1=bank(row_bank(k)), op0=ALU.mult, op1=ALU.mult).then_inc(scaled, 1)
                        if k < kt - 6:
                            dve.wait_ge(scaled, base["scaled"] + k + 1)
                            dve.sem_inc(row_free, 1)
                        if times is not None:
                            dve.wait_ge(scaled, base["scaled"] + k + 1)
                            dve.tensor_tensor(times(k), dst[:, k, :], times(k), ALU.mult)

                @block.sync
                def _(sync):
                    feed(sync)

        sum_bank = [0]

        def norm_all(src, sq, dst, kt, tiles, scale, gain, shift, base, presummed):
            squares, summed, rooted, inverted, spread, scaled, row_free = norm_sems
            parts = [(a, min(4, tiles - a) * P) for a in range(0, tiles, 4)]
            width = tiles * P
            s0 = 512 * sum_bank[0] if presummed else 0
            with nc.Block() as block:
                @block.scalar
                def _(act):
                    if not presummed:
                        for k in range(kt):
                            act.activation(sq[:, k, 0:width], src[:, k, 0:width], ACT.Square).then_inc(squares, 1)
                        act.wait_ge(summed, base["summed"] + 1)
                    act.activation(psum[:, s0:s0 + width], psum[:, s0:s0 + width], ACT.Sqrt, bias=epsc[:, 0:1], scale=scale)\
                       .then_inc(rooted, 1)
                    if shift is not None:
                        for k in range(kt):
                            act.wait_ge(scaled, base["scaled"] + k + 1)
                            act.activation(dst[:, k, 0:width], dst[:, k, 0:width], ACT.Identity, bias=shift(k),
                                           scale=1.0)

                @block.tensor
                def _(pe):
                    if presummed:
                        return
                    for k in range(kt):
                        pe.wait_ge(squares, base["squares"] + k + 1)
                        for a, n in parts:
                            last = pe.matmul(bank(a // 4, n), C("ones"), sq[:, k, a * P:a * P + n], start=(k == 0),
                                             stop=(k == kt - 1))
                    last.then_inc(summed, 1)

                @block.vector
                def _(dve):
                    dve.wait_ge(rooted, base["rooted"] + 1)
                    dve.reciprocal(psum[:, 1024:1024 + width], psum[:, s0:s0 + width]).then_inc(inverted, 1)
                    dve.wait_ge(inverted, base["inverted"] + 1)
                    for k in range(kt):
                        dve.scalar_tensor_tensor(out=dst[:, k, 0:width], in0=src[:, k, 0:width], scalar=gain(k),
                                                 in1=psum[:, 1024:1024 + width], op0=ALU.mult, op1=ALU.mult)\
                           .then_inc(scaled, 1)

                @block.sync
                def _(sync):
                    feed(sync)

        norm(xT, hT, hT, KD, TT, 1.0 / D, lambda k: gmod[:, k:k + 1], shift=lambda k: mod[:, k, 0:1])
        norm(ctxT, hcT, hcT, KD, TCT, 1.0 / D, lambda k: gmod[:, KD + k:KD + k + 1], shift=lambda k: mod[:, k, 1:2])

        s1 = ExitStack()
        v_hg = sb("v_hg", [P, TAT, HH * HV], early)
        s2 = ExitStack()
        fn_tok = sb("fn_tok", [P, TT, 256], s2)
        cqT = sb("cqT", [P, 2, T], s1)
        ckvT = sb("ckvT", [P, 1, TA], s1)
        kpe_raw = sb("kpe_raw", [P, TA], s1)
        tile_done, tile_out = sem("tile_done"), sem("tile_out")
        with nc.Block() as block:
            @block.tensor
            def _(pe):
                w = take(pe, "hi_fn").rearrange("p (k n) -> p k n", k=KD)
                for i in range(TT):
                    last = product(pe, bank(i), lambda k: hT[:, k, i * P:(i + 1) * P], lambda k: w[:, k, :], KD)
                    last.then_inc(tile_done, 1)
                for i in range(TCT):
                    last = product(pe, bank(4 + i, 256), lambda k: hcT[:, k, i * P:(i + 1) * P],
                                   lambda k: w[:, k, 0:256], KD)
                    last.then_inc(tile_done, 1)
                used(tile_done, 6)
                w = take(pe, "mla_in").rearrange("p (k n) -> p k n", k=KD)
                for j in range(4):
                    if j >= 2:
                        pe.wait_ge(tile_out, j - 1)
                    last = product(pe, bank((6 + j) % 8), lambda k: w[:, k, j * P:(j + 1) * P],
                                   lambda k: hT[:, k, :], KD)
                    last.then_inc(tile_done, 1)
                for j in (2, 3):
                    pe.wait_ge(tile_out, j + 1)
                    last = product(pe, bank(j, TC), lambda k: w[:, k, j * P:(j + 1) * P],
                                   lambda k: hcT[:, k, :], KD)
                    last.then_inc(tile_done, 1)
                used(tile_done, 12)
                w = take(pe, "hg_gate")[:, 0:8 * 256].rearrange("p (k n) -> p k n", k=KD)
                for j in range(2):
                    pe.wait_ge(tile_out, 5 + j)
                    last = product(pe, bank(4 + j), lambda k: w[:, k, j * P:(j + 1) * P], lambda k: hT[:, k, :], KD)
                    last.then_inc(tile_done, 1)
                used(tile_done, 14)

            @block.scalar
            def _(act):
                n = 0
                for i in range(TAT):
                    n += 1
                    act.wait_ge(tile_done, n)
                    if i < TT:
                        act.copy(fn_tok[:, i, :], bank(i)[:, 256:512])
                    act.copy(v_hg[:, i, :], bank(i, 256)).then_inc(tile_out, 1)
                for b, dst in ((6, cqT[:, 0, :]), (7, cqT[:, 1, :]), (0, ckvT[:, 0, 0:T]), (1, kpe_raw[:, 0:T])):
                    n += 1
                    act.wait_ge(tile_done, n)
                    act.copy(dst, bank(b)).then_inc(tile_out, 1)
                for b, dst in ((2, ckvT[:, 0, T:TA]), (3, kpe_raw[:, T:TA])):
                    n += 1
                    act.wait_ge(tile_done, n)
                    act.copy(dst, bank(b, TC)).then_inc(tile_out, 1)
                for j in range(2):
                    n += 1
                    act.wait_ge(tile_done, n)
                    act.activation(mixT[:, 4 + j, :], bank(4 + j), ACT.Silu)

            @block.sync
            def _(sync):
                feed(sync)

        s3 = ExitStack()
        fa = sb("fa", [P, 2, 2, T], s3)
        fm = sb("fm", [P, 2, T], s3)
        f_done, f_out = sem("f_done"), sem("f_out")
        with nc.Block() as block:
            @block.tensor
            def _(pe):
                w = take(pe, "dft").rearrange("p (f k n) -> p f k n", f=2, k=TT)
                for f in range(2):
                    for j in range(2):
                        last = product(pe, bank(2 * f + j), lambda k: fn_tok[:, k, j * P:(j + 1) * P],
                                       lambda k: w[:, f, k, :], TT)
                        last.then_inc(f_done, 1)
                used(f_done, 4)
                pe.wait_ge(f_out, 4)
                for j in range(2):
                    pe.matmul(bank(4 + j), C("dft_cos64"), fa[:, 0, j, :], start=True, stop=False)
                    pe.matmul(bank(4 + j), C("dft_nsin64"), fa[:, 1, j, :], start=False, stop=True).then_inc(f_done, 1)
                pe.wait_ge(f_out, 6)
                w = take(pe, "fourier")[:, 0:512].rearrange("p (k n) -> p k n", k=2)
                for j in range(2):
                    last = product(pe, bank(6 + j), lambda k: w[:, k, j * P:(j + 1) * P], lambda k: fm[:, k, :], 2)
                    last.then_inc(f_done, 1)
                used(f_done, 8)

            @block.scalar
            def _(act):
                for n in range(8):
                    act.wait_ge(f_done, n + 1)
                    dst = fa[:, n // 2, n % 2, :] if n < 4 else fm[:, n - 4, :] if n < 6 else mixT[:, n, :]
                    act.copy(dst, bank(n)).then_inc(f_out, 1)

            @block.sync
            def _(sync):
                feed(sync)
        s3.close()
        s2.close()

        norm(cqT, mixT, cqT, 2, TT, 1.0 / QL, lambda k: V("q_norm_g", k, 1))
        sqk = mixT[:, 0:2, :].rearrange("p (o a) n -> p o (a n)", o=1)
        norm(ckvT, sqk, ckvT, 1, TAT, 1.0 / KVL, lambda k: V("kv_norm_g", k, 1))
        s4 = ExitStack()
        qn = mixT[:, 0:4, :]
        qp = sb("qp", [P, 2, T], s4)
        kn = sb("kn", [P, MH, TA], s4)
        v_mla = sb("v_mla", [P, TAT, MH * VH], s4)
        t_done, t_out, rot_done, roped = sem("t_done"), sem("t_out"), sem("rot_done"), sem("roped")
        with nc.Block() as block:
            outs = [(T, qp[:, j, :]) for j in range(2)] + [(T, qn[:, h, :]) for h in range(MH)]
            outs += [(n, kn[:, h, a:a + n]) for h in range(MH) for a, n in ((0, T), (T, TC))]
            outs += [(512, v_mla[:, i, :]) for i in range(TAT)]

            @block.tensor
            def _(pe):
                ch = take(pe, "mla_up")
                wq = ch[:, 0:2 * 768].rearrange("p (k n) -> p k n", k=2)
                wkv = ch[:, 2 * 768:2 * 768 + 1024]
                for n, (width, _) in enumerate(outs):
                    if n >= 6:
                        pe.wait_ge(t_out, n - 5)
                    out = bank(n % 6, width)
                    if n < 6:
                        c0 = (512 + n * P) if n < 2 else (n - 2) * P
                        last = product(pe, out, lambda k: wq[:, k, c0:c0 + P], lambda k: cqT[:, k, :], 2)
                    elif n < 6 + 2 * MH:
                        h, a = (n - 6) // 2, (n - 6) % 2
                        last = pe.matmul(out, wkv[:, h * P:(h + 1) * P], ckvT[:, 0, a * T:a * T + width],
                                         start=True, stop=True)
                    else:
                        i = n - 6 - 2 * MH
                        last = pe.matmul(out, ckvT[:, 0, i * P:(i + 1) * P], wkv[:, 512:1024], start=True, stop=True)
                    last.then_inc(t_done, 1)
                used(t_done, len(outs))
                for r in range(3):
                    if r == 2:
                        pe.wait_ge(roped, 1)
                    src = qp[:, r, :] if r < 2 else kpe_raw[:, 0:T]
                    pe.wait_ge(t_out, 2)
                    pe.matmul(bank(6 + r % 2), C("rot_mla"), src, start=True, stop=True).then_inc(rot_done, 1)

            @block.scalar
            def _(act):
                for n, (width, dst) in enumerate(outs):
                    act.wait_ge(t_done, n + 1)
                    act.copy(dst, bank(n % 6, width)).then_inc(t_out, 1)

            @block.vector
            def _(dve):
                link = chain(dve, "rope_chain")
                for r in range(3):
                    x = qp[:, r, :] if r < 2 else kpe_raw[:, 0:T]
                    dve.wait_ge(rot_done, r + 1)
                    link(dve.tensor_tensor(bank(6 + r % 2), bank(6 + r % 2), C("sin_mla"), ALU.mult))
                    link(dve.tensor_tensor(x, x, C("cos_mla"), ALU.mult))
                    dve.tensor_tensor(x, x, bank(6 + r % 2), ALU.add).then_inc(roped, 1)

            @block.sync
            def _(sync):
                feed(sync)

        s5 = ExitStack()
        prob = sb("prob", [P, 2, TA], s5)
        probT = sb("probT", [P, 2, TAT, T], s5)
        stat = sb("stat", [P, 16, 4], s5)
        score_done, max_done, exp_done, prob_done = (sem(n) for n in ("score_done", "max_done", "exp_done", "prob_done"))
        turn_done, turn_a, turn_v, pv_done, pv_out = (sem(n) for n in ("turn_done", "turn_a", "turn_v", "pv_done", "pv_out"))
        units = [(h, i) for h in range(MH) for i in range(TT)]
        with nc.Block() as block:
            @block.tensor
            def _(pe):
                def scores(u):
                    h, i = units[u]
                    par = 64 * (h % 2)
                    if u >= 2:
                        pe.wait_ge(exp_done, u - 1)
                    for a, n in ((0, T), (T, TC)):
                        out = bank(2 * (u % 2) + a // T, n)
                        pe.matmul(out, qn[:, h, i * P:(i + 1) * P], kn[:, h, a:a + n], start=True, stop=False)
                        last = pe.matmul(out, qp[par:par + 64, h // 2, i * P:(i + 1) * P],
                                         kpe_raw[par:par + 64, a:a + n], start=False, stop=True)
                    last.then_inc(score_done, 1)

                def turn(u):
                    pe.wait_ge(prob_done, u + 1)
                    if u >= 1:
                        pe.wait_ge(turn_a, u)
                        pe.wait_ge(turn_v, u)
                    for k in range(TAT):
                        last = pe.transpose(psum[:, 4 * 512 + k * P:4 * 512 + (k + 1) * P],
                                            prob[:, u % 2, k * P:(k + 1) * P], ident)
                    last.then_inc(turn_done, 1)

                def values(h):
                    pe.wait_ge(turn_a, 4 * h + 4)
                    pe.wait_ge(turn_v, 4 * h + 4)
                    if h >= 2:
                        pe.wait_ge(pv_out, h - 1)
                    product(pe, bank(6 + h % 2), lambda k: v_mla[:, k, h * VH:(h + 1) * VH],
                            lambda k: probT[:, h % 2, k, :], TAT).then_inc(pv_done, 1)

                scores(0)
                scores(1)
                for u in range(16):
                    if u + 2 < 16:
                        scores(u + 2)
                    if u % 4 == 1 and u > 1:
                        values(u // 4 - 1)
                    turn(u)
                values(MH - 1)

            @block.vector
            def _(dve):
                link = chain(dve, "softmax_chain")

                def peak(u):
                    dve.wait_ge(score_done, u + 1)
                    s = psum[:, 2 * (u % 2) * 512:2 * (u % 2) * 512 + TA]
                    link(dve.tensor_reduce(stat[:, u, 0:1], s, AX.X, ALU.max, negate=True))
                    dve.tensor_scalar(stat[:, u, 1:2], stat[:, u, 0:1], MLA_SCALE, None, ALU.mult).then_inc(max_done, 1)

                def out(u):
                    h, i = units[u]
                    dve.wait_ge(turn_done, u + 1)
                    dve.tensor_copy(probT[:, h % 2, 4:6, i * P:(i + 1) * P],
                                    bank(5, 256).rearrange("p (k n) -> p k n", k=2)).then_inc(turn_v, 1)

                peak(0)
                peak(1)
                for u in range(16):
                    dve.wait_ge(exp_done, u + 1)
                    link(dve.reciprocal(stat[:, u, 3:4], stat[:, u, 2:3]))
                    dve.tensor_scalar(prob[:, u % 2, :], prob[:, u % 2, :], stat[:, u, 3:4], None, ALU.mult)\
                       .then_inc(prob_done, 1)
                    if u + 2 < 16:
                        peak(u + 2)
                    out(u)

            @block.scalar
            def _(act):
                def exps(u):
                    act.wait_ge(max_done, u + 1)
                    if u >= 2:
                        act.wait_ge(turn_done, u - 1)
                    s = psum[:, 2 * (u % 2) * 512:2 * (u % 2) * 512 + TA]
                    act.activation(prob[:, u % 2, :], s, ACT.Exp, bias=stat[:, u, 1:2], scale=MLA_SCALE,
                                   accum_out=stat[:, u, 2:3]).then_inc(exp_done, 1)

                exps(0)
                for u in range(16):
                    h, i = units[u]
                    if u + 1 < 16:
                        exps(u + 1)
                    act.wait_ge(turn_done, u + 1)
                    act.copy(probT[:, h % 2, 0:4, i * P:(i + 1) * P],
                             bank(4).rearrange("p (k n) -> p k n", k=4)).then_inc(turn_a, 1)
                    if i == 1 and h >= 1:
                        act.wait_ge(pv_done, h)
                        act.copy(mixT[:, h - 1, :], bank(6 + (h - 1) % 2)).then_inc(pv_out, 1)
                act.wait_ge(pv_done, MH)
                act.copy(mixT[:, MH - 1, :], bank(6 + (MH - 1) % 2)).then_inc(pv_out, 1)
        s5.close()
        s4.close()
        s1.close()

        s6 = ExitStack()
        WB = P + 1
        hq = sb("hq", [P, HH, T], s6)
        kk = sb("kk", [P, 2, HH, TA], s6)
        cum = sb("cum", [P, 2 * HH, TAT, WB], s6)
        lb = sb("lb", [P, 4, 8], s6)
        logf = sb("logf", [P, 2, TA], s6)
        z_done, z_out, sig_done, f_done, ln_done, scan_done = (
            sem(n) for n in ("z_done", "z_out", "sig_done", "f_done", "ln_done", "scan_done"))
        with nc.Block() as block:
            @block.tensor
            def _(pe):
                n = 0
                for d, name in enumerate(("hff", "hfb")):
                    w = take(pe, name).rearrange("p (k n) -> p k n", k=KD)
                    for h in range(HH):
                        for part, src in ((0, hT), (1, hcT)):
                            if n >= 8:
                                pe.wait_ge(sig_done, n - 7)
                            last = product(pe, bank(n % 8, T if part == 0 else TC),
                                           lambda k: w[:, k, h * P:(h + 1) * P], lambda k: src[:, k, :], KD)
                            last.then_inc(z_done, 1)
                            n += 1
                    used(z_done, n)
                w = take(pe, "hq").rearrange("p (k n) -> p k n", k=KD)
                for h in range(HH):
                    pe.wait_ge(sig_done, n - 7)
                    last = product(pe, bank(n % 8), lambda k: w[:, k, h * P:(h + 1) * P], lambda k: hT[:, k, :], KD)
                    last.then_inc(z_done, 1)
                    n += 1
                used(z_done, n)

            @block.scalar
            def _(act):
                for n in range(16):
                    act.wait_ge(z_done, n + 1)
                    j, part = n // 2, n % 2
                    width = T if part == 0 else TC
                    act.activation(kk[:, j // 4, j % 4, part * T:part * T + width], bank(n % 8, width), ACT.Sigmoid)\
                       .then_inc(sig_done, 1)
                for h in range(HH):
                    act.wait_ge(z_done, 17 + h)
                    act.activation(hq[:, h, :], bank((16 + h) % 8), ACT.Silu).then_inc(sig_done, 1)
                for j in range(2 * HH):
                    act.wait_ge(f_done, j + 1)
                    if j >= 2:
                        act.wait_ge(scan_done, j - 1)
                    act.activation(logf[:, j % 2, :], kk[:, j // 4, j % 4, :], ACT.Ln).then_inc(ln_done, 1)

            @block.vector
            def _(dve):
                link = chain(dve, "gate_chain")
                p = V("lb_param")
                link(dve.tensor_tensor(lb[:, 0, :], p, p, ALU.subtract))
                link(dve.tensor_scalar(lb[:, 1, :], lb[:, 0, :], 1.0, None, ALU.add))
                link(dve.tensor_tensor(lb[:, 2, :], lb[:, 1, :], lb[:, 1, :], ALU.subtract))
                link(dve.tensor_scalar(lb[:, 3, :], lb[:, 2, :], -1.0, 1.0, ALU.mult, ALU.add))
                link(dve.memset(cum[:, :, :, 0:1], 0.0))
                for j in range(2 * HH):
                    k = kk[:, j // 4, j % 4, :]
                    dve.wait_ge(sig_done, 2 * j + 2)
                    link(dve.tensor_scalar(k, k, lb[:, 3, j:j + 1], lb[:, 2, j:j + 1], ALU.mult, ALU.add))
                    dve.tensor_scalar(k, k, 2.0 ** -63, None, ALU.max).then_inc(f_done, 1)
                for j in range(2 * HH):
                    dve.wait_ge(ln_done, j + 1)
                    k = kk[:, j // 4, j % 4, :]
                    dve.tensor_scalar(k, k, -1.0, 1.0, ALU.mult, ALU.add)
                    for i in range(TAT):
                        x = logf[:, j % 2, i * P:(i + 1) * P]
                        last = dve.tensor_tensor_scan(cum[:, j, i, 1:WB], C("ones"), x, 0.0, ALU.mult, ALU.add)
                    last.then_inc(scan_done, 1)

            @block.sync
            def _(sync):
                feed(sync)

        wsc = hT[:, 0:4, :]
        e_buf = [hT[:, 4, :], hT[:, 5, :]]
        q_buf = [hT[:, 6, :], hT[:, 7, :]]
        k_buf = [hcT[:, 0:2, :].rearrange("p a b -> p (a b)"), hcT[:, 2:4, :].rearrange("p a b -> p (a b)")]
        k_sum = hcT[:, 4:6, :].rearrange("p a b -> p (a b)")
        d_buf = [logf[:, 0, 0:T], logf[:, 1, 0:T]]
        s7 = ExitStack()
        state = sb("state", [P, 2 * HH, 6, HV], s7)
        dec = sb("dec", [P, 2 * HH, TAT], s7)
        lev_units = [(h, d, lev) for h in range(HH) for d in range(2) for lev in range(LEVELS)]
        NU = len(lev_units)

        def halves(ap, lev):
            v = ap.rearrange("p i (b s n) -> p i b s n", s=2, n=1 << lev)
            return v[:, :, :, 0, :], v[:, :, :, 1, :]

        diff_done, e_done, pair_done, lev_done, sel_done, ksum_done = (
            sem(n) for n in ("diff_done", "e_done", "pair_done", "lev_done", "sel_done", "ksum_done"))
        diag_done = sem("diag_done")
        with nc.Block() as block:
            @block.gpsimd
            def _(pool):
                for u in range(NU):
                    h, d, lev = lev_units[u]
                    j = d * HH + h
                    if u >= 2:
                        pool.wait_ge(e_done, u - 1)
                    view = cum[:, j, 0:TT, 1 - d:WB - d]
                    first, second = halves(view, lev)
                    df, ds = halves(d_buf[u % 2].rearrange("p (i n) -> p i n", i=TT), lev)
                    half = 1 << lev
                    nb = 64 // half
                    mid = cum[:, j, 0:TT, half:P:2 * half].rearrange("p i (b o) -> p i b o", o=1)\
                        .to_broadcast([P, TT, nb, half])
                    pool.tensor_tensor(df, mid, first, ALU.subtract)
                    pool.tensor_tensor(ds, second, mid, ALU.subtract).then_inc(diff_done, 1)

            @block.vector
            def _(dve):
                link = chain(dve, "pair_chain")

                def pairs(u):
                    h, d, lev = lev_units[u]
                    if u % (2 * LEVELS) == 0:
                        if h >= 1:
                            dve.wait_ge(diag_done, h)
                        dve.tensor_tensor(k_sum, kk[:, 0, h, 0:T], kk[:, 1, h, 0:T], ALU.add).then_inc(ksum_done, 1)
                    dve.wait_ge(e_done, u + 1)
                    if u >= 2:
                        dve.wait_ge(lev_done, u - 1)
                    ef, es = halves(e_buf[u % 2].rearrange("p (i n) -> p i n", i=TT), lev)
                    qf, qs = halves(q_buf[u % 2].rearrange("p (i n) -> p i n", i=TT), lev)
                    kf, ks = halves(k_buf[u % 2].rearrange("p (i n) -> p i n", i=TT), lev)
                    q1, q2 = halves(hq[:, h, :].rearrange("p (i n) -> p i n", i=TT), lev)
                    k1, k2 = halves(kk[:, d, h, 0:T].rearrange("p (i n) -> p i n", i=TT), lev)
                    if d == 0:
                        dve.tensor_tensor(qs, q2, es, ALU.mult)
                        dve.tensor_tensor(kf, k1, ef, ALU.mult).then_inc(pair_done, 1)
                    else:
                        dve.tensor_tensor(qf, q1, ef, ALU.mult)
                        dve.tensor_tensor(ks, k2, es, ALU.mult).then_inc(pair_done, 1)

                def choose(u):
                    h, d, lev = lev_units[u]
                    w = wsc[:, h, :].rearrange("p (i n) -> p i n", i=TT)
                    if u % (2 * LEVELS) == 0:
                        dve.wait_ge(diag_done, h + 1)
                        link(dve.tensor_copy(w, bank(4 + h % 2).rearrange("p (i n) -> p i n", i=TT)))
                    dve.wait_ge(lev_done, u + 1)
                    mask = C(("first_second" if d == 0 else "second_first") + str(lev)).bitcast(U32)
                    mask = mask.rearrange("p (o n) -> p o n", o=1).to_broadcast([P, TT, P])
                    link(dve.copy_predicated(w, mask, bank(u % 4).rearrange("p (i n) -> p i n", i=TT)))
                    dve.sem_inc(sel_done, 1)

                for b in (q_buf[0], q_buf[1], k_buf[0], k_buf[1]):
                    link(dve.memset(b, 0.0))
                for u in range(NU):
                    pairs(u)
                    if u >= 1:
                        choose(u - 1)
                choose(NU - 1)
                mod_finish(dve, 16, 48)

            @block.scalar
            def _(act):
                for j in range(2 * HH):
                    act.activation(dec[:, j, :], cum[:, j, :, P], ACT.Exp)
                for u in range(NU):
                    act.wait_ge(diff_done, u + 1)
                    if u >= 2:
                        act.wait_ge(pair_done, u - 1)
                    act.activation(e_buf[u % 2], d_buf[u % 2], ACT.Exp).then_inc(e_done, 1)
                    m = 2 * u if u < 8 else u + 8
                    if u >= 4 and (m % KD == 0):
                        mod_copy(act, 4 + m // KD - 1)
                mod_copy(act, 11)

            @block.tensor
            def _(pe):
                for u in range(NU):
                    h, d, lev = lev_units[u]
                    if u % (2 * LEVELS) == 0:
                        pe.wait_ge(ksum_done, h + 1)
                        if h >= 2:
                            pe.wait_ge(sel_done, (h - 1) * 2 * LEVELS)
                        for i in range(TT):
                            last = pe.matmul(bank(4 + h % 2)[:, i * P:(i + 1) * P], k_sum[:, i * P:(i + 1) * P],
                                             hq[:, h, i * P:(i + 1) * P], start=True, stop=True)
                        last.then_inc(diag_done, 1)
                    pe.wait_ge(pair_done, u + 1)
                    if u >= 4:
                        pe.wait_ge(sel_done, u - 3)
                    for i in range(TT):
                        sl = slice(i * P, (i + 1) * P)
                        last = pe.matmul(bank(u % 4)[:, sl], k_buf[u % 2][:, sl], q_buf[u % 2][:, sl],
                                         start=True, stop=True)
                    last.then_inc(lev_done, 1)
                    for m in ((2 * u, 2 * u + 1) if u < 8 else (u + 8,)):
                        ch, k = 4 + m // KD, m % KD
                        if k == 0:
                            view = take(pe, f"mod{ch}").rearrange("p (k n) -> p k n", k=KD)
                        if k == 2 and ch > 4:
                            mod_turn(pe, ch - 1)
                        mod_step(pe, view, ch, k)
                mod_turn(pe, 11)

            @block.sync
            def _(sync):
                feed(sync)

        kd_all = [hT[:, 4:6, :].rearrange("p a b -> p (a b)"), hcT[:, 0:4, :].rearrange("p a b -> p (a b)")]
        kt_all = [hT[:, 6:8, :].rearrange("p a b -> p (a b)"), hcT[:, 4:8, :].rearrange("p a b -> p (a b)")]
        order = ((4, 5, 0, 1, 2), (5, 4, 3, 2, 1))
        kd_diff, kd_ready, kd_e, kd_turn, kd_tok, kd_upd, kd_state = (
            sem(n) for n in ("kd_diff", "kd_ready", "kd_e", "kd_turn", "kd_tok", "kd_upd", "kd_state"))
        NS = 2 * HH

        def decayed(j):
            return kd_all[j % 2][:, 0:TA].rearrange("p (i n) -> p i n", i=TAT)

        with nc.Block() as block:
            @block.vector
            def _(dve):
                link = chain(dve, "state_chain")

                def differ(j):
                    if j >= HH:
                        return
                    if j >= 2:
                        dve.wait_ge(kd_turn, j - 1)
                    end = cum[:, j, :, P:WB].to_broadcast([P, TAT, P])
                    dve.tensor_tensor(decayed(j), end, cum[:, j, :, 1:WB], ALU.subtract).then_inc(kd_diff, 1)

                def decay(j):
                    dve.wait_ge(kd_e, j + 1)
                    dve.tensor_tensor(decayed(j), decayed(j),
                                      kk[:, j // HH, j % HH, :].rearrange("p (i n) -> p i n", i=TAT), ALU.mult)\
                       .then_inc(kd_ready, 1)

                differ(0)
                differ(1)
                decay(0)
                for j in range(NS):
                    if j + 1 < NS:
                        decay(j + 1)
                    dve.wait_ge(kd_turn, j + 1)
                    at = 2048 * (j % 2)
                    dve.tensor_copy(kt_all[j % 2][:, 0:5 * P], psum[:, at:at + 5 * P]).then_inc(kd_tok, 1)
                    differ(j + 2)
                    dve.wait_ge(kd_upd, j + 1)
                    for n in range(5):
                        u_n = bank(2 + j % 2)[:, n * HV:(n + 1) * HV]
                        if n == 0:
                            link(dve.tensor_copy(state[:, j, 1, :], u_n))
                        else:
                            i = order[j // HH][n]
                            link(dve.scalar_tensor_tensor(out=state[:, j, n + 1, :], in0=state[:, j, n, :],
                                                          scalar=dec[:, j, i:i + 1], in1=u_n, op0=ALU.mult,
                                                          op1=ALU.add))
                    dve.sem_inc(kd_state, 1)

            @block.scalar
            def _(act):
                for j in range(NS):
                    if j < HH:
                        act.wait_ge(kd_diff, j + 1)
                        act.activation(decayed(j), decayed(j), ACT.Exp).then_inc(kd_e, 1)
                    else:
                        act.wait_ge(kd_turn, j - 1)
                        act.activation(decayed(j), cum[:, j, :, 0:P], ACT.Exp).then_inc(kd_e, 1)

            @block.tensor
            def _(pe):
                def turn(j):
                    pe.wait_ge(kd_ready, j + 1)
                    if j >= 2:
                        pe.wait_ge(kd_tok, j - 1)
                    for n in range(5):
                        i = order[j // HH][n]
                        at = 2048 * (j % 2) + n * P
                        last = pe.transpose(psum[:, at:at + P], kd_all[j % 2][:, i * P:(i + 1) * P], ident)
                    last.then_inc(kd_turn, 1)

                turn(0)
                for j in range(NS):
                    if j + 1 < NS:
                        turn(j + 1)
                    h = j % HH
                    pe.wait_ge(kd_tok, j + 1)
                    if j >= 2:
                        pe.wait_ge(kd_state, j - 1)
                    for n in range(5):
                        i = order[j // HH][n]
                        last = pe.matmul(bank(2 + j % 2)[:, n * HV:(n + 1) * HV],
                                         kt_all[j % 2][:, n * P:(n + 1) * P],
                                         v_hg[:, i, h * HV:(h + 1) * HV], start=True, stop=True)
                    last.then_inc(kd_upd, 1)

        o_hg = logf.rearrange("p a n -> p (a n)")[:, 0:2 * T].rearrange("p (a n) -> p a n", a=2)
        qd = [hT[:, 4, :], hT[:, 5, :]]
        qd2 = [hT[:, 6, :], hT[:, 7, :]]
        qe_diff, qe_exp, qe_done, oh_done = (sem(n) for n in ("qe_diff", "qe_exp", "qe_done", "oh_done"))
        with nc.Block() as block:
            @block.vector
            def _(dve):
                for h in range(HH):
                    b = h % 2
                    if h >= 2:
                        dve.wait_ge(oh_done, h - 1)
                    j = HH + h
                    end = cum[:, j, 0:TT, P:WB].to_broadcast([P, TT, P])
                    dve.tensor_tensor(qd2[b].rearrange("p (i n) -> p i n", i=TT), end, cum[:, j, 0:TT, 0:P],
                                      ALU.subtract).then_inc(qe_diff, 1)
                    dve.wait_ge(qe_exp, h + 1)
                    dve.tensor_tensor(qd[b], qd[b], hq[:, h, :], ALU.mult)
                    dve.tensor_tensor(qd2[b], qd2[b], hq[:, h, :], ALU.mult).then_inc(qe_done, 1)

            @block.scalar
            def _(act):
                for h in range(HH):
                    b = h % 2
                    if h >= 2:
                        act.wait_ge(oh_done, h - 1)
                    act.activation(qd[b].rearrange("p (i n) -> p i n", i=TT), cum[:, h, 0:TT, 1:WB], ACT.Exp)
                    act.wait_ge(qe_diff, h + 1)
                    act.activation(qd2[b], qd2[b], ACT.Exp).then_inc(qe_exp, 1)
                for h in range(HH):
                    act.wait_ge(oh_done, h + 1)
                    par = 64 * (h % 2)
                    act.copy(o_hg[par:par + 64, h // 2, :], psum[par:par + 64, h * 512:(h + 1) * 512])

            @block.tensor
            def _(pe):
                for h in range(HH):
                    b, par = h % 2, 64 * (h % 2)
                    pe.wait_ge(qe_done, h + 1)
                    for i in range(TT):
                        out = psum[par:par + 64, h * 512 + i * P:h * 512 + (i + 1) * P]
                        sl = slice(i * P, (i + 1) * P)
                        pe.matmul(out, v_hg[:, i, h * HV:(h + 1) * HV], wsc[:, h, sl], start=True, stop=False)
                        pe.matmul(out, state[:, h, 2 + i, :], qd[b][:, sl], start=False, stop=False)
                        last = pe.matmul(out, state[:, HH + h, 5 - i, :], qd2[b][:, sl], start=False, stop=True)
                    last.then_inc(oh_done, 1)
        norm(o_hg, hT, o_hg, 2, TT, 1.0 / HV, lambda k: V("hg_norm_g", k, 1), heads=True,
             times=lambda k: mixT[:, 4 + k, :])
        s7.close()
        s6.close()

        early.close()

        projected = [0]
        x_set, sq_set = sem("x_set"), sem("sq_set")

        def project(names, src, gate):
            sum_bank[0] = 0
            base = projected[0]
            projected[0] += 8
            close_upper()
            mem, hs, wsp = split_space(names[0])
            high, low, unit, group_done = split_products(names, src, hs, wsp)
            with nc.Block() as block:
                @block.tensor
                def _(pe):
                    def add_square(n):
                        pe.wait_ge(sq_set, base + n + 1)
                        pe.matmul(bank(0), C("ones"), hT[:, n, :], start=(n == 0), stop=(n == 7))

                    for q in range(8):
                        unit(pe, q)
                        if q >= 5:
                            if q == 5:
                                pe.wait_ge(x_set, base + 1)
                            add_square(q - 5)
                    for n in range(3, 8):
                        add_square(n)

                @block.scalar
                def _(act):
                    high(act, 0)
                    for q in range(13):
                        high(act, q + 1)
                        if q >= 5:
                            n = q - 5
                            act.wait_ge(x_set, base + n + 1)
                            act.activation(hT[:, n, :], xT[:, n, :], ACT.Square).then_inc(sq_set, 1)

                @block.vector
                def _(dve):
                    low(dve, 0)
                    for q in range(12):
                        low(dve, q + 1)
                        if q < 4:
                            continue
                        n = q - 4
                        group_done(dve, n // 4)
                        if gate is None:
                            ins = dve.tensor_tensor(xT[:, n, :], bank(n), xT[:, n, :], ALU.add)
                        else:
                            ins = dve.scalar_tensor_tensor(out=xT[:, n, :], in0=bank(n), scalar=gate(n),
                                                           in1=xT[:, n, :], op0=ALU.mult, op1=ALU.add)
                        ins.then_inc(x_set, 1)

                @block.sync
                def _(sync):
                    feed(sync)
            mem.close()

        project(["out0", "out1"], mixT, lambda n: mod[:, 2 * KD + n, 0:1])

        def feed_forward(tag, up, ups, down, downs, gated, gain, shift, gate):
            mem = ExitStack()

            def fsb(name, shape, dt):
                return mem.enter_context(nc.sbuf_tensor(name + tag, shape, dt))
            hs = fsb("hs", [P, 2, KD, T], F32R)
            acts = fsb("acts", [P, 2, 16, T], F32R)
            wsp = fsb("wsp", [P, 2, 2, 1024], F32R)
            tmp = fsb("tmp", [P, 4, T], F32)
            s, b0 = f_sems, dict(f_at)

            def wait(eng, name, n):
                eng.wait_ge(s[name], b0[name] + n)

            s0 = 512 * sum_bank[0]
            with nc.Block() as block:
                @block.scalar
                def _(act):
                    act.activation(psum[:, s0:s0 + T], psum[:, s0:s0 + T], ACT.Sqrt, bias=epsc[:, 0:1],
                                   scale=1.0 / D).then_inc(s["nrm_root"], 1)
                    for k in range(KD):
                        wait(act, "nrm_h", k + 1)
                        if shift is not None:
                            act.activation(tmp[:, k % 4, :], tmp[:, k % 4, :], ACT.Identity, bias=shift(k), scale=1.0)\
                               .then_inc(s["nrm_s"], 1)
                            wait(act, "nrm_s", k + 1)
                        act.copy(hs[:, 0, k, :], tmp[:, k % 4, :]).then_inc(s["nrm_hi"], 1)

                @block.vector
                def _(dve):
                    def low(k):
                        wait(dve, "nrm_hi", k + 1)
                        dve.tensor_tensor(hs[:, 1, k, :], tmp[:, k % 4, :], hs[:, 0, k, :].bitcast(F32), ALU.subtract)\
                           .then_inc(s["nrm_lo"], 1)
                    wait(dve, "nrm_root", 1)
                    dve.reciprocal(psum[:, 1024:1024 + T], psum[:, s0:s0 + T]).then_inc(s["nrm_inv"], 1)
                    wait(dve, "nrm_inv", 1)
                    for k in range(KD):
                        if k >= 4:
                            wait(dve, "nrm_lo", k - 3)
                        dve.scalar_tensor_tensor(out=tmp[:, k % 4, :], in0=xT[:, k, :], scalar=gain(k),
                                                 in1=psum[:, 1024:1024 + T], op0=ALU.mult, op1=ALU.mult)\
                           .then_inc(s["nrm_h"], 1)
                        if k >= 1:
                            low(k - 1)
                    low(KD - 1)

                @block.sync
                def _(sync):
                    feed(sync)

            units, groups, chunks, c, e0 = [], [], [], 0, 0
            for part in range(2):
                for i in range(ups[part]):
                    lo = len(units)
                    units += [(len(chunks), 2 * u, hs, 2 * u, u == 0, u == 3, len(groups), 0) for u in range(4)]
                    chunks.append((f"{up}{c + i}", lo, lo + 4))
                    groups.append(("up", lo + 3, e0))
                    e0 += 2 if gated else 4
                c += ups[part]
                ready0 = e0 - sum(downs[part])
                for h in range(2):
                    k0, n = 0, sum(downs[part])
                    for i, kt in enumerate(downs[part]):
                        lo = len(units)
                        units += [(len(chunks), 2 * u, acts, k0 + 2 * u, k0 + u == 0, k0 + 2 * u + 2 == n, len(groups),
                                   ready0 + k0 + 2 * u + 2) for u in range(kt // 2)]
                        chunks.append((f"{down}{part}_{h}_{i}", lo, len(units)))
                        k0 += kt
                    groups.append(("down", len(units) - 1, 4 * h, part))
            NQ, NG_ = len(units), len(groups)
            part_of = [0] * sum(downs[0]) + [1] * sum(downs[1])
            on_act = [[] for _ in range(NQ + 8)]
            on_dve = [[] for _ in range(NQ + 8)]
            freed = []
            na = nb = nr = 0
            for g, grp in enumerate(groups):
                at = grp[1] + 1
                if grp[0] == "down":
                    for j in range(4):
                        on_dve[at + j].append(("res", g, j, grp[2] + j, nr))
                        if grp[3] == 1:
                            on_act[at + j + 1].append(("square", grp[2] + j, nr))
                        nr += 1
                else:
                    for j in range(4):
                        if gated:
                            e = grp[2] + j % 2
                            if j < 2:
                                on_act[at + j].append(("a", g, j, e))
                                na += 1
                        else:
                            e = grp[2] + j
                            on_act[at + j].append(("a", g, j, e))
                            na += 1
                        if not gated or j >= 2:
                            on_dve[at + j].append(("b", g, j, e))
                            nb += 1
                            on_act[at + j + 1].append(("hi", e))
                            on_dve[at + j + 1].append(("lo", e))
                freed.append((na, nb, nr))
            sum_bank[0] = 4 * ((NG_ - 2) % 2)
            first_chunk = cursor[0]
            raw = []
            for n, (name, lo, hi) in enumerate(chunks):
                i = cursor[0]
                assert PLAN[i][0] == name, (PLAN[i], name)
                cursor[0] += 1
                raw.append(i)
                used(s["w_lo"], b0["w_lo"] + hi)

            def raw_view(q):
                i, k = raw[units[q][0]], units[q][1]
                return ring[:, i % RING, k * 512:(k + 2) * 512]

            def tile_bank(g, j):
                return bank(4 * (g % 2) + j)

            def place(e):
                return e - (sum(downs[0]) if part_of[e] else 0)

            with nc.Block() as block:
                @block.tensor
                def _(pe):
                    sq = 0

                    def add_square():
                        wait(pe, "sq2_set", sq + 1)
                        pe.matmul(bank(sum_bank[0]), C("ones"), tmp[:, sq % 4, :], start=(sq == 0), stop=(sq == 7))\
                          .then_inc(s["sq2_read"], 1)
                        return sq + 1

                    for q, (n, k, src, k0, first, last_k, g, ready) in enumerate(units):
                        wait(pe, "w_lo", q + 1)
                        if ready:
                            wait(pe, "act_lo", ready)
                        if first and g >= 2:
                            for name, v in zip(("act_a", "act_b", "res_set"), freed[g - 2]):
                                if v:
                                    wait(pe, name, v)
                        for j in range(4):
                            for i in range(2):
                                w_hi = wsp[:, q % 2, 0, i * 512 + j * P:i * 512 + (j + 1) * P]
                                w_lo = wsp[:, q % 2, 1, i * 512 + j * P:i * 512 + (j + 1) * P]
                                pe.matmul(tile_bank(g, j), w_hi, src[:, 0, k0 + i, :], start=(first and i == 0),
                                          stop=False)
                                pe.matmul(tile_bank(g, j), w_hi, src[:, 1, k0 + i, :], start=False, stop=False)
                                last = pe.matmul(tile_bank(g, j), w_lo, src[:, 0, k0 + i, :], start=False,
                                                 stop=(last_k and i == 1))
                        last.then_inc(s["unit_done"], 1)
                        if g == NG_ - 1 and q >= groups[NG_ - 2][1] + 3 and sq < 4:
                            sq = add_square()
                    while sq < 8:
                        sq = add_square()

                @block.scalar
                def _(act):
                    def split(q):
                        i = raw[units[q][0]]
                        act.wait_ge(weight_landed[i % RING], 16 * (i // RING + 1))
                        if q >= 2:
                            wait(act, "unit_done", q - 1)
                        act.copy(wsp[:, q % 2, 0, :], raw_view(q)).then_inc(s["w_hi"], 1)

                    split(0)
                    for q in range(NQ + 8):
                        if q + 1 < NQ:
                            split(q + 1)
                        for job in on_act[q]:
                            if job[0] == "a":
                                _, g, j, e = job
                                wait(act, "unit_done", groups[g][1] + 1)
                                if e >= 4:
                                    wait(act, "act_lo", e - 3)
                                act.activation(tmp[:, e % 4, :], tile_bank(g, j), ACT.Silu if gated else ACT.Relu)\
                                   .then_inc(s["act_a"], 1)
                            elif job[0] == "hi":
                                e = job[1]
                                wait(act, "act_b", e + 1)
                                act.copy(acts[:, 0, place(e), :], tmp[:, e % 4, :]).then_inc(s["act_hi"], 1)
                            else:
                                _, n, r = job
                                wait(act, "res_set", r + 1)
                                if n >= 4:
                                    wait(act, "sq2_read", n - 3)
                                act.activation(tmp[:, n % 4, :], xT[:, n, :], ACT.Square).then_inc(s["sq2_set"], 1)

                @block.vector
                def _(dve):
                    def split(q):
                        wait(dve, "w_hi", q + 1)
                        dve.tensor_tensor(wsp[:, q % 2, 1, :], raw_view(q), wsp[:, q % 2, 0, :].bitcast(F32),
                                          ALU.subtract).then_inc(s["w_lo"], 1)

                    split(0)
                    for q in range(NQ + 8):
                        if q + 1 < NQ:
                            split(q + 1)
                        for job in on_dve[q]:
                            if job[0] == "b":
                                _, g, j, e = job
                                wait(dve, "unit_done", groups[g][1] + 1)
                                wait(dve, "act_a", e + 1)
                                t = tmp[:, e % 4, :]
                                dve.tensor_tensor(t, t, tile_bank(g, j) if gated else t, ALU.mult)\
                                   .then_inc(s["act_b"], 1)
                            elif job[0] == "lo":
                                e = job[1]
                                wait(dve, "act_hi", e + 1)
                                dve.tensor_tensor(acts[:, 1, place(e), :], tmp[:, e % 4, :],
                                                  acts[:, 0, place(e), :].bitcast(F32), ALU.subtract)\
                                   .then_inc(s["act_lo"], 1)
                            else:
                                _, g, j, n, r = job
                                wait(dve, "unit_done", groups[g][1] + 1)
                                if r >= 8:
                                    wait(dve, "res_set", r - 7)
                                if gate is None:
                                    ins = dve.tensor_tensor(xT[:, n, :], tile_bank(g, j), xT[:, n, :], ALU.add)
                                else:
                                    ins = dve.scalar_tensor_tensor(out=xT[:, n, :], in0=tile_bank(g, j),
                                                                   scalar=gate(n), in1=xT[:, n, :], op0=ALU.mult,
                                                                   op1=ALU.add)
                                ins.then_inc(s["res_set"], 1)

                @block.sync
                def _(sync):
                    feed(sync)
            for name, n in (("w_hi", NQ), ("w_lo", NQ), ("unit_done", NQ), ("act_a", na), ("act_b", nb), ("act_hi", nb),
                            ("act_lo", nb), ("res_set", nr), ("sq2_set", 8), ("sq2_read", 8), ("nrm_root", 1),
                            ("nrm_inv", 1), ("nrm_h", KD), ("nrm_s", KD if shift is not None else 0), ("nrm_hi", KD),
                            ("nrm_lo", KD)):
                f_at[name] += n
            mem.close()

        phase.close()
        feed_forward("_ffn", "gu", FFN1_UP, "dn", FFN1_DOWN, True, lambda k: gmod[:, 2 * KD + k:2 * KD + k + 1],
                     lambda k: mod[:, 3 * KD + k, 0:1], lambda n: mod[:, 5 * KD + n, 0:1])
        phase, hT, mixT = mixer_memory(1, LOW)
        norm(xT, hT, xT, KD, TT, 1.0 / D, lambda k: V("final_norm_g", k, 1), presummed=True)

        norm(xT, hT, hT, KD, TT, 1.0 / D, lambda k: V("mix0", k, 1))
        e1 = ExitStack()
        cv = sb("cv", [P, 12, T], e1)
        tok = sb("tok", [P, 12, TT * GH], e1)
        e2 = ExitStack()
        ch = mixT[:, 4:8, :]
        cs = sb("cs", [P, 4, T], e2)
        ab_done, conv_out, ab_out = sem("ab_done"), sem("conv_out"), sem("ab_out")
        z_out, cg_out, hs_out = sem("z_out"), sem("cg_out"), sem("hs_out")
        parts, hs, wsp = split_space("ev")
        ev_ab = claim("ev_ab")
        used(ab_done, 1)
        high, low, unit, group_done = split_products([f"ev{g}" for g in range(7)], hT, hs, wsp)
        with nc.Block() as block:
            @block.tensor
            def _(pe):
                pe.wait_ge(weight_landed[ev_ab % RING], 16 * (ev_ab // RING + 1))
                w = ring[:, ev_ab % RING, 0:128].rearrange("p (k n) -> p k n", k=KD)
                for i in range(TT):
                    last = product(pe, psum[:, 7 * 512 + i * 16:7 * 512 + (i + 1) * 16],
                                   lambda k: hT[:, k, i * P:(i + 1) * P], lambda k: w[:, k, :], KD)
                last.then_inc(ab_done, 1)
                for q in range(28):
                    if q % 4 == 0 and q >= 4:
                        g = q // 4 - 2
                        if g < 0:
                            pe.wait_ge(ab_out, 1)
                        elif g < 3:
                            pe.wait_ge(conv_out, 4 * g + 4)
                        else:
                            pe.wait_ge(z_out, 4 * (g - 3) + 4)
                    unit(pe, q)

            @block.vector
            def _(dve):
                link = chain(dve, "conv_chain")

                def conv(dst, src, taps, width, last_sem):
                    link(dve.tensor_scalar(dst, src, taps(width - 1), None, ALU.mult))
                    for j in range(1, width):
                        ins = dve.scalar_tensor_tensor(out=dst[:, j:T], in0=src[:, 0:T - j], scalar=taps(width - 1 - j),
                                                       in1=dst[:, j:T], op0=ALU.mult, op1=ALU.add)
                        if j < width - 1:
                            link(ins)
                    ins.then_inc(last_sem, 1)

                low(dve, 0)
                for q in range(32):
                    low(dve, q + 1)
                    n = q - 4
                    if 0 <= n < 12:
                        group_done(dve, n // 4)
                        conv(cv[:, n, :], bank(n % 8), lambda j: V("conv", 4 * n + j, 1), 4, conv_out)
                    elif 20 <= n < 24:
                        i = n - 20
                        group_done(dve, n // 4)
                        dve.wait_ge(z_out, 4 + i + 1)
                        dve.tensor_tensor(ch[:, i, :], bank(n % 8), ch[:, i, :], ALU.mult).then_inc(hs_out, 1)
                        dve.wait_ge(hs_out, i + 1)
                        conv(cs[:, i, :], ch[:, i, :], lambda j: V("sc_conv", 3 * i + j, 1), 3, cg_out)
                    elif n >= 24:
                        i = n - 24
                        group_done(dve, n // 4)
                        dve.wait_ge(cg_out, i + 1)
                        dve.tensor_tensor(mixT[:, 4 + i, :], bank(n % 8), cs[:, i, :], ALU.mult)

            @block.scalar
            def _(act):
                high(act, 0)
                high(act, 1)
                act.wait_ge(ab_done, 1)
                act.copy(sums[:, :], psum[:, 7 * 512:7 * 512 + 64]).then_inc(ab_out, 1)
                for q in range(1, 28):
                    high(act, q + 1)
                    n = q - 4
                    if 1 <= n <= 12:
                        act.wait_ge(conv_out, n)
                        act.activation(cv[:, n - 1, :], cv[:, n - 1, :], ACT.Silu)
                    if 12 <= n < 16:
                        group_done(act, 3)
                        act.activation(mixT[:, n - 12, :], bank(n % 8), ACT.Silu).then_inc(z_out, 1)
                    elif 16 <= n < 20:
                        group_done(act, 4)
                        act.copy(ch[:, n - 16, :], bank(n % 8)).then_inc(z_out, 1)

            @block.sync
            def _(sync):
                feed(sync)
        e2.close()
        parts.close()
        open_upper(1, LOW)

        G, BETA, GC, GTOT, EGC, KDE, BEG, T0, T1, T2 = range(10)

        def tk(i):
            return tok[:, i, :].rearrange("p (c h) -> p c h", h=GH)

        lin, lin2, abs_done, exp1, sp_done, g_done, gc_done, gd2 = (
            sem(n) for n in ("lin", "lin2", "abs_done", "exp1", "sp_done", "g_done", "gc_done", "gd2"))
        alog = sb("alog", [P, GH], e1)
        with nc.Block() as block:
            ab = sums[:, :].rearrange("p (c n) -> p c n", n=16)

            @block.vector
            def _(dve):
                link = chain(dve, "tok_chain")
                dtb = V("dt_bias").rearrange("p (o h) -> p o h", o=1).to_broadcast([P, TT, GH])
                dve.tensor_tensor(tk(T0), ab[:, :, 0:GH], dtb, ALU.add).then_inc(lin, 1)
                dve.wait_ge(sp_done, 1)
                link(dve.tensor_scalar(tk(T2), tk(T0), 0.0, None, ALU.max))
                link(dve.tensor_tensor(tk(T2), tk(T2), tk(T1), ALU.add))
                link(dve.tensor_scalar(tk(T2), tk(T2), -1.0, None, ALU.mult))
                ea = alog[:, :].rearrange("p (o h) -> p o h", o=1).to_broadcast([P, TT, GH])
                dve.tensor_tensor(tk(G), tk(T2), ea, ALU.mult).then_inc(g_done, 1)
                dve.wait_ge(gc_done, 1)
                link(dve.tensor_copy(tk(GC), psum[:, 512:544].rearrange("p (c h) -> p c h", h=GH)))
                dve.tensor_tensor(tk(T1), psum[:, 1024:1056].rearrange("p (c h) -> p c h", h=GH), tk(GC),
                                  ALU.subtract).then_inc(lin2, 1)
                dve.wait_ge(gd2, 1)
                dve.tensor_tensor(tk(BEG), tk(EGC), tk(BETA), ALU.mult)

            @block.scalar
            def _(act):
                act.activation(alog[:, :], V("a_log"), ACT.Exp)
                act.wait_ge(lin, 1)
                act.activation(tk(BETA), ab[:, :, GH:2 * GH], ACT.Sigmoid)
                act.activation(tk(T1), tk(T0), ACT.Abs).then_inc(abs_done, 1)
                act.wait_ge(abs_done, 1)
                act.activation(tk(T1), tk(T1), ACT.Exp, scale=-1.0).then_inc(exp1, 1)
                act.wait_ge(exp1, 1)
                act.activation(tk(T1), tk(T1), ACT.Ln, bias=1.0, scale=1.0).then_inc(sp_done, 1)
                act.wait_ge(lin2, 1)
                act.activation(tk(KDE), tk(T1), ACT.Exp)
                act.activation(tk(EGC), tk(GC), ACT.Exp).then_inc(gd2, 1)

            @block.tensor
            def _(pe):
                pe.wait_ge(g_done, 1)
                for c in range(TT):
                    pe.matmul(psum[:, 512 + c * GH:512 + (c + 1) * GH], C("upto"), tk(G)[:, c, :],
                              start=True, stop=True)
                for c in range(TT):
                    last = pe.matmul(psum[:, 1024 + c * GH:1024 + (c + 1) * GH], C("ones"), tk(G)[:, c, :],
                                     start=True, stop=True)
                last.then_inc(gc_done, 1)

        norm(cv, hT, cv, 8, TT, 1.0, lambda k: C("eighth") if k < 4 else C("one"), heads=True)

        mt = hT[:, 0:4, :]
        attn = hT[:, 4:8, :]
        e3 = ExitStack()
        X = sb("X", [P, 4, T], e3)
        XT = sb("XT", [P, 4, T], e3)
        Y = sb("Y", [P, 4, T], e3)
        ml = sb("ml", [P, 4, T], e3)
        kbg = sb("kbg", [P, TT, 4 * GD], e3)
        kde = sb("kde", [P, TT, 4 * GD], e3)
        bv = sb("bv", [P, TT, 4 * GD], e3)
        qg = sb("qg", [P, 2, T], e3)
        edge = sb("edge", [P, 4, TT], e3)
        st = sb("st", [P, 2, GD], e3)
        vn = sb("vn", [P, 4, GD], e3)

        def c4(ap):
            return ap.rearrange("p (c n) -> p c n", c=TT)

        half_sems = {}
        sem_of_program = sem

        def half_sem(name):
            if name not in half_sems:
                half_sems[name] = sem_of_program(name)
            return half_sems[name]

        for half in range(2):
            h0 = 4 * half
            if half:
                with nc.Block() as block:
                    @block.gpsimd
                    def _(pool):
                        for s in half_sems.values():
                            pool.sem_clear(s)
            kv_turn, kv_out = half_sem("kv_turn"), half_sem("kv_out")
            with nc.Block() as block:
                @block.tensor
                def _(pe):
                    for c in range(TT):
                        for s, base in enumerate((4, 8)):
                            for j in range(2):
                                at = c * 1024 + s * 512
                                last = pe.transpose(psum[:, at + j * P:at + (j + 1) * P],
                                                    cv[:, base + 2 * half + j, c * P:(c + 1) * P], ident)
                        last.then_inc(kv_turn, 1)

                @block.vector
                def _(dve):
                    for c in range(TT):
                        dve.wait_ge(kv_turn, c + 1)

                        def per_head(i):
                            return tk(i)[:, c, h0:h0 + 4].rearrange("p (h o) -> p h o", o=1).to_broadcast([P, 4, GD])

                        def heads(ap):
                            return ap.rearrange("p (h n) -> p h n", h=4)
                        k_t, v_t = heads(psum[:, c * 1024:c * 1024 + 256]), heads(psum[:, c * 1024 + 512:c * 1024 + 768])
                        dve.tensor_tensor(heads(kbg[:, c, :]), k_t, per_head(BEG), ALU.mult)
                        dve.tensor_tensor(heads(kde[:, c, :]), k_t, per_head(KDE), ALU.mult)
                        dve.tensor_tensor(heads(bv[:, c, :]), v_t, per_head(BETA), ALU.mult)

            raw_done, dt_done, dec_done, raw_free, edge_done = (
                half_sem(n) for n in ("raw_done", "dt_done", "dec_done", "raw_free", "edge_done"))
            with nc.Block() as block:
                @block.tensor
                def _(pe):
                    for n in range(4):
                        h = h0 + n
                        par, tile = 64 * (h % 2), h // 2
                        b = 4 * (n % 2)
                        if n >= 2:
                            pe.wait_ge(raw_free, n - 1)
                            pe.wait_ge(edge_done, n - 1)
                        for c in range(TT):
                            sl = slice(c * P, (c + 1) * P)
                            kT = cv[par:par + 64, 4 + tile, sl]
                            qT = cv[par:par + 64, tile, sl]
                            pe.matmul(bank(b)[:, sl], tk(G)[:, c, h:h + 1].to_broadcast([P, P]), C("upto"),
                                      start=True, stop=True)
                            pe.matmul(bank(b + 1)[:, sl], tk(BETA)[:, c, h:h + 1].to_broadcast([P, P]), ident,
                                      start=True, stop=True)
                            pe.matmul(bank(b + 2)[:, sl], kT, kT, start=True, stop=True)
                            last = pe.matmul(bank(b + 3)[:, sl], kT, qT, start=True, stop=True)
                        last.then_inc(raw_done, 1)

                @block.vector
                def _(dve):
                    link = chain(dve, "m_chain", half_sem)
                    for n in range(4):
                        h = h0 + n
                        b = 4 * (n % 2)
                        par, tile = 64 * (h % 2), h // 2
                        dve.wait_ge(raw_done, n + 1)
                        gc = tk(GC)[:, :, h:h + 1].to_broadcast([P, TT, P])
                        d = Y[:, n, :]
                        link(dve.tensor_tensor(c4(d), c4(bank(b)), gc, ALU.subtract))
                        dve.tensor_scalar(d, d, 0.0, None, ALU.min).then_inc(dt_done, 1)
                        dve.wait_ge(dec_done, n + 1)
                        upto = C("upto").rearrange("p (o n) -> p o n", o=1).to_broadcast([P, TT, P])
                        link(dve.tensor_tensor(c4(d), c4(d), upto, ALU.mult))
                        dve.tensor_tensor(attn[:, n, :], bank(b + 3), d, ALU.mult)
                        link(dve.tensor_tensor(mt[:, n, :], bank(b + 2), d, ALU.mult))
                        dve.tensor_tensor(mt[:, n, :], mt[:, n, :], bank(b + 1), ALU.mult).then_inc(raw_free, 1)
                        dve.wait_ge(edge_done, n + 1)
                        rows = slice(par, par + 64)
                        dve.tensor_tensor(qg[rows, n // 2, :], cv[rows, tile, :], X[rows, n, :], ALU.mult)

                @block.scalar
                def _(act):
                    for n in range(4):
                        b = 4 * (n % 2)
                        act.wait_ge(dt_done, n + 1)
                        act.activation(X[:, n, :], bank(b), ACT.Exp)
                        act.activation(edge[:, n, :], c4(bank(b))[:, :, P - 1], ACT.Exp).then_inc(edge_done, 1)
                        act.activation(Y[:, n, :], Y[:, n, :], ACT.Exp).then_inc(dec_done, 1)

            init_done, x_turn, xi_set = half_sem("init_done"), half_sem("x_turn"), half_sem("xi_set")
            ml_done, y_done, y_out, zz_done, xx_done = (half_sem(n) for n in ("ml_done", "y_done", "y_out", "zz_done", "xx_done"))
            NS = 4 * (LEVELS - 1)
            with nc.Block() as block:
                @block.vector
                def _(dve):
                    link = chain(dve, "init_chain", half_sem)
                    idb = ident.rearrange("p (o n) -> p o n", o=1).to_broadcast([P, TT, P])

                    def mask(lev):
                        return C(f"first_second{lev}").rearrange("p (o n) -> p o n", o=1).to_broadcast([P, TT, P])
                    for n in range(4):
                        link(dve.tensor_tensor(c4(XT[:, n, :]), c4(mt[:, n, :]), mask(0), ALU.mult))
                        dve.tensor_tensor(c4(XT[:, n, :]), idb, c4(XT[:, n, :]), ALU.subtract).then_inc(init_done, 1)

                    def masked(s):
                        lev, n = 1 + s // 4, s % 4
                        if s >= 4:
                            dve.wait_ge(y_done, s - 3)
                        dve.tensor_tensor(c4(ml[:, s % 4, :]), c4(mt[:, n, :]), mask(lev), ALU.mult).then_inc(ml_done, 1)
                    for s in range(4):
                        masked(s)
                    for s in range(NS):
                        n = s % 4
                        dve.wait_ge(zz_done, s + 1)
                        if s < NS - 4:
                            dve.tensor_tensor(X[:, n, :], X[:, n, :], bank(4 + 2 * (s % 2)), ALU.subtract)
                        dve.tensor_tensor(XT[:, n, :], XT[:, n, :], bank(5 + 2 * (s % 2)), ALU.subtract)\
                           .then_inc(xx_done, 1)
                        if s + 4 < NS:
                            masked(s + 4)

                @block.tensor
                def _(pe):
                    for n in range(4):
                        pe.wait_ge(init_done, n + 1)
                        for c in range(TT):
                            sl = slice(c * P, (c + 1) * P)
                            last = pe.transpose(bank(n)[:, sl], XT[:, n, sl], ident)
                        last.then_inc(x_turn, 1)

                    def first(s):
                        n = s % 4
                        pe.wait_ge(ml_done, s + 1)
                        if s >= 4:
                            pe.wait_ge(xx_done, s - 3)
                            pe.wait_ge(y_out, s - 3)
                        else:
                            pe.wait_ge(xi_set, n + 1)
                        for c in range(TT):
                            sl = slice(c * P, (c + 1) * P)
                            last = pe.matmul(bank(s % 4)[:, sl], ml[:, s % 4, sl], X[:, n, sl], start=True, stop=True)
                        last.then_inc(y_done, 1)

                    def second(s):
                        n = s % 4
                        pe.wait_ge(y_out, s + 1)
                        if s >= 2:
                            pe.wait_ge(xx_done, s - 1)
                        for c in range(TT):
                            sl = slice(c * P, (c + 1) * P)
                            if s < NS - 4:
                                pe.matmul(bank(4 + 2 * (s % 2))[:, sl], XT[:, n, sl], Y[:, n, sl], start=True, stop=True)
                            last = pe.matmul(bank(5 + 2 * (s % 2))[:, sl], Y[:, n, sl], XT[:, n, sl], start=True,
                                             stop=True)
                        last.then_inc(zz_done, 1)
                    first(0)
                    for s in range(NS):
                        if s + 1 < NS:
                            first(s + 1)
                        second(s)

                @block.scalar
                def _(act):
                    for n in range(4):
                        act.wait_ge(x_turn, n + 1)
                        act.copy(X[:, n, :], bank(n)).then_inc(xi_set, 1)
                    for s in range(NS):
                        act.wait_ge(y_done, s + 1)
                        if s >= 4:
                            act.wait_ge(zz_done, s - 3)
                        act.copy(Y[:, s % 4, :], bank(s % 4)).then_inc(y_out, 1)

            uw_done, uw_out = half_sem("uw_done"), half_sem("uw_out")
            u_v = X[:, 0:2, :].rearrange("p a (c n) -> p (a c) n", c=2)
            w_t = Y[:, 0:2, :]
            with nc.Block() as block:
                @block.tensor
                def _(pe):
                    for n in range(4):
                        par = 64 * (n % 2)
                        for c in range(TT):
                            sl = slice(c * P, (c + 1) * P)
                            pe.matmul(bank(n)[:, c * GD:(c + 1) * GD], XT[:, n, sl], bv[:, c, n * GD:(n + 1) * GD],
                                      start=True, stop=True)
                        for c in range(TT):
                            sl = slice(c * P, (c + 1) * P)
                            last = pe.matmul(psum[par:par + 64, (4 + n) * 512 + c * P:(4 + n) * 512 + (c + 1) * P],
                                             kbg[:, c, n * GD:(n + 1) * GD], XT[:, n, sl], start=True, stop=True)
                        last.then_inc(uw_done, 1)

                @block.scalar
                def _(act):
                    for n in range(4):
                        par = 64 * (n % 2)
                        act.wait_ge(uw_done, n + 1)
                        act.copy(u_v[:, n, :], bank(n, 256))
                        act.copy(w_t[par:par + 64, n // 2, :], psum[par:par + 64, (4 + n) * 512:(5 + n) * 512])

            pred_done, vn_done, o_done, up_done, st_done = (
                half_sem(n) for n in ("pred_done", "vn_done", "o_done", "up_done", "st_done"))
            with nc.Block() as block:
                @block.tensor
                def _(pe):
                    for c in range(TT):
                        sl = slice(c * P, (c + 1) * P)
                        for n in range(4):
                            par = 64 * (n % 2)
                            rows = slice(par, par + 64)
                            if c >= 1:
                                pe.wait_ge(st_done, 4 * (c - 1) + n + 1)
                                pe.matmul(bank(n)[:, 0:GD], w_t[rows, n // 2, sl], st[rows, n // 2, :],
                                          start=True, stop=True).then_inc(pred_done, 1)
                        for n in range(4):
                            par = 64 * (n % 2)
                            rows = slice(par, par + 64)
                            pe.wait_ge(vn_done, 4 * c + n + 1)
                            out = psum[par:par + 64, (4 + n) * 512 + c * P:(4 + n) * 512 + (c + 1) * P]
                            pe.matmul(out, vn[:, n, :], attn[:, n, sl], start=True, stop=(c == 0))
                            if c >= 1:
                                pe.matmul(out, st[rows, n // 2, :], qg[rows, n // 2, sl], start=False, stop=True)
                            pe.matmul(psum[par:par + 64, n * 512 + 256:n * 512 + 256 + GD],
                                      kde[:, c, n * GD:(n + 1) * GD], vn[:, n, :], start=True, stop=True)\
                              .then_inc(up_done, 1)

                @block.vector
                def _(dve):
                    for c in range(TT):
                        for n in range(4):
                            u_c = u_v[:, n, c * GD:(c + 1) * GD]
                            if c == 0:
                                dve.tensor_copy(vn[:, n, :], u_c).then_inc(vn_done, 1)
                            else:
                                dve.wait_ge(pred_done, 4 * (c - 1) + n + 1)
                                dve.wait_ge(up_done, 4 * (c - 1) + n + 1)
                                dve.tensor_tensor(vn[:, n, :], u_c, bank(n)[:, 0:GD], ALU.subtract).then_inc(vn_done, 1)
                        for n in range(4):
                            par = 64 * (n % 2)
                            rows = slice(par, par + 64)
                            dve.wait_ge(up_done, 4 * c + n + 1)
                            up = psum[rows, n * 512 + 256:n * 512 + 256 + GD]
                            if c == 0:
                                dve.tensor_copy(st[rows, n // 2, :], up).then_inc(st_done, 1)
                            else:
                                dve.wait_ge(st_done, 4 * (c - 1) + n + 1)
                                dve.scalar_tensor_tensor(out=st[rows, n // 2, :], in0=st[rows, n // 2, :],
                                                         scalar=edge[rows, n, c:c + 1], in1=up, op0=ALU.mult,
                                                         op1=ALU.add).then_inc(st_done, 1)

                @block.scalar
                def _(act):
                    act.wait_ge(up_done, 16)
                    for n in range(4):
                        par = 64 * (n % 2)
                        act.copy(cv[par:par + 64, 8 + 2 * half + n // 2, :],
                                 psum[par:par + 64, (4 + n) * 512:(5 + n) * 512])
        e3.close()
        norm(cv[:, 8:12, :], hT, cv[:, 8:12, :], 4, TT, 1.0 / GD, lambda k: V("o_norm"), heads=True,
             times=lambda k: mixT[:, k, :])
        e1.close()
        project(["evo0", "evo1"], mixT, None)

        phase.close()
        feed_forward("_mlp0", "up0_", MLP_UP, "down0_", MLP_DOWN, False, lambda k: V("mlp0", k, 1), None, None)
        phase, hT, mixT = mixer_memory(2, LOW)

        norm(xT, hT, hT, KD, TT, 1.0 / D, lambda k: V("mix1", k, 1), presummed=True)
        n1 = ExitStack()
        kr = sb("kr", [P, 4, T], n1)
        vtok = sb("vtok", [P, TT, 512], n1)
        gates = sb("gates", [P, TT, 48], n1)
        n2 = ExitStack()
        qT = mixT
        kvc = sb("kvc", [P, 4, T], n2)
        gl_done, t_out = sem("gl_done"), sem("t_out")
        parts, hs, wsp = split_space("od")
        gl = claim("gl")
        used(gl_done, 1)
        high, low, unit, group_done = split_products([f"od{g}" for g in range(5)], hT, hs, wsp, tokens=(4,))
        with nc.Block() as block:
            dests = [(qT[:, n, :], 0.125) for n in range(8)] + [(kvc[:, n, :], 1.0) for n in range(4)]
            dests += [(kr[:, n, :], 1.0) for n in range(4)] + [(vtok[:, n, :], 1.0) for n in range(4)]

            @block.tensor
            def _(pe):
                pe.wait_ge(weight_landed[gl % RING], 16 * (gl // RING + 1))
                w = ring[:, gl % RING, 0:8 * 48].rearrange("p (k n) -> p k n", k=KD)
                for i in range(TT):
                    last = product(pe, psum[:, 7 * 512 + i * 48:7 * 512 + (i + 1) * 48],
                                   lambda k: hT[:, k, i * P:(i + 1) * P], lambda k: w[:, k, :], KD)
                last.then_inc(gl_done, 1)
                for q in range(20):
                    if q == 4:
                        pe.wait_ge(t_out, 1)
                    if q >= 8 and q % 4 == 0:
                        pe.wait_ge(t_out, 1 + q - 4)
                    unit(pe, q)

            @block.scalar
            def _(act):
                high(act, 0)
                high(act, 1)
                act.wait_ge(gl_done, 1)
                act.activation(gates[:, :, :].rearrange("p c n -> p (c n)"), psum[:, 7 * 512:7 * 512 + 192],
                               ACT.Sigmoid).then_inc(t_out, 1)
                for q in range(1, 24):
                    high(act, q + 1)
                    if q >= 4:
                        n = q - 4
                        dst, scale = dests[n]
                        group_done(act, n // 4)
                        act.mul(dst, bank(n % 8), scale).then_inc(t_out, 1)

            @block.vector
            def _(dve):
                for q in range(20):
                    low(dve, q)

            @block.sync
            def _(sync):
                feed(sync)
        parts.close()
        open_upper(2, LOW)
        qr = sb("qr", [P, 8, T], n1)

        r_done, r_out, stacked = sem("r_done"), sem("r_out"), sem("stacked")
        pairs_ = hT[:, :, :].rearrange("p (v g) n -> p v g n", v=2)
        with nc.Block() as block:
            @block.sync
            def _(sync):
                for kv in range(2):
                    for g in range(NG):
                        src = kvc[64 * (g % 2):64 * (g % 2) + 64, 2 * kv + g // 2, :]
                        sync.dma_start(pairs_[0:64, kv, g, :], src).then_inc(stacked, 16)
                        sync.dma_start(pairs_[64:P, kv, g, 0:T - 1], src[:, 1:T]).then_inc(stacked, 16)
                sync.wait_ge(stacked, 16 * 16)
                feed(sync)

            @block.tensor
            def _(pe):
                for n in range(12):
                    if n >= 8:
                        pe.wait_ge(r_out, n - 7)
                    pe.matmul(bank(n % 8), C("rot_nsa"), qT[:, n, :] if n < 8 else kr[:, n - 8, :],
                              start=True, stop=True).then_inc(r_done, 1)

            @block.vector
            def _(dve):
                link = chain(dve, "rope2_chain")
                for n in range(12):
                    src = qT[:, n, :] if n < 8 else kr[:, n - 8, :]
                    dst = qr[:, n, :] if n < 8 else kr[:, n - 8, :]
                    dve.wait_ge(r_done, n + 1)
                    link(dve.tensor_tensor(bank(n % 8), bank(n % 8), C("sin_nsa"), ALU.mult))
                    link(dve.tensor_tensor(dst, src, C("cos_nsa"), ALU.mult))
                    dve.tensor_tensor(dst, dst, bank(n % 8), ALU.add).then_inc(r_out, 1)

        n3 = ExitStack()
        hidc = sb("hidc", [P, 2, 2, NG * 31], n3).rearrange("p v m (g n) -> p v m g n", g=NG)
        posb = sb("posb", [P, 2, 2], n3)
        kcb = sb("kcb", [P, 62], n3)
        vcb = sb("vcb", [P, NG * ND], n3)
        h_done, b_out, hid_out, w2_done = sem("h_done"), sem("b_out"), sem("hid_out"), sem("w2_done")
        with nc.Block() as block:
            @block.tensor
            def _(pe):
                for kv in range(2):
                    w = take(pe, f"{'kv'[kv]}w1").rearrange("p (l n) -> p l n", l=16)
                    pe.wait_ge(stacked, 16 * 16)
                    for m in range(2):
                        b = 2 * (2 * kv + m)
                        if b >= 6:
                            pe.wait_ge(hid_out, 1)
                        for l in range(16):
                            lhs = w[:, l, m * P:(m + 1) * P]
                            rhs = pairs_[:, kv, :, 2 * l:2 * l + 30 * CMP_STRIDE + 1:CMP_STRIDE]
                            pe.matmul(psum[:, (b % 6) * 512:(b % 6) * 512 + 124].rearrange("p (a b) -> p a b", a=NG),
                                      lhs, rhs, start=(l == 0), stop=(l == 15))
                            last = pe.matmul(psum[:, (b % 6 + 1) * 512:(b % 6 + 1) * 512 + 1], lhs, V("pos", l, 1),
                                             start=(l == 0), stop=(l == 15))
                        last.then_inc(h_done, 1)
                    used(h_done, 2 * kv + 2)
                pe.wait_ge(hid_out, 4)
                w2 = take(pe, "cw2")[:, 0:256].rearrange("p (v m n) -> p v m n", v=2, m=2)
                for par in range(2):
                    product(pe, psum[64 * par:64 * par + 64, 6 * 512:6 * 512 + 62]
                            .rearrange("p (a b) -> p a b", a=2), lambda m: w2[:, 0, m, :],
                            lambda m: hidc[:, 0, m, :, :].rearrange("p (t q) n -> p q t n", q=2)[:, par], 2)
                for g in range(NG):
                    tile, par = g // 2, g % 2
                    for j in range(4):
                        last = product(pe, psum[32 * j:32 * j + 31, 7 * 512 + g * ND:7 * 512 + (g + 1) * ND],
                                       lambda m: hidc[:, 1, m, g, :],
                                       lambda m: w2[:, 1, m, :], 2)
                last.then_inc(w2_done, 1)
                used(w2_done, 1)

            @block.scalar
            def _(act):
                for n in range(4):
                    kv, m = n // 2, n % 2
                    b = (2 * n % 6) * 512
                    act.wait_ge(h_done, n + 1)
                    act.copy(posb[:, kv, m:m + 1], psum[:, b + 512:b + 513]).then_inc(b_out, 1)
                    act.wait_ge(b_out, n + 1)
                    act.activation(hidc[:, kv, m, :, :].rearrange("p g n -> p (g n)"), psum[:, b:b + 124],
                                   ACT.Silu, bias=posb[:, kv, m:m + 1], scale=1.0).then_inc(hid_out, 1)
                act.wait_ge(w2_done, 1)
                act.copy(kcb[:, :], psum[:, 6 * 512:6 * 512 + 62])
                for j in range(4):
                    rows = slice(32 * j, 32 * j + 31)
                    act.copy(vcb[rows, :], psum[rows, 7 * 512:7 * 512 + 256])

            @block.sync
            def _(sync):
                feed(sync)

        pc = sb("pc", [P, 2, NH, 32], n3)
        cst8 = sb("cst8", [P, TT, 4, NH], n3)
        n4 = ExitStack()
        pcT = hT[:, 0:4, :]
        cs_done, cs_sub, cs_exp, cs_prob, cs_turn, cs_out = (
            sem(n) for n in ("cs_done", "cs_sub", "cs_exp", "cs_prob", "cs_turn", "cs_out"))
        with nc.Block() as block:
            @block.tensor
            def _(pe):
                def cmp_scores(i):
                    for h in range(NH):
                        g, j = h // 4, h % 4
                        rows = slice(64 * (g % 2), 64 * (g % 2) + 64)
                        at = 512 * (i + 4 * (g % 2)) + (4 * (g // 2) + j) * 32
                        last = pe.matmul(psum[:, at:at + 31], qT[rows, 4 * (g // 2) + j, i * P:(i + 1) * P],
                                         kcb[rows, (g // 2) * 31:(g // 2) * 31 + 31], start=True, stop=True)
                    last.then_inc(cs_done, 1)
                for i in range(TT):
                    cmp_scores(i)
                for i in range(TT):
                    pe.wait_ge(cs_prob, i + 1)
                    for g in range(NG):
                        last = pe.transpose(bank(i)[:, g * P:(g + 1) * P],
                                            pc[:, i % 2, 4 * g:4 * g + 4, :].rearrange("p a b -> p (a b)"), ident)
                    last.then_inc(cs_turn, 1)

            @block.vector
            def _(dve):
                link = chain(dve, "cmp_chain")
                link(dve.memset(pc[:, :, :, :], 0.0))
                for i in range(TT):
                    e = pc[:, i % 2, :, 0:31]

                    def row(name, n=NH):
                        return C(name, 32 * i, 31).rearrange("p (o n) -> p o n", o=1).to_broadcast([P, n, 31])

                    def col(k):
                        return cst8[:, i, k, :].rearrange("p (h o) -> p h o", o=1)
                    dve.wait_ge(cs_done, i + 1)
                    if i >= 2:
                        dve.wait_ge(cs_turn, i - 1)
                    for g in range(NG):
                        s = bank(i + 4 * (g % 2))[:, 128 * (g // 2):128 * (g // 2) + P]
                        last = dve.tensor_tensor(e[:, 4 * g:4 * g + 4, :],
                                                 s.rearrange("p (h n) -> p h n", n=32)[:, :, 0:31],
                                                 row("cmp_neg", 4), ALU.add)
                    link(last)
                    link(dve.tensor_reduce(cst8[:, i, 0, :], e, AX.X, ALU.max))
                    dve.tensor_tensor(e, e, col(0).to_broadcast([P, NH, 31]), ALU.subtract).then_inc(cs_sub, 1)
                    dve.wait_ge(cs_exp, i + 1)
                    link(dve.tensor_tensor(e, e, row("cmp_ok"), ALU.mult))
                    link(dve.tensor_reduce(cst8[:, i, 1, :], e, AX.X, ALU.add))
                    link(dve.tensor_scalar(cst8[:, i, 2, :], cst8[:, i, 1, :], 0.0, None, ALU.is_equal))
                    link(dve.tensor_tensor(cst8[:, i, 1, :], cst8[:, i, 1, :], cst8[:, i, 2, :], ALU.add))
                    link(dve.reciprocal(cst8[:, i, 2, :], cst8[:, i, 1, :]))
                    link(dve.tensor_tensor(cst8[:, i, 3, :], cst8[:, i, 2, :], gates[:, i, 0:48:3], ALU.mult))
                    dve.tensor_tensor(e, e, col(3).to_broadcast([P, NH, 31]), ALU.mult).then_inc(cs_prob, 1)

            @block.scalar
            def _(act):
                for i in range(TT):
                    act.wait_ge(cs_sub, i + 1)
                    e = pc[:, i % 2, :, 0:31]
                    act.activation(e, e, ACT.Exp).then_inc(cs_exp, 1)
                for i in range(TT):
                    act.wait_ge(cs_turn, i + 1)
                    act.copy(pcT[:, :, i * P:(i + 1) * P], bank(i).rearrange("p (g n) -> p g n", g=NG))

        n2.close()
        n5 = ExitStack()
        pp = sb("pp", [P, 2, 2, T], n5)
        pT = [sb(f"pT{b}", [P, 2, TT, T], n5) for b in range(2)]
        st2 = sb("st2", [P, 64, 8], n5)
        heads_ = [(g, j) for g in range(NG) for j in range(4)]
        units = [(hd, i) for hd in range(NH) for i in range(TT)]
        NU2 = len(units)
        score_done, max_done, exp_done, prob_done = (sem(n) for n in ("score2", "max2", "exp2", "prob2"))
        turn_done, turn_a, turn_v, pv_done, pv_out = (sem(n) for n in ("turn2", "turn_a2", "turn_v2", "pv2", "pv_out2"))
        with nc.Block() as block:
            @block.tensor
            def _(pe):
                def scores(u):
                    hd, i = units[u]
                    g, j = heads_[hd]
                    rows = slice(64 * (g % 2), 64 * (g % 2) + 64)
                    if u >= 2:
                        pe.wait_ge(exp_done, u - 1)
                    for br in range(2):
                        last = pe.matmul(bank(2 * (u % 2) + br, (i + 1) * P), qr[rows, 4 * (g // 2) + j, i * P:(i + 1) * P],
                                         kr[rows, 2 * br + g // 2, 0:(i + 1) * P], start=True, stop=True)
                    last.then_inc(score_done, 1)

                def turn(u):
                    hd, i = units[u]
                    pe.wait_ge(prob_done, u + 1)
                    if u >= 1:
                        pe.wait_ge(turn_a, u)
                        pe.wait_ge(turn_v, u)
                    for br in range(2):
                        for k in range(i + 1):
                            last = pe.transpose(bank(4 + br)[:, k * P:(k + 1) * P], pp[:, u % 2, br, k * P:(k + 1) * P],
                                                ident)
                    last.then_inc(turn_done, 1)

                def values(hd):
                    g, j = heads_[hd]
                    rows = slice(64 * (g % 2), 64 * (g % 2) + 64)
                    pe.wait_ge(turn_a, 4 * hd + 4)
                    pe.wait_ge(turn_v, 4 * hd + 4)
                    if hd >= 2:
                        pe.wait_ge(pv_out, hd - 1)
                    b = (6 + hd % 2) * 512
                    for br in range(2):
                        for k in range(TT):
                            pe.matmul(psum[rows, b + k * P:b + 512], vtok[:, k, br * 256 + g * ND:br * 256 + (g + 1) * ND],
                                      pT[hd % 2][:, br, k, k * P:T], start=(br == 0 and k == 0), stop=False)
                    blk = slice(32 * j, 32 * j + 31)
                    pe.matmul(psum[rows, b:b + 512], vcb[blk, g * ND:(g + 1) * ND], pcT[blk, g, :], start=False,
                              stop=True).then_inc(pv_done, 1)

                scores(0)
                scores(1)
                for u in range(NU2):
                    if u + 2 < NU2:
                        scores(u + 2)
                    if u % 4 == 1 and u > 1:
                        values(u // 4 - 1)
                    turn(u)
                values(NH - 1)

            @block.vector
            def _(dve):
                link = chain(dve, "soft2_chain")

                def peak(u):
                    hd, i = units[u]
                    dve.wait_ge(score_done, u + 1)
                    s = psum[:, 2 * (u % 2) * 512:(2 * (u % 2) + 2) * 512].rearrange("p (b n) -> p b n", b=2)
                    diag = s[:, :, i * P:(i + 1) * P]
                    neg = C("causal_neg").rearrange("p (o n) -> p o n", o=1).to_broadcast([P, 2, P])
                    link(dve.tensor_tensor(diag, diag, neg, ALU.add))
                    dve.tensor_reduce(st2[:, u, 0:2], s[:, :, 0:(i + 1) * P], AX.X, ALU.max, negate=True)\
                       .then_inc(max_done, 1)

                peak(0)
                peak(1)
                for u in range(NU2):
                    hd, i = units[u]
                    g, j = heads_[hd]
                    h = 4 * g + j
                    dve.wait_ge(exp_done, u + 1)
                    link(dve.reciprocal(st2[:, u, 4:6], st2[:, u, 2:4]))
                    link(dve.tensor_tensor(st2[:, u, 6:8], st2[:, u, 4:6], gates[:, i, 3 * h + 1:3 * h + 3], ALU.mult))
                    w = (i + 1) * P
                    for br in range(2):
                        last = dve.tensor_scalar(pp[:, u % 2, br, 0:w], pp[:, u % 2, br, 0:w],
                                                 st2[:, u, 6 + br:7 + br], None, ALU.mult)
                    last.then_inc(prob_done, 1)
                    if u + 2 < NU2:
                        peak(u + 2)
                    dve.wait_ge(turn_done, u + 1)
                    dve.tensor_copy(pT[hd % 2][:, 1, 0:i + 1, i * P:(i + 1) * P],
                                    bank(5, w).rearrange("p (k n) -> p k n", n=P)).then_inc(turn_v, 1)

            @block.scalar
            def _(act):
                def exps(u):
                    hd, i = units[u]
                    act.wait_ge(max_done, u + 1)
                    if u >= 2:
                        act.wait_ge(turn_done, u - 1)
                    w = (i + 1) * P
                    for br in range(2):
                        last = act.activation(pp[:, u % 2, br, 0:w], bank(2 * (u % 2) + br, w), ACT.Exp,
                                              bias=st2[:, u, br:br + 1], scale=1.0, accum_out=st2[:, u, 2 + br:3 + br])
                    last.then_inc(exp_done, 1)

                def store(hd):
                    g, j = heads_[hd]
                    rows = slice(64 * (g % 2), 64 * (g % 2) + 64)
                    b = (6 + hd % 2) * 512
                    act.wait_ge(pv_done, hd + 1)
                    act.copy(mixT[rows, 4 * (g // 2) + j, :], psum[rows, b:b + 512]).then_inc(pv_out, 1)

                exps(0)
                for u in range(NU2):
                    hd, i = units[u]
                    if u + 1 < NU2:
                        exps(u + 1)
                    act.wait_ge(turn_done, u + 1)
                    act.copy(pT[hd % 2][:, 0, 0:i + 1, i * P:(i + 1) * P],
                             bank(4, (i + 1) * P).rearrange("p (k n) -> p k n", n=P)).then_inc(turn_a, 1)
                    if hd >= 1 and i == 1:
                        store(hd - 1)
                store(NH - 1)
        n5.close()
        n3.close()
        n1.close()
        project(["odo0", "odo1"], mixT, None)
        phase.close()
        feed_forward("_mlp1", "up1_", MLP_UP, "down1_", MLP_DOWN, False, lambda k: V("mlp1", k, 1), None, None)
        phase, hT, mixT = mixer_memory(3, 0)
        norm(xT, hT, xT, KD, TT, 1.0 / D, lambda k: V("final_norm", k, 1), presummed=True)
        stored = sem("stored")
        with nc.Block() as block:
            @block.sync
            def _(sync):
                sync.dma_start(out_d, xT[:, :, :]).then_inc(stored, 16)
                sync.wait_ge(stored, 16)
        phase.close()
        assert cursor[0] == len(PLAN)


def chunk(w, cols, rows=None):
    w = w[:, cols] if rows is None else w[rows][:, cols]
    return w.reshape(-1, P, w.shape[1]).transpose(1, 0, 2).reshape(P, -1)


def span(a, n):
    return list(range(a, a + n))


def lay_out(inp):
    f = {k: np.asarray(v) for k, v in inp.items()}
    w_mod, w_in = f["w_mod"][0], f["w_in"][0]
    o_cq, o_ckv, o_kr, o_hq, o_hff, o_hfb, o_hi, o_hg, o_fn = 0, 256, 384, 448, 960, 1472, 1984, 2240, 2496
    parts = {}
    for i in range(12):
        parts[f"mod{i}"] = chunk(w_mod, slice(512 * i, 512 * i + 512))
    parts["hi_fn"] = chunk(w_in, span(o_hi, 256) + span(o_fn, 256))
    parts["mla_in"] = chunk(w_in, span(o_cq, 256) + span(o_ckv, 128) + span(o_kr, 64) * 2)
    parts["hg_gate"] = chunk(w_in, span(o_hg, 256))
    parts["hff"], parts["hfb"], parts["hq"] = (chunk(w_in, span(o, 512)) for o in (o_hff, o_hfb, o_hq))
    n = np.arange(T)
    ang = 2 * np.pi * ((np.outer(n, n)) % T) / T
    both = [(g(ang) / math.sqrt(T)).astype(np.float32).reshape(TT, P, T).transpose(1, 0, 2).reshape(P, -1)
            for g in (np.cos, np.sin)]
    parts["dft"] = np.concatenate(both, axis=1)
    parts["fourier"] = chunk(f["w_fourier"][0], slice(0, 256))
    qcols = [h * 192 + i for h in range(MH) for i in range(128)] + [h * 192 + 128 + i for h in range(MH) for i in range(64)]
    kcols = [h * 256 + i for h in range(MH) for i in range(128)] + [h * 256 + 128 + i for h in range(MH) for i in range(128)]
    parts["mla_up"] = np.concatenate([chunk(f["w_uq"][0], qcols), chunk(f["w_ukv"][0], kcols)], axis=1)
    for i in range(2):
        parts[f"out{i}"] = chunk(f["w_out"][0], slice(512 * i, 512 * i + 512))
    for i in range(11):
        parts[f"gu{i}"] = chunk(f["w_gate_up"][0], span(256 * i, 256) + span(FFN + 256 * i, 256))

    def down_chunks(name, w, downs):
        row = 0
        for part in range(2):
            for i, kt in enumerate(downs[part]):
                for h in range(2):
                    parts[f"{name}{part}_{h}_{i}"] = chunk(w, slice(512 * h, 512 * h + 512), slice(row, row + kt * P))
                row += kt * P
    down_chunks("dn", f["w_down"][0], FFN1_DOWN)
    ev = f["ev_w_in_2"][0]
    parts["ev_ab"] = chunk(ev, span(2048, 16))
    order = span(0, 2048) + span(2064 + 512, 512) + span(2064 + 1024, 512) + span(2064, 512)
    for i in range(7):
        parts[f"ev{i}"] = chunk(ev, order[512 * i:512 * i + 512])
    for i in range(2):
        parts[f"evo{i}"] = chunk(f["ev_w_out_2"][0], slice(512 * i, 512 * i + 512))
    for l in range(2):
        for i in range(8):
            parts[f"up{l}_{i}"] = chunk(f["w_up_2"][l], slice(512 * i, 512 * i + 512))
        down_chunks(f"down{l}_", f["w_down_2"][l], MLP_DOWN)
    od = f["od_w_in_2"][0]
    slots = [(2 * (i // 4) + p) * 4 + i % 4 for i in range(8) for p in range(2)]
    qcols = [h * 64 + i for h in slots for i in range(64)]
    kc, vc, ks, vs, kw, vw, gl = (1024 + 256 * i for i in range(7))
    cols = qcols + span(kc, 256) + span(vc, 256) + span(ks, 256) + span(kw, 256) + span(vs, 256) + span(vw, 256)
    parts["gl"] = chunk(od, span(gl, 48))
    for i in range(5):
        parts[f"od{i}"] = chunk(od, cols[512 * i:512 * i + 512])
    for n_, key in (("k", "od_cmp_k_w1_2"), ("v", "od_cmp_v_w1_2")):
        parts[f"{n_}w1"] = chunk(f[key][0], slice(0, 256))
    parts["cw2"] = np.concatenate([chunk(f[k][0], slice(0, 64)) for k in ("od_cmp_k_w2_2", "od_cmp_v_w2_2")], axis=1)
    for i in range(2):
        parts[f"odo{i}"] = chunk(f["od_w_out_2"][0][qcols], slice(512 * i, 512 * i + 512))
    for name, w in PLAN:
        assert parts[name].shape == (P, w), (name, parts[name].shape, w)
    weights = np.concatenate([parts[name].reshape(-1) for name, _ in PLAN])

    def col(v):
        return v.reshape(-1, P).T

    v = {}
    v["c2"] = np.stack([col(f["c"][0]), col(f["c_ctx"])], axis=2).reshape(P, -1)
    v["b_mod"] = col(f["b_mod"][0])
    for name in ("norm1_g", "norm2_g", "q_norm_g", "kv_norm_g", "hg_norm_g"):
        v[name] = col(f[name][0])
    v["lb_param"] = col(f["lb_param"][0].reshape(-1))
    v["final_norm_g"], v["final_norm"] = col(f["final_norm_g"]), col(f["final_norm_2"])
    for l in range(2):
        v[f"mix{l}"], v[f"mlp{l}"] = col(f["mix_norm_2"][l]), col(f["mlp_norm_2"][l])
    v["conv"] = f["ev_qkv_conv_2"][0].T.reshape(12, P, 4).transpose(1, 0, 2).reshape(P, -1)
    v["o_norm"] = np.concatenate([f["ev_o_norm_2"][0]] * 2).reshape(P, 1)
    v["sc_conv"] = f["ev_sc_conv_2"][0].T.reshape(4, P, 3).transpose(1, 0, 2).reshape(P, -1)
    v["pos"] = col(f["od_cmp_pos_2"][0].reshape(-1))
    v["a_log"] = np.broadcast_to(f["ev_a_log_2"][0][None, :], (P, GH))
    v["dt_bias"] = np.broadcast_to(f["ev_dt_bias_2"][0][None, :], (P, GH))
    vecs = np.concatenate([v[name] for name, _ in VECS], axis=1)
    assert vecs.shape == (P, NVEC)
    xt = f["x"][0].T.reshape(KD, P, T).transpose(1, 0, 2)
    ct = f["ctx"][0].T.reshape(KD, P, TC).transpose(1, 0, 2)
    consts = np.concatenate(list(CONSTS.values()), axis=1)
    return [weights, consts, vecs, xt, ct]


INPUTS = [("weights", (NWEIGHT,)), ("consts", (P, NCONST)), ("vecs", (P, NVEC)), ("xin", (P, KD, T)),
          ("ctxin", (P, KD, TC))]


def kernel(**inputs):
    import concourse.bacc as bacc
    from concourse.bass_utils import run_bass_kernel_spmd
    arrays = lay_out(inputs)
    nc = bacc.Bacc("TRN2", target_bir_lowering=False, num_devices=1)
    aps = [nc.dram_tensor(n, s, F32, kind="ExternalInput").ap() for n, s in INPUTS]
    out = nc.dram_tensor("out", (P, KD, T), F32, kind="ExternalOutput").ap()
    program(nc, *aps, out)
    r = run_bass_kernel_spmd(nc, [{n: np.ascontiguousarray(a) for (n, _), a in zip(INPUTS, arrays)}], core_ids=[0])
    return r.results[0]["out"].transpose(1, 0, 2).reshape(D, T).T.reshape(1, T, D)
```
